# Optimizing a Trainium2 kernel written in Bass

```python
import jax, jax.numpy as jnp
from jax import lax
import numpy as np

D_MODEL = 1024
BATCH = 1
SEQ = 1024
DEPTH = 1
DEC_BATCH = 1
DEC_SEQ = 64
PAST_LEN = 256

CHUNK = 64
MIX_WIDTH = D_MODEL
RWKV_WIDTH = MIX_WIDTH // 2
RWKV_HEAD = 64
RWKV_HEADS = RWKV_WIDTH // RWKV_HEAD
DECAY_LORA = 32
AAA_LORA = 32
GATE_LORA = 64
GLA_WIDTH = MIX_WIDTH - RWKV_WIDTH
GLA_HEADS = 4
GLA_DV = GLA_WIDTH // GLA_HEADS
GLA_DK = GLA_DV // 2
GLA_KEY_WIDTH = GLA_HEADS * GLA_DK
GLA_GATE_RANK = 16
GLA_TAU = 16.0
RWKV_PROJ = 3 * RWKV_WIDTH + DECAY_LORA + AAA_LORA + GATE_LORA
GLA_PROJ = 2 * GLA_KEY_WIDTH + GLA_WIDTH + GLA_GATE_RANK + GLA_WIDTH
IN_PROJ = RWKV_PROJ + GLA_PROJ
N_GROUPS = 4
EXPERTS_PER_GROUP = 4
N_EXPERTS = N_GROUPS * EXPERTS_PER_GROUP
TOP_K = 2
D_EXPERT = 512
RMS_EPS = 1e-6
LNX_EPS = 64e-5

kernel_name = "rwkv7_gla_hier_moe_streaming_step"

def rmsnorm(x, g):
    xf = x.astype(jnp.float32)
    y = xf * lax.rsqrt(jnp.mean(xf * xf, axis=-1, keepdims=True) + RMS_EPS)
    return (y * g).astype(x.dtype)

def modulation(c, w, b, n):
    m = jax.nn.silu(c) @ w + b
    return jnp.split(m[:, None, :], n, axis=-1)

def rwkv7_group(p, shift_prev, s0, lp):
    B, L, _ = p.shape
    W = RWKV_WIDTH
    xx = jnp.concatenate([shift_prev[:, None, :].astype(p.dtype), p[:, :-1]], axis=1)
    ps = p + (xx - p) * lp["mu_shift"]
    r, k, v, dw, da, dg = jnp.split(
        ps, [W, 2 * W, 3 * W, 3 * W + DECAY_LORA, 3 * W + DECAY_LORA + AAA_LORA], axis=-1)
    logw = -jax.nn.softplus(-(lp["w0"] + jnp.tanh(dw) @ lp["w_decay_up"])) - 0.5
    decay = jnp.exp(-jnp.exp(logw.astype(jnp.float32)))
    a = jax.nn.sigmoid(lp["a0"] + da @ lp["w_a_up"])
    g = jax.nn.sigmoid(dg) @ lp["w_g_up"]
    heads = lambda t: t.reshape(B, L, RWKV_HEADS, RWKV_HEAD)
    kk = heads(k * lp["k_k"]).astype(jnp.float32)
    kk = kk / jnp.maximum(jnp.sqrt(jnp.sum(kk * kk, axis=-1, keepdims=True)), 1e-12)
    k = k * (1 + (a - 1) * lp["k_a"])
    r_h, k_h, v_h = heads(r), heads(k), heads(v)

    def step(S, inp):
        r_t, w_t, k_t, v_t, kk_t, a_t = inp
        sa = jnp.einsum("bhvk,bhk->bhv", S, -kk_t)
        S = (S * w_t[:, :, None, :] + sa[..., None] * (kk_t * a_t)[:, :, None, :]
             + v_t[..., None] * k_t[:, :, None, :])
        return S, jnp.einsum("bhvk,bhk->bhv", S, r_t)

    tm = lambda t: jnp.moveaxis(t.astype(jnp.float32), 1, 0)
    S, y = lax.scan(step, s0.astype(jnp.float32),
                    (tm(r_h), tm(heads(decay)), tm(k_h), tm(v_h), tm(kk), tm(heads(a))),
                    unroll=4)
    y = jnp.moveaxis(y, 0, 1)
    mu = jnp.mean(y, axis=-1, keepdims=True)
    var = jnp.mean(jnp.square(y - mu), axis=-1, keepdims=True)
    y = ((y - mu) * lax.rsqrt(var + LNX_EPS)).reshape(B, L, W) * lp["lnx_w"] + lp["lnx_b"]
    bonus = jnp.sum(r_h * k_h * lp["r_k"], axis=-1, keepdims=True) * v_h
    y = (y + bonus.reshape(B, L, W)) * g
    return y.astype(p.dtype), p[:, -1], S.astype(s0.dtype)

def gla_group(p, s0, lp):
    B, L, _ = p.shape
    KW, GW = GLA_KEY_WIDTH, GLA_WIDTH
    q, k, v, dgt, og = jnp.split(p, [KW, 2 * KW, 2 * KW + GW, 2 * KW + GW + GLA_GATE_RANK], axis=-1)
    log_alpha = jax.nn.log_sigmoid(
        (dgt @ lp["w_gla_gate_up"] + lp["b_gla_gate"]).astype(jnp.float32)) / GLA_TAU
    cs = CHUNK if L >= CHUNK else L
    n = L // cs
    blk = lambda t, d: t.reshape(B, n, cs, GLA_HEADS, d).transpose(0, 3, 1, 2, 4).astype(jnp.float32)
    qb = blk(q, GLA_DK) * (GLA_DK ** -0.5)
    kb, vb, lab = blk(k, GLA_DK), blk(v, GLA_DV), blk(log_alpha, GLA_DK)
    b = jnp.cumsum(lab, axis=3)
    b_last = b[:, :, :, -1:, :]
    q_dec = qb * jnp.exp(b)
    k_inv = kb * jnp.exp(-b)
    k_end = kb * jnp.exp(b_last - b)
    causal = jnp.tril(jnp.ones((cs, cs), dtype=bool))
    att = jnp.where(causal, jnp.einsum("bhnid,bhnjd->bhnij", q_dec, k_inv), 0.0)
    o = jnp.einsum("bhnij,bhnjv->bhniv", att, vb)
    u = jnp.einsum("bhnjd,bhnjv->bhndv", k_end, vb)
    dec = jnp.exp(b_last[:, :, :, 0, :])

    def step(S, inp):
        d_n, u_n = inp
        return d_n[..., None] * S + u_n, S

    S, s_in = lax.scan(step, s0.astype(jnp.float32),
                       (jnp.moveaxis(dec, 2, 0), jnp.moveaxis(u, 2, 0)))
    o = o + jnp.einsum("bhnid,nbhdv->bhniv", q_dec, s_in)
    o = o.transpose(0, 2, 3, 1, 4).reshape(B, L, GLA_HEADS, GLA_DV)
    o = o * lax.rsqrt(jnp.mean(o * o, axis=-1, keepdims=True) + RMS_EPS)
    o = o.reshape(B, L, GW) * lp["gla_norm_g"] * jax.nn.silu(og)
    return o.astype(p.dtype), S.astype(s0.dtype)

def hier_moe(h, lp):
    B, L, D = h.shape
    t = h.reshape(B * L, D)
    lg = (t @ lp["w_router_group"] + lp["b_router_group"]).astype(jnp.float32)
    pg = jax.nn.softmax(lg, axis=-1)
    gi = jnp.argmax(lg, axis=-1)
    pg_top = jnp.take_along_axis(pg, gi[:, None], axis=1)
    le = (t @ lp["w_router_expert"] + lp["b_router_expert"]).astype(jnp.float32)
    le = le.reshape(-1, N_GROUPS, EXPERTS_PER_GROUP)
    le = jnp.take_along_axis(le, gi[:, None, None], axis=1)[:, 0]
    top_v, top_i = lax.top_k(jax.nn.softmax(le, axis=-1), TOP_K)
    wts = pg_top * top_v / jnp.sum(top_v, axis=-1, keepdims=True)
    eid = gi[:, None] * EXPERTS_PER_GROUP + top_i
    comb = jnp.einsum("tk,tke->te", wts, jax.nn.one_hot(eid, N_EXPERTS, dtype=jnp.float32))
    out = jnp.zeros((B * L, D), jnp.float32)
    for e in range(N_EXPERTS):
        hid = jax.nn.silu(t @ lp["w_expert_gate"][e]) * (t @ lp["w_expert_up"][e])
        out = out + comb[:, e:e + 1] * (hid @ lp["w_expert_down"][e])
    return out.reshape(B, L, D).astype(h.dtype)

def layer(x, c, shift0, wkv0, gla0, lp):
    sh1, sc1, gt1, sh2, sc2, gt2 = modulation(c, lp["w_ada"], lp["b_ada"], 6)
    h = rmsnorm(x, lp["norm1_g"]) * (1 + sc1) + sh1
    proj = h @ lp["w_in"]
    y_r, new_shift, new_wkv = rwkv7_group(proj[..., :RWKV_PROJ], shift0, wkv0, lp)
    y_g, new_gla = gla_group(proj[..., RWKV_PROJ:], gla0, lp)
    x = x + gt1 * (jnp.concatenate([y_r, y_g], axis=-1) @ lp["w_out"])
    h = rmsnorm(x, lp["norm2_g"]) * (1 + sc2) + sh2
    x = x + gt2 * hier_moe(h, lp)
    return x, new_shift, new_wkv, new_gla

def setup_inputs(seed: int = 0) -> dict:
    key = jax.random.key(seed)
    keys = iter(jax.random.split(key, 48))
    f32 = jnp.float32

    def nrm(shape, scale):
        return jax.random.normal(next(keys), shape, f32) * scale

    def unif(shape, lo, hi):
        return jax.random.uniform(next(keys), shape, f32, lo, hi)

    D, L = D_MODEL, DEPTH
    return {
        "x_prompt": nrm((BATCH, SEQ, D), 1.0),
        "x_sample": nrm((DEC_BATCH, DEC_SEQ, D), 1.0),
        "c_prompt": nrm((BATCH, D), 1.0),
        "c_sample": nrm((DEC_BATCH, D), 1.0),
        "state_rwkv_shift": nrm((L, DEC_BATCH, RWKV_PROJ), 1.0),
        "state_rwkv_wkv": nrm((L, DEC_BATCH, RWKV_HEADS, RWKV_HEAD, RWKV_HEAD), 0.5),
        "state_gla_kv": nrm((L, DEC_BATCH, GLA_HEADS, GLA_DK, GLA_DV), 0.5),
        "w_ada": nrm((L, D, 6 * D), D ** -0.5),
        "b_ada": nrm((L, 6 * D), 0.02),
        "norm1_g": 1.0 + nrm((L, D), 0.02),
        "norm2_g": 1.0 + nrm((L, D), 0.02),
        "w_in": nrm((L, D, IN_PROJ), D ** -0.5),
        "mu_shift": unif((L, RWKV_PROJ), 0.0, 1.0),
        "w0": unif((L, RWKV_WIDTH), -6.0, 1.0),
        "w_decay_up": nrm((L, DECAY_LORA, RWKV_WIDTH), DECAY_LORA ** -0.5),
        "a0": nrm((L, RWKV_WIDTH), 0.1),
        "w_a_up": nrm((L, AAA_LORA, RWKV_WIDTH), AAA_LORA ** -0.5),
        "w_g_up": nrm((L, GATE_LORA, RWKV_WIDTH), GATE_LORA ** -0.5),
        "k_k": 0.85 + nrm((L, RWKV_WIDTH), 0.02),
        "k_a": 1.0 + nrm((L, RWKV_WIDTH), 0.02),
        "r_k": nrm((L, RWKV_HEADS, RWKV_HEAD), 0.1),
        "lnx_w": 1.0 + nrm((L, RWKV_WIDTH), 0.02),
        "lnx_b": nrm((L, RWKV_WIDTH), 0.01),
        "w_gla_gate_up": nrm((L, GLA_GATE_RANK, GLA_KEY_WIDTH), GLA_GATE_RANK ** -0.5),
        "b_gla_gate": nrm((L, GLA_KEY_WIDTH), 0.1),
        "gla_norm_g": 1.0 + nrm((L, GLA_WIDTH), 0.02),
        "w_out": nrm((L, MIX_WIDTH, D), MIX_WIDTH ** -0.5),
        "w_router_group": nrm((L, D, N_GROUPS), D ** -0.5),
        "b_router_group": nrm((L, N_GROUPS), 0.01),
        "w_router_expert": nrm((L, D, N_EXPERTS), D ** -0.5),
        "b_router_expert": nrm((L, N_EXPERTS), 0.01),
        "w_expert_gate": nrm((L, N_EXPERTS, D, D_EXPERT), D ** -0.5),
        "w_expert_up": nrm((L, N_EXPERTS, D, D_EXPERT), D ** -0.5),
        "w_expert_down": nrm((L, N_EXPERTS, D_EXPERT, D), D_EXPERT ** -0.5),
        "w_ada_final": nrm((D, 2 * D), D ** -0.5),
        "b_ada_final": nrm((2 * D,), 0.02),
        "normf_g": 1.0 + nrm((D,), 0.02),
    }

def reference(x_prompt, x_sample, c_prompt, c_sample, state_rwkv_shift, state_rwkv_wkv, state_gla_kv,
              w_ada, b_ada, norm1_g, norm2_g, w_in, mu_shift, w0, w_decay_up, a0, w_a_up, w_g_up,
              k_k, k_a, r_k, lnx_w, lnx_b, w_gla_gate_up, b_gla_gate, gla_norm_g, w_out,
              w_router_group, b_router_group, w_router_expert, b_router_expert,
              w_expert_gate, w_expert_up, w_expert_down, w_ada_final, b_ada_final, normf_g):
    def layer_params(l):
        return dict(w_ada=w_ada[l], b_ada=b_ada[l], norm1_g=norm1_g[l], norm2_g=norm2_g[l],
                    w_in=w_in[l], mu_shift=mu_shift[l], w0=w0[l], w_decay_up=w_decay_up[l],
                    a0=a0[l], w_a_up=w_a_up[l], w_g_up=w_g_up[l], k_k=k_k[l], k_a=k_a[l],
                    r_k=r_k[l], lnx_w=lnx_w[l], lnx_b=lnx_b[l], w_gla_gate_up=w_gla_gate_up[l],
                    b_gla_gate=b_gla_gate[l], gla_norm_g=gla_norm_g[l], w_out=w_out[l],
                    w_router_group=w_router_group[l], b_router_group=b_router_group[l],
                    w_router_expert=w_router_expert[l], b_router_expert=b_router_expert[l],
                    w_expert_gate=w_expert_gate[l], w_expert_up=w_expert_up[l],
                    w_expert_down=w_expert_down[l])

    def run(x, c, shift0, wkv0, gla0):
        shifts, wkvs, glas = [], [], []
        for l in range(DEPTH):
            x, s_shift, s_wkv, s_gla = layer(x, c, shift0[l], wkv0[l], gla0[l], layer_params(l))
            shifts.append(s_shift)
            wkvs.append(s_wkv)
            glas.append(s_gla)
        shf, scf = modulation(c, w_ada_final, b_ada_final, 2)
        y = rmsnorm(x, normf_g) * (1 + scf) + shf
        return y, jnp.stack(shifts), jnp.stack(wkvs), jnp.stack(glas)

    bp = x_prompt.shape[0]
    shift_p0 = jnp.zeros((DEPTH, bp, RWKV_PROJ), x_prompt.dtype)
    wkv_p0 = jnp.zeros((DEPTH, bp, RWKV_HEADS, RWKV_HEAD, RWKV_HEAD), state_rwkv_wkv.dtype)
    gla_p0 = jnp.zeros((DEPTH, bp, GLA_HEADS, GLA_DK, GLA_DV), state_gla_kv.dtype)
    y_p, sh_p, wkv_p, gla_p = run(x_prompt, c_prompt, shift_p0, wkv_p0, gla_p0)
    y_s, sh_s, wkv_s, gla_s = run(x_sample, c_sample, state_rwkv_shift, state_rwkv_wkv, state_gla_kv)
    return (y_p, y_s, sh_p, wkv_p, gla_p, sh_s, wkv_s, gla_s)


_drawn_inputs = setup_inputs


def setup_inputs(seed=0):
    import zlib

    import numpy as np

    out = dict(_drawn_inputs(seed))
    spreads = {}
    factors = {'lnx_w': 39.488,
     'lnx_b': 71.381,
     'b_router_group': 200.0,
     'b_router_expert': 39.748,
     'b_ada_final': 2.675,
     'normf_g': 8.019,
     'state_gla_kv': 3.024,
     'gla_norm_g': 27.69,
     'norm2_g': 5.88}
    for name, (base, spread) in spreads.items():
        noise = np.random.default_rng([zlib.crc32(name.encode()), seed]).standard_normal(out[name].shape)
        drawn = base * np.exp(spread * noise) if base else spread * noise
        out[name] = __import__('jax').numpy.asarray(drawn.astype(out[name].dtype))
    for name, factor in factors.items():
        out[name] = (out[name] * factor).astype(out[name].dtype)
    return out
```

```python
from contextlib import ExitStack

import concourse.bass as bass
from concourse import mybir

F32 = mybir.dt.float32
I32 = mybir.dt.int32
U32 = mybir.dt.uint32
ALU = mybir.AluOpType
ACT = mybir.ActivationFunctionType
AX_X = mybir.AxisListType.X

P = 128
D = 1024
KT = D // P
SEQ = 1024
DEC = 64
T = SEQ + DEC
NP = SEQ // P
NT = NP + 1
RW = 512
NJ = RW // P
RP = 3 * RW + 128
GK, GV, GR = 256, 512, 16
IN_COLS = RP + 2 * GK + 2 * GV + GR
NE, NG, EG = 16, 4, 4
DE = 512
NB = (2 * T + NE * (P - 1)) // P
RMS_EPS, LNX_EPS = 1e-6, 64e-5
DECAY_SCALE = -0.6065306597126334

F_A, F_B, F_K, F_R, F_V, F_WG, F_BG = [NJ * i for i in range(7)]
F_QD, F_KI, F_GV, F_SG = 28, 30, 32, 36
F_TILES = 40
PC = {}
_rows = 0
for _name, _n in (("mu", 13), ("w0", 4), ("a0", 4), ("kk", 4), ("ka", 4), ("rk", 4), ("lw", 4), ("lb", 4),
                  ("bg", 2), ("gn", 4), ("n1", 8), ("sh", 13)):
    PC[_name] = _rows
    _rows += _n
NPAR = _rows


def build(nc, a, o, debug=None):
    ctx = ExitStack()
    with ctx:
        def sem(name):
            return nc.alloc_semaphore(name=name)

        def sb(name, shape, dt=F32):
            return ctx.enter_context(nc.sbuf_tensor(name, shape, dt))

        def dram(name, shape, dt=F32):
            return nc.dram_tensor(name, shape, dt, kind="Internal").ap()

        d = {
            "mod": dram("mod_rows", (2, 8 * D)),
            "feat": dram("feature_major", (F_TILES * P, T)),
            "x1": dram("x_after_mixer", (T, D)),
            "h2": dram("moe_input", (T, D)),
            "tok": dram("plan", (NB * P, 2), I32),
            "y": dram("expert_rows", (NB * P, D)),
        }
        banks = ctx.enter_context(nc.psum_tensor("banks", [P, 8 * 512], F32))
        psum = [banks[:, 512 * i:512 * i + 512] for i in range(8)]
        c = {
            "ident": sb("ident", [P, P]), "ones": sb("ones", [P, P]), "headones": sb("headones", [P, P]),
            "after": sb("after", [P, P]),
            "upto": sb("upto", [P, P]),
            "below": sb("below", [P, P]),
            "level": sb("level", [P, 7, P]),
            "par": sb("par", [P, NPAR]),
            "modT": sb("modT", [P, 8 * KT, 2]),
            "hscale": sb("hscale", [P, KT, 2]),
            "decay_mid": sb("decay_mid", [P, NJ, NT]),
            "decay_end": sb("decay_end", [P, NJ, NT]),
            "gla_mid": sb("gla_mid", [P, 2, NT]),
            "gla_end": sb("gla_end", [P, 2, NT]),
            "logits": sb("logits", [P, NT, NG + NE]),
            "slots": sb("slots", [P, NT, 2], I32),
            "block_expert": sb("block_expert", [1, NB], I32),
            "shifts": sb("shifts", [P, 13, 2]),
        }
        with nc.sbuf_tensor("xT", [P, KT, T], F32) as xT:
            c["xT"] = xT
            modulation_block(nc, a, d, c, psum)
            projection_block(nc, a, d, c, banks)
        recurrence_block(nc, a, o, d, c, psum)
        experts_block(nc, a, d, c, psum)
        combine_block(nc, a, o, d, c)
        if debug:
            debug(nc, d, c)


def bank4(bank):
    return bank[:, :].rearrange("p (a b) -> p a b", a=4)


def over4(mask):
    return mask.unsqueeze(1).to_broadcast([mask.shape[0], 4, mask.shape[1]])


def modulation_block(nc, a, d, c, psum):
    with nc.cleanup_on_exit(), ExitStack() as ctx:
        def sem(name):
            return nc.alloc_semaphore(name=name)

        def sb(name, shape, dt=F32):
            return ctx.enter_context(nc.sbuf_tensor(name, shape, dt))

        W = sb("wada", [P, 4, KT, 512])
        brow = sb("brow", [2, 4, 512])
        modrow = sb("modrow", [2, 4, 512])
        cs = sb("cs", [2, D])
        ce = sb("ce", [2, D])
        cT = sb("cT", [P, KT, 2])
        prow = sb("prow", [P, P])
        xin = sb("xin", [P, 2, D])
        xn = sb("xn", [P, 2, D])
        sq = sb("sq", [P, D])
        ss = sb("ss", [P, 2])
        ms = sb("ms", [P, 2])
        rstd = sb("rstd", [P, 2])
        ri = sb("ri", [P, P], I32)
        fi = sb("fi", [P, P], I32)
        xi = sb("xi", [P, P], I32)
        xf = sb("xf", [P, P])
        odd = sb("odd", [P, P])
        odi = sb("odi", [P, P], I32)
        ge = sb("ge", [P, 8, P])
        xT = c["xT"]

        w_loaded = [sem(f"w_loaded{i}") for i in range(4)]
        x_loaded = [sem(f"x_loaded{i}") for i in range(2)]
        c_loaded = sem("c_loaded")
        p_loaded = sem("p_loaded")
        consts_made = sem("consts_made")
        ident_made = sem("ident_made")
        mask_step = sem("mask_step")
        c_step = sem("c_step")
        c_turned = sem("c_turned")
        cT_ready = sem("cT_ready")
        p_turned = sem("p_turned")
        p_read = sem("p_read")
        mod_done = sem("mod_done")
        row_ready = sem("row_ready")
        row_turned = sem("row_turned")
        modT_read = sem("modT_read")
        row_stored = [sem(f"row_stored{i}") for i in range(4)]
        squared = sem("squared")
        rstd_ready = sem("rstd_ready")
        mean_ready = sem("mean_ready")
        log_ready = sem("log_ready")
        xn_ready = sem("xn_ready")
        x_turned = [sem(f"x_turned{i}") for i in range(2)]
        x_read = [sem(f"x_read{i}") for i in range(2)]
        scale_ready = sem("scale_ready")

        xp = a["x_prompt"].rearrange("a t d -> (a t) d")
        xs = a["x_sample"].rearrange("a t d -> (a t) d")
        wa = a["w_ada"].rearrange("l (k p) n -> p (l k) n", p=P)
        wf = a["w_ada_final"].rearrange("(k p) n -> p k n", p=P)
        mod_b = [psum[0], psum[1]]
        x_b = [psum[2], psum[3]]
        row_b = [psum[4], psum[5]]

        block = ctx.enter_context(nc.Block())

        @block.sync
        def _(sp):
            sp.dma_start(cs[0:1, :], a["c_prompt"]).then_inc(c_loaded, 16)
            sp.dma_start(cs[1:2, :], a["c_sample"]).then_inc(c_loaded, 16)

            def chunk(s, src, bias, at):
                sp.dma_start(W[:, s], src[:, :, bass.ds(at, 512)]).then_inc(w_loaded[s], 16)
                sp.dma_start(brow[:, s, :], bias[:, bass.ds(at, 512)].to_broadcast([2, 512])).then_inc(w_loaded[s], 16)

            def x_tile(n, u):
                sp.dma_start(xin[:, u, :], xp[bass.ds(n * P, P), :]).then_inc(x_loaded[u], 16)

            x_tile(0, 0)
            x_tile(1, 1)
            for s in range(4):
                chunk(s, wa, a["b_ada"], s * 512)
            for name, src in (("mu", a["mu_shift"]), ("w0", a["w0"]), ("a0", a["a0"]), ("kk", a["k_k"]),
                              ("ka", a["k_a"]), ("lw", a["lnx_w"]), ("lb", a["lnx_b"]), ("bg", a["b_gla_gate"]),
                              ("gn", a["gla_norm_g"]), ("n1", a["norm1_g"]), ("sh", a["state_rwkv_shift"])):
                v = src.rearrange("l b (n p) -> (l b n) p", p=P) if name == "sh" else src.rearrange("l (n p) -> (l n) p", p=P)
                sp.dma_start(prow[PC[name]:PC[name] + v.shape[0], :], v).then_inc(p_loaded, 16)
            sp.dma_start(prow[PC["rk"]:PC["rk"] + 4, :],
                         a["r_k"].rearrange("l (n h) k -> (l n) (h k)", h=2)).then_inc(p_loaded, 16)
            b_final = a["b_ada_final"].rearrange("(l n) -> l n", l=1)

            def group(k, src, bias, at):
                for s in range(4):
                    sp.wait_ge(mod_done, 4 * k + s - 3)
                    sp.wait_ge(row_ready, 4 * k + s - 3)
                    chunk(s, src, bias, at + s * 512)
                    if s % 2 == 1:
                        sp.wait_ge(xn_ready, 2 * k + s // 2 - 1)
                        x_tile(2 * k + s // 2, s // 2)

            with sp.Fori(1, 3) as k:
                group(k, wa, a["b_ada"], k * 2048)
            group(3, wf, b_final, 0)
            sp.wait_ge(xn_ready, 7)
            sp.dma_start(xin[0:DEC, 0, :], xs).then_inc(x_loaded[0], 16)

        @block.gpsimd
        def _(pool):
            nc.gpsimd.memset(c["ones"][:, :], 1.0).then_inc(consts_made, 1)
            nc.gpsimd.memset(c["headones"][:, :], 0.0).then_inc(consts_made, 1)
            nc.gpsimd.memset(c["logits"][:, :, :], 0.0).then_inc(consts_made, 1)
            nc.gpsimd.iota(ri[:, :], [[0, P]], base=0, channel_multiplier=1).then_inc(consts_made, 1)
            nc.gpsimd.iota(fi[:, :], [[1, P]], base=0, channel_multiplier=0).then_inc(consts_made, 1)
            pool.wait_ge(consts_made, 5)
            nc.gpsimd.memset(c["headones"][0:64, 0:64], 1.0).then_inc(consts_made, 1)
            nc.gpsimd.memset(c["headones"][64:128, 64:128], 1.0).then_inc(consts_made, 1)
            pool.wait_ge(consts_made, 7)
            nc.gpsimd.affine_select(out=c["ident"][:, :], in_=c["ones"][:, :], pattern=[[1, P]], compare_op=ALU.is_equal,
                                    fill=0.0, base=0, channel_multiplier=-1).then_inc(ident_made, 1)
            nc.gpsimd.affine_select(out=c["after"][:, :], in_=c["ones"][:, :], pattern=[[1, P]], compare_op=ALU.is_gt,
                                    fill=0.0, base=0, channel_multiplier=-1).then_inc(ident_made, 1)
            nc.gpsimd.affine_select(out=c["upto"][:, :], in_=c["ones"][:, :], pattern=[[1, P]], compare_op=ALU.is_ge,
                                    fill=0.0, base=0, channel_multiplier=-1).then_inc(ident_made, 1)
            nc.gpsimd.affine_select(out=c["below"][:, :], in_=c["ones"][:, :], pattern=[[1, P]], compare_op=ALU.is_equal,
                                    fill=0.0, base=1, channel_multiplier=-1).then_inc(ident_made, 1)
            pool.wait_ge(consts_made, 7)
            pool.wait_ge(ident_made, 4)
            with pool.Fori(0, 4) as k:
                for s in range(4):
                    pool.wait_ge(row_ready, 4 * k + s + 1)
                    pool.dma_start(d["mod"][:, bass.ds((4 * k + s) * 512, 512)], modrow[:, s, :]).then_inc(row_stored[s], 16)
            for s in range(4):
                pool.wait_ge(row_stored[s], 64)

        @block.tensor
        def _(pe):
            pe.wait_ge(ident_made, 1)
            pe.wait_ge(c_step, 4)
            for k in range(KT):
                mm = pe.transpose(psum[6][:, 2 * k:2 * k + 2], cs[:, k * P:(k + 1) * P], c["ident"][0:2, 0:2])
            mm.then_inc(c_turned, 1)
            pe.wait_ge(p_loaded, 16 * 12)
            pe.transpose(psum[7][:, 0:NPAR], prow[0:NPAR, :], c["ident"][0:NPAR, 0:NPAR]).then_inc(p_turned, 1)
            pe.wait_ge(cT_ready, 1)

            def x_tile(n, u, m):
                pe.wait_ge(xn_ready, n + 1)
                for h in range(2):
                    pe.wait_ge(x_read[h], n)
                    for q in range(4):
                        mm = pe.transpose(x_b[h][:, q * P:q * P + m], xn[0:m, u, (4 * h + q) * P:(4 * h + q + 1) * P],
                                          c["ident"][0:m, 0:m])
                    mm.then_inc(x_turned[h], 1)

            def turn_row(i, v, s):
                now = pe.to_reg(i + 1)
                pe.wait_ge(ident_made, 1)
                pe.wait_ge(row_ready, now)
                for q in range(4):
                    mm = pe.transpose(row_b[v][:, 2 * q:2 * q + 2], modrow[:, s, q * P:(q + 1) * P], c["ident"][0:2, 0:2])
                mm.then_inc(row_turned, 1)

            with pe.Fori(0, 4) as k:
                for s in range(4):
                    i = 4 * k + s
                    pe.wait_ge(w_loaded[s], 32 * (k + 1))
                    if s >= 2:
                        pe.wait_ge(row_ready, i - 1)
                        pe.wait_ge(modT_read, i - 1)
                    else:
                        pe.wait_ge(row_ready, 4 * k)
                        pe.wait_ge(modT_read, 4 * k)
                    for q in range(KT):
                        mm = pe.matmul(mod_b[s % 2][0:2, :], cT[:, q, :], W[:, s, q, :], start=q == 0, stop=q == KT - 1)
                    mm.then_inc(mod_done, 1)
                    if s % 2 == 0:
                        x_tile(2 * k + s // 2, s // 2, P)
                    turn_row(i, s % 2, s)
            x_tile(NP, 0, DEC)

        @block.scalar
        def _(act):
            nc.scalar.preload_act_table_set("natural_log_exp_and_others")
            act.wait_ge(c_loaded, 32)
            nc.scalar.activation(ce[:, :], cs[:, :], ACT.Exp, scale=-1.0).then_inc(c_step, 1)
            act.wait_ge(c_step, 1)
            nc.scalar.activation(ce[:, :], ce[:, :], ACT.Ln, bias=1.0).then_inc(c_step, 1)
            act.wait_ge(c_step, 2)
            nc.scalar.activation(ce[:, :], ce[:, :], ACT.Exp, scale=-1.0).then_inc(c_step, 1)
            act.wait_ge(p_turned, 1)
            nc.scalar.copy(c["par"][:, :], psum[7][:, 0:NPAR]).then_inc(p_read, 1)

            def rstd_of(n, u, m):
                act.wait_ge(mean_ready, n + 1)
                nc.scalar.activation(rstd[0:m, u:u + 1], ms[0:m, u:u + 1], ACT.Ln).then_inc(log_ready, 1)
                act.wait_ge(log_ready, n + 1)
                nc.scalar.activation(rstd[0:m, u:u + 1], rstd[0:m, u:u + 1], ACT.Exp, scale=-0.5).then_inc(rstd_ready, 1)

            def evacuate(n, m):
                act.wait_ge(x_turned[0], n + 1)
                nc.scalar.copy(xT[:, 0:4, bass.ds(n * P, m)], bank4(x_b[0])[:, :, 0:m]).then_inc(x_read[0], 1)

            with act.Fori(0, 4) as k:
                for s in range(4):
                    i = 4 * k + s
                    if s % 2 == 0:
                        n, u = 2 * k + s // 2, s // 2
                        act.wait_ge(x_loaded[u], 16 * (k + 1))
                        act.wait_ge(xn_ready, n)
                        act.wait_ge(squared, n)
                        nc.scalar.activation(sq[:, :], xin[:, u, :], ACT.Square, accum_out=ss[:, u:u + 1]).then_inc(squared, 1)
                        rstd_of(n, u, P)
                        evacuate(n, P)
                    act.wait_ge(row_turned, i + 1)
                    nc.scalar.copy(c["modT"][:, bass.ds(i * 4, 4), :],
                                   row_b[s % 2][:, 0:8].rearrange("p (a b) -> p a b", a=4)).then_inc(modT_read, 1)
            act.wait_ge(x_loaded[0], 16 * 5)
            act.wait_ge(xn_ready, NP)
            act.wait_ge(squared, NP)
            nc.scalar.activation(sq[0:DEC, :], xin[0:DEC, 0, :], ACT.Square, accum_out=ss[0:DEC, 0:1]).then_inc(squared, 1)
            rstd_of(NP, 0, DEC)
            evacuate(NP, DEC)

        @block.vector
        def _(dve):
            dve.wait_ge(c_step, 3)
            nc.vector.tensor_tensor(cs[:, :], cs[:, :], ce[:, :], ALU.mult).then_inc(c_step, 1)
            dve.wait_ge(c_turned, 1)
            nc.vector.tensor_copy(cT[:, :, :], psum[6][:, 0:2 * KT].rearrange("p (k b) -> p k b", b=2)).then_inc(cT_ready, 1)
            dve.wait_ge(consts_made, 7)
            nc.vector.tensor_tensor(xi[:, :], ri[:, :], fi[:, :], ALU.bitwise_xor).then_inc(mask_step, 1)
            nc.vector.tensor_scalar(odi[:, :], ri[:, :], 1, None, ALU.bitwise_and).then_inc(mask_step, 1)
            dve.wait_ge(mask_step, 2)
            nc.vector.tensor_copy(xf[:, :], xi[:, :]).then_inc(mask_step, 1)
            nc.vector.tensor_copy(odd[:, :], odi[:, :]).then_inc(mask_step, 1)
            dve.wait_ge(mask_step, 4)
            for k in range(8):
                nc.vector.tensor_scalar(ge[:, k, :], xf[:, :], float(2 ** k), None, ALU.is_ge).then_inc(mask_step, 1)
            dve.wait_ge(mask_step, 12)
            dve.wait_ge(ident_made, 4)
            for k in range(7):
                nc.vector.tensor_tensor(c["level"][:, k, :], ge[:, k, :], ge[:, k + 1, :], ALU.subtract).then_inc(mask_step, 1)
            nc.vector.tensor_tensor(c["below"][:, :], c["below"][:, :], odd[:, :], ALU.mult).then_inc(mask_step, 1)
            dve.wait_ge(mask_step, 20)

            def x_tile(n, u, m):
                dve.wait_ge(squared, n + 1)
                nc.vector.tensor_scalar(ms[0:m, u:u + 1], ss[0:m, u:u + 1], 1.0 / D, RMS_EPS, ALU.mult, ALU.add).then_inc(mean_ready, 1)
                dve.wait_ge(rstd_ready, n + 1)
                nc.vector.tensor_scalar(xn[0:m, u, :], xin[0:m, u, :], rstd[0:m, u:u + 1], None, ALU.mult).then_inc(xn_ready, 1)
                dve.wait_ge(x_turned[1], n + 1)
                nc.vector.tensor_copy(xT[:, 4:8, bass.ds(n * P, m)], bank4(x_b[1])[:, :, 0:m]).then_inc(x_read[1], 1)

            with dve.Fori(0, 4) as k:
                for s in range(4):
                    i = 4 * k + s
                    dve.wait_ge(mod_done, i + 1)
                    dve.wait_ge(row_stored[s], 16 * k)
                    nc.vector.tensor_tensor(modrow[:, s, :], psum[s % 2][0:2, :], brow[:, s, :], ALU.add).then_inc(row_ready, 1)
                    if s % 2 == 0:
                        x_tile(2 * k + s // 2, s // 2, P)
            x_tile(NP, 0, DEC)
            dve.wait_ge(modT_read, 16)
            dve.wait_ge(p_read, 1)
            nc.vector.tensor_scalar(c["hscale"][:, :, :], c["modT"][:, KT:2 * KT, :], 1.0, None, ALU.add).then_inc(scale_ready, 1)
            dve.wait_ge(scale_ready, 1)
            for b in range(2):
                nc.vector.tensor_tensor(c["hscale"][:, :, b], c["hscale"][:, :, b], c["par"][:, PC["n1"]:PC["n1"] + 8], ALU.mult).then_inc(scale_ready, 1)
            dve.wait_ge(scale_ready, 3)


def projection_block(nc, a, d, c, banks):
    with nc.cleanup_on_exit(), ExitStack() as ctx:
        sems = {}

        def sg(name):
            if name not in sems:
                sems[name] = nc.alloc_semaphore(name=name)
            return sems[name]

        def sb(name, shape, dt=F32):
            return ctx.enter_context(nc.sbuf_tensor(name, shape, dt))

        hT = c["xT"]
        par, shifts = c["par"], c["shifts"]
        W = {n: sb("w_" + n, [P, KT, P]) for n in "rkv"}
        up = sb("up", [P, P])
        raw = {n: sb("raw_" + n, [P, T + 2]) for n in "rkv"}
        df = sb("df", [P, T])
        t3, kp, kn = [sb(n, [P, T]) for n in ("t3", "kp", "kn")]
        mid = sb("mid", [P, NT])
        mix = {n: sb("mix_" + n, [P, T]) for n in "rkv"}
        lora = sb("lora", [P, T])
        reset = sb("reset", [P, T])
        sig_w, sig_a, gate, b, t1, t2, kk = [sb(n, [P, T]) for n in ("sig_w", "sig_a", "gate", "b", "t1", "t2", "kkn")]
        ep, em, eprev = [sb(n, [P, T]) for n in ("ep", "em", "eprev")]
        out = {n: sb("out_" + n, [P, T]) for n in "ABKRWG"}
        dg = sb("dg", [GR, T])
        omka = sb("omka", [P, NJ])
        sh = sb("sh_state", [P, 13])
        A, B = banks[:, 0:T], banks[:, 3 * 512:3 * 512 + T]
        X1 = slice(0, SEQ)
        X2 = slice(SEQ, T)
        w_in = a["w_in"].rearrange("l (k p) n -> p (l k) n", p=P)
        feat = d["feat"]
        block = ctx.enter_context(nc.Block())

        def tiles(ap):
            return ap[:, X1].rearrange("p (n t) -> p n t", t=P)

        def col(name, j):
            return par[:, bass.ds(PC[name] + j, 1)]

        @block.sync
        def _(sp):
            def w_load(n, at, m=P):
                sp.dma_start(W[n][:, :, 0:m], w_in[:, :, bass.ds(at, m)]).then_inc(sg("w_loaded_" + n), 16)

            w_load("v", 3 * RW)
            sp.dma_start(sh[:, :], par[:, PC["sh"]:PC["sh"] + 13]).then_inc(sg("sh_loaded"), 16)
            with sp.Fori(0, NJ) as j:
                sp.wait_ge(sg("g_done"), j)
                for lo, hi, name in ((0, 32, "w_decay_up"), (32, 64, "w_a_up"), (64, 128, "w_g_up")):
                    sp.dma_start(up[lo:hi, :], a[name][0][:, bass.ds(j * P, P)]).then_inc(sg("up_loaded"), 16)
                sp.wait_ge(sg("k_done"), j)
                w_load("k", RW + j * P)
                sp.wait_ge(sg("r_done"), j)
                w_load("r", j * P)
                sp.wait_ge(sg("v_done"), j + 1)
                w_load("v", 2 * RW + j * P)
            q0, k0, v0, r0 = RP, RP + GK, RP + 2 * GK, RP + 2 * GK + GV
            g0 = r0 + GR
            sp.wait_ge(sg("v_done"), NJ + 1)
            w_load("v", r0, GR)
            sp.wait_ge(sg("g_done"), NJ)
            with sp.Fori(0, 2) as p:
                sp.wait_ge(sg("z_done"), p)
                sp.dma_start(up[0:GR, :], a["w_gla_gate_up"][0][:, bass.ds(p * P, P)]).then_inc(sg("gate_up_loaded"), 16)
                sp.wait_ge(sg("k_done"), NJ + 2 * p)
                w_load("k", q0 + p * P)
                sp.wait_ge(sg("r_done"), NJ + 2 * p)
                w_load("r", k0 + p * P)
                sp.wait_ge(sg("v_done"), NJ + 2 + 2 * p)
                w_load("v", v0 + 2 * p * P)
                sp.wait_ge(sg("k_done"), NJ + 1 + 2 * p)
                w_load("k", v0 + P + 2 * p * P)
                sp.wait_ge(sg("r_done"), NJ + 1 + 2 * p)
                w_load("r", g0 + 2 * p * P)
                sp.wait_ge(sg("v_done"), NJ + 3 + 2 * p)
                w_load("v", g0 + P + 2 * p * P)

        @block.gpsimd
        def _(pool):
            nc.gpsimd.memset(reset[:, :], 1.0).then_inc(sg("reset_filled"), 1)
            for n in "rkv":
                nc.gpsimd.memset(raw[n][:, 0:1], 0.0).then_inc(sg("reset_filled"), 1)
            pool.wait_ge(sg("reset_filled"), 4)
            nc.gpsimd.memset(tiles(reset)[:, :, 0:1], 0.0).then_inc(sg("reset_made"), 1)
            nc.gpsimd.memset(reset[:, SEQ:SEQ + 1], 0.0).then_inc(sg("reset_made"), 1)

            def store(n, row, src, ready):
                pool.wait_ge(sg("made_" + n), ready)
                pool.dma_start(feat[bass.ds(row * P, P), :], src[:, :]).then_inc(sg("stored_" + n), 16)

            with pool.Fori(0, NJ) as j:
                for n, f in (("R", F_R), ("K", F_K), ("A", F_A), ("B", F_B), ("W", F_WG)):
                    store(n, f + j, out[n], j + 1)
                pool.wait_ge(sg("v_mixed"), 2 * j + 2)
                pool.dma_start(feat[bass.ds((F_V + j) * P, P), :], mix["v"][:, :]).then_inc(sg("stored_V"), 16)
                store("G", F_BG + j, out["G"], j + 1)
            with pool.Fori(0, 2) as p:
                for n, f in (("R", F_QD + p), ("K", F_KI + p), ("A", F_GV + 2 * p), ("B", F_GV + 2 * p + 1),
                             ("W", F_SG + 2 * p), ("G", F_SG + 2 * p + 1)):
                    store(n, f, out[n], NJ + p + 1)
            for n in "ABKRWG":
                pool.wait_ge(sg("stored_" + n), 16 * (NJ + 2))
            pool.wait_ge(sg("stored_V"), 16 * NJ)

        def project(pe, dst, w, m=P):
            for lo in (0, 512, 1024):
                hi = min(lo + 512, T)
                for q in range(KT):
                    mm = pe.matmul(dst[0:m, lo:hi], w[:, q, 0:m], hT[:, q, lo:hi], start=q == 0, stop=q == KT - 1)
            return mm

        def raise_rank(pe, dst, lo_row, hi_row, src):
            for lo in (0, 512, 1024):
                hi = min(lo + 512, T)
                mm = pe.matmul(dst[:, lo:hi], up[lo_row:hi_row, :], src[lo_row:hi_row, lo:hi], start=True, stop=True)
            return mm

        def head_sums(pe, dst, src):
            for lo in (0, 512, 1024):
                hi = min(lo + 512, T)
                mm = pe.matmul(dst[:, lo:hi], c["headones"][:, :], src[:, lo:hi], start=True, stop=True)
            return mm

        @block.tensor
        def _(pe):
            pe.wait_ge(sg("h_made"), 2 * KT)
            pe.wait_ge(sg("w_loaded_v"), 16)
            project(pe, B, W["v"]).then_inc(sg("v_done"), 1)
            pe.wait_ge(sg("lora_read"), 2)
            with pe.Fori(0, NJ) as j:
                j0, j1, j3 = pe.to_reg(j + 0), pe.to_reg(j + 1), pe.to_reg((j + 1) * 48)
                pe.wait_ge(sg("v_read"), 2 * j)
                pe.wait_ge(sg("lora_made"), 3)
                pe.wait_ge(sg("up_loaded"), j3)
                raise_rank(pe, A, 0, 32, lora).then_inc(sg("w_done"), 1)
                pe.wait_ge(sg("lora_made"), 3)
                pe.wait_ge(sg("bonus_used"), j0)
                raise_rank(pe, B, 32, 64, lora).then_inc(sg("a_done"), 1)
                pe.wait_ge(sg("lora_made"), 3)
                pe.wait_ge(sg("w_read"), j1)
                raise_rank(pe, A, 64, 128, lora).then_inc(sg("g_done"), 1)
                pe.wait_ge(sg("w_loaded_k"), 16 * (j + 1))
                pe.wait_ge(sg("a_read"), j1)
                project(pe, B, W["k"]).then_inc(sg("k_done"), 1)
                pe.wait_ge(sg("w_loaded_r"), 16 * (j + 1))
                pe.wait_ge(sg("g_read"), j1)
                project(pe, A, W["r"]).then_inc(sg("r_done"), 1)
                pe.wait_ge(sg("k_read"), 2 * j + 2)
                pe.wait_ge(sg("k_squared"), j1)
                head_sums(pe, B, t2).then_inc(sg("norm_done"), 1)
                pe.wait_ge(sg("w_loaded_v"), 16 * (j + 2))
                pe.wait_ge(sg("r_read"), 2 * j + 2)
                project(pe, A, W["v"]).then_inc(sg("v_done"), 1)
                pe.wait_ge(sg("norm_read"), j1)
                pe.wait_ge(sg("rk_made"), j1)
                head_sums(pe, B, t1).then_inc(sg("bonus_done"), 1)
            pe.wait_ge(sg("w_loaded_v"), 16 * (NJ + 2))
            pe.wait_ge(sg("v_read"), 2 * NJ)
            project(pe, A, W["v"], GR).then_inc(sg("v_done"), 1)
            with pe.Fori(0, 2) as p:
                pe.wait_ge(sg("bonus_used"), NJ)
                pe.wait_ge(sg("made_G"), NJ + p)
                pe.wait_ge(sg("dg_made"), 1)
                pe.wait_ge(sg("gate_up_loaded"), pe.to_reg(16 * (p + 1)))
                for lo in (0, 512, 1024):
                    hi = min(lo + 512, T)
                    mm = pe.matmul(B[:, lo:hi], up[0:GR, :], dg[:, lo:hi], start=True, stop=True)
                mm.then_inc(sg("z_done"), 1)
                for dst, slot, count, read, need in (
                        (A, "k", NJ + 1 + 2 * p, "made_W", NJ + p), (B, "r", NJ + 1 + 2 * p, "z_read", 2 * p + 2),
                        (A, "v", NJ + 3 + 2 * p, "made_R", NJ + p + 1), (B, "k", NJ + 2 + 2 * p, "made_K", NJ + p + 1),
                        (A, "r", NJ + 2 + 2 * p, "made_A", NJ + p + 1), (B, "v", NJ + 4 + 2 * p, "made_B", NJ + p + 1)):
                    pe.wait_ge(sg("w_loaded_" + slot), 16 * count)
                    pe.wait_ge(sg(read), need)
                    project(pe, dst, W[slot]).then_inc(sg(slot + "_done"), 1)

        @block.scalar
        def _(act):
            for q in range(0, KT, 2):
                for r, span in ((0, X1), (1, X2)):
                    nc.scalar.activation(hT[:, q, span], hT[:, q, span], ACT.Identity, scale=c["hscale"][:, q, r:r + 1],
                                         bias=c["modT"][:, q, r:r + 1]).then_inc(sg("h_made"), 1)
            act.wait_ge(sg("sh_loaded"), 16)

            def take(n, src, done, index):
                act.wait_ge(sg(n + "_mixed"), done * 2)
                nc.scalar.copy(raw[n][:, 1:SEQ + 1], src[:, X1]).then_inc(sg(n + "_read"), 1)
                nc.scalar.copy(raw[n][:, SEQ + 2:], src[:, X2]).then_inc(sg(n + "_read"), 1)
                nc.scalar.copy(raw[n][:, SEQ + 1:SEQ + 2], sh[:, index]).then_inc(sg(n + "_before"), 1)

            act.wait_ge(sg("v_done"), 1)
            nc.scalar.copy(raw["v"][:, 1:SEQ + 1], B[:, X1]).then_inc(sg("lora_read"), 1)
            nc.scalar.copy(raw["v"][:, SEQ + 2:], B[:, X2]).then_inc(sg("lora_read"), 1)
            nc.scalar.copy(raw["v"][:, SEQ + 1:SEQ + 2], sh[:, 12:13]).then_inc(sg("lora_read"), 1)
            act.wait_ge(sg("lora_mixed"), 2)
            nc.scalar.activation(lora[0:32, :], kk[0:32, :], ACT.Tanh).then_inc(sg("lora_made"), 1)
            nc.scalar.copy(lora[32:64, :], kk[32:64, :]).then_inc(sg("lora_made"), 1)
            nc.scalar.activation(lora[64:128, :], kk[64:128, :], ACT.Sigmoid).then_inc(sg("lora_made"), 1)
            with act.Fori(0, NJ) as j:
                act.wait_ge(sg("w_done"), j + 1)
                act.wait_ge(sg("prev_made"), j)
                nc.scalar.activation(sig_w[:, :], A, ACT.Sigmoid, bias=col("w0", j)).then_inc(sg("w_read"), 1)
                act.wait_ge(sg("a_done"), j + 1)
                act.wait_ge(sg("kka_made"), j)
                nc.scalar.activation(sig_a[:, :], B, ACT.Sigmoid, bias=col("a0", j)).then_inc(sg("a_read"), 1)
                act.wait_ge(sg("g_done"), j + 1)
                act.wait_ge(sg("made_G"), j)
                act.wait_ge(sg("made_W"), j)
                nc.scalar.copy(gate[:, :], A).then_inc(sg("g_read"), 1)
                nc.scalar.preload_act_table_set("natural_log_exp_and_others")
                act.wait_ge(sg("k_done"), j + 1)
                take("k", B, j, bass.ds(4 + j, 1))
                act.wait_ge(sg("prev_made"), j + 1)
                act.wait_ge(sg("made_R"), j)
                act.wait_ge(sg("made_K"), j)
                act.wait_ge(sg("made_A"), j)
                act.wait_ge(sg("made_B"), j)
                act.wait_ge(sg("end_made"), 2 * j)
                nc.scalar.activation(ep[:, :], b[:, :], ACT.Exp).then_inc(sg("ep_made"), 1)
                nc.scalar.activation(em[:, :], b[:, :], ACT.Exp, scale=-1.0).then_inc(sg("em_made"), 1)
                nc.scalar.activation(eprev[:, :], sig_w[:, :], ACT.Exp).then_inc(sg("eprev_made"), 1)
                nc.scalar.activation(c["decay_mid"][:, bass.ds(j, 1), :].rearrange("p a n -> p (a n)"), mid[:, :], ACT.Exp).then_inc(sg("mid_made"), 1)
                act.wait_ge(sg("k_mixed"), 2 * j + 2)
                act.wait_ge(sg("norm_done"), j)
                nc.scalar.activation(t2[:, :], mix["k"][:, :], ACT.Square, scale=col("kk", j)).then_inc(sg("k_squared"), 1)
                act.wait_ge(sg("r_done"), j + 1)
                take("r", A, j, bass.ds(j, 1))
                act.wait_ge(sg("norm_read"), j + 1)
                nc.scalar.activation(kn[:, :], kn[:, :], ACT.Ln).then_inc(sg("norm_log"), 1)
                act.wait_ge(sg("norm_log"), j + 1)
                nc.scalar.activation(kn[:, :], kn[:, :], ACT.Exp, scale=-0.5).then_inc(sg("norm_made"), 1)
                act.wait_ge(sg("v_done"), j + 2)
                take("v", A, j, bass.ds(8 + j, 1))
            act.wait_ge(sg("v_done"), NJ + 2)
            nc.scalar.copy(dg[:, :], A[0:GR, :]).then_inc(sg("dg_made"), 1)
            with act.Fori(0, 2) as p:
                act.wait_ge(sg("z_done"), p + 1)
                act.wait_ge(sg("la_made"), p)
                act.wait_ge(sg("kka_made"), NJ)
                nc.scalar.activation(sig_a[:, :], B, ACT.Abs, bias=col("bg", p)).then_inc(sg("z_read"), 1)
                act.wait_ge(sg("z_read"), 2 * p + 1)
                act.wait_ge(sg("z_abs"), p)
                nc.scalar.activation(sig_a[:, :], sig_a[:, :], ACT.Exp, scale=-1.0).then_inc(sg("z_abs"), 1)
                act.wait_ge(sg("z_abs"), p + 1)
                nc.scalar.activation(sig_a[:, :], sig_a[:, :], ACT.Ln, bias=1.0).then_inc(sg("z_log"), 1)
                act.wait_ge(sg("b_centred"), 2 * (NJ + p) + 2)
                act.wait_ge(sg("made_R"), NJ + p)
                act.wait_ge(sg("made_K"), NJ + p)
                act.wait_ge(sg("end_made"), 2 * (NJ + p))
                nc.scalar.activation(ep[:, :], b[:, :], ACT.Exp).then_inc(sg("ep_made"), 1)
                nc.scalar.activation(em[:, :], b[:, :], ACT.Exp, scale=-1.0).then_inc(sg("em_made"), 1)
                nc.scalar.activation(c["gla_mid"][:, bass.ds(p, 1), :].rearrange("p a n -> p (a n)"), mid[:, :], ACT.Exp).then_inc(sg("mid_made"), 1)
                act.wait_ge(sg("v_done"), NJ + 3 + 2 * p)
                act.wait_ge(sg("stored_A"), 16 * (NJ + p))
                nc.scalar.copy(out["A"][:, :], A).then_inc(sg("made_A"), 1)
                act.wait_ge(sg("k_done"), NJ + 2 + 2 * p)
                act.wait_ge(sg("stored_B"), 16 * (NJ + p))
                nc.scalar.copy(out["B"][:, :], B).then_inc(sg("made_B"), 1)
                for i, (src, done, buf, name, before) in enumerate(((A, sg("r_done"), t1, "og0", "made_W"), (B, sg("v_done"), t2, "og1", "made_G"))):
                    act.wait_ge(done, NJ + 2 + 2 * p if i == 0 else NJ + 4 + 2 * p)
                    act.wait_ge(sg(before), NJ + p)
                    act.wait_ge(sg("bonus_done"), NJ)
                    nc.scalar.activation(buf[:, :], src, ACT.Exp, scale=-1.0).then_inc(sg(name + "_exp"), 1)
                    act.wait_ge(sg(name + "_exp"), p + 1)
                    nc.scalar.activation(buf[:, :], buf[:, :], ACT.Ln, bias=1.0).then_inc(sg(name + "_log"), 1)
                    act.wait_ge(sg(name + "_log"), p + 1)
                    nc.scalar.activation(buf[:, :], buf[:, :], ACT.Exp, scale=-1.0).then_inc(sg(name + "_sig"), 1)

        @block.vector
        def _(dve):
            for q in range(1, KT, 2):
                for r, span in ((0, X1), (1, X2)):
                    nc.vector.tensor_scalar(hT[:, q, span], hT[:, q, span], c["hscale"][:, q, r:r + 1], c["modT"][:, q, r:r + 1],
                                            ALU.mult, ALU.add).then_inc(sg("h_made"), 1)
            nc.vector.tensor_scalar(omka[:, :], par[:, PC["ka"]:PC["ka"] + NJ], -1.0, 1.0, ALU.mult, ALU.add).then_inc(sg("omka_made"), 1)
            dve.wait_ge(sg("reset_made"), 2)
            dve.wait_ge(sg("omka_made"), 1)

            def token_mix(n, dst, mu, done, index, step):
                r = raw[n]
                nc.vector.tensor_tensor(df[:, X1], r[:, 0:SEQ], r[:, 1:SEQ + 1], ALU.subtract).then_inc(sg("df_made"), 1)
                nc.vector.tensor_tensor(df[:, X2], r[:, SEQ + 1:T + 1], r[:, SEQ + 2:T + 2], ALU.subtract).then_inc(sg("df_made"), 1)
                nc.vector.tensor_copy(shifts[:, index, 0:1], r[:, SEQ:SEQ + 1].unsqueeze(1)).then_inc(sg("shifts_made"), 1)
                nc.vector.tensor_copy(shifts[:, index, 1:2], r[:, T + 1:T + 2].unsqueeze(1)).then_inc(sg("shifts_made"), 1)
                dve.wait_ge(sg("df_made"), 2 * step + 2)
                nc.vector.scalar_tensor_tensor(dst[:, X1], df[:, X1], mu, r[:, 1:SEQ + 1], ALU.mult, ALU.add).then_inc(sg(done), 1)
                nc.vector.scalar_tensor_tensor(dst[:, X2], df[:, X2], mu, r[:, SEQ + 2:], ALU.mult, ALU.add).then_inc(sg(done), 1)

            def centre(i):
                dve.wait_ge(sg("b_summed"), i + 1)
                dve.wait_ge(sg("mid_made"), i)
                nc.vector.tensor_copy(mid[:, 0:NP], tiles(b)[:, :, 63]).then_inc(sg("mid_taken"), 1)
                nc.vector.tensor_copy(mid[:, NP:NT], b[:, SEQ + 63:SEQ + 64]).then_inc(sg("mid_taken"), 1)
                dve.wait_ge(sg("mid_taken"), 2 * i + 2)
                nc.vector.tensor_tensor(tiles(b), tiles(b), mid[:, 0:NP].unsqueeze(2).to_broadcast([P, NP, P]), ALU.subtract).then_inc(sg("b_centred"), 1)
                nc.vector.tensor_scalar(b[:, X2], b[:, X2], mid[:, NP:NT], None, ALU.subtract).then_inc(sg("b_centred"), 1)
                dve.wait_ge(sg("b_centred"), 2 * i + 2)

            def ends(dst, i, at):
                dve.wait_ge(sg("ep_made"), i + 1)
                d2 = dst[:, at, :].rearrange("p a n -> p (a n)")
                nc.vector.tensor_copy(d2[:, 0:NP], tiles(ep)[:, :, P - 1]).then_inc(sg("end_made"), 1)
                nc.vector.tensor_copy(d2[:, NP:NT], ep[:, T - 1:T]).then_inc(sg("end_made"), 1)

            dve.wait_ge(sg("lora_read"), 3)
            token_mix("v", kk, par[:, PC["mu"] + 12:PC["mu"] + 13], "lora_mixed", slice(12, 13), 0)
            dve.wait_ge(sg("lora_made"), 3)
            with dve.Fori(0, NJ) as j:
                dve.wait_ge(sg("w_read"), j + 1)
                nc.vector.tensor_scalar(sig_w[:, :], sig_w[:, :], DECAY_SCALE, None, ALU.mult).then_inc(sg("ld_made"), 1)
                dve.wait_ge(sg("ld_made"), j + 1)
                dve.wait_ge(sg("em_made"), j)
                nc.vector.tensor_tensor_scan(b[:, :], reset[:, :], sig_w[:, :], 0.0, ALU.mult, ALU.add).then_inc(sg("b_summed"), 1)
                centre(j)
                nc.vector.tensor_tensor(sig_w[:, :], b[:, :], sig_w[:, :], ALU.subtract).then_inc(sg("prev_made"), 1)
                dve.wait_ge(sg("a_read"), j + 1)
                dve.wait_ge(sg("bonus_used"), j)
                nc.vector.tensor_scalar(t3[:, :], sig_a[:, :], col("ka", j), omka[:, bass.ds(j, 1)], ALU.mult, ALU.add).then_inc(sg("ka_made"), 1)
                dve.wait_ge(sg("k_read"), 2 * j + 2)
                dve.wait_ge(sg("k_before"), j + 1)
                dve.wait_ge(sg("k_squared"), j)
                token_mix("k", mix["k"], col("mu", j + 4), "k_mixed", bass.ds(4 + j, 1), 3 * j + 1)
                dve.wait_ge(sg("k_mixed"), 2 * j + 2)
                dve.wait_ge(sg("ka_made"), j + 1)
                nc.vector.tensor_tensor(kp[:, :], mix["k"][:, :], t3[:, :], ALU.mult).then_inc(sg("kp_made"), 1)
                nc.vector.tensor_scalar(kk[:, :], mix["k"][:, :], col("kk", j), None, ALU.mult).then_inc(sg("kk_made"), 1)
                dve.wait_ge(sg("r_read"), 2 * j + 2)
                dve.wait_ge(sg("r_before"), j + 1)
                token_mix("r", mix["r"], col("mu", j), "r_mixed", bass.ds(j, 1), 3 * j + 2)
                dve.wait_ge(sg("r_mixed"), 2 * j + 2)
                dve.wait_ge(sg("kp_made"), j + 1)
                dve.wait_ge(sg("bonus_done"), j)
                nc.vector.scalar_tensor_tensor(t1[:, :], mix["r"][:, :], col("rk", j), kp[:, :], ALU.mult, ALU.mult).then_inc(sg("rk_made"), 1)
                dve.wait_ge(sg("norm_done"), j + 1)
                nc.vector.tensor_scalar(kn[:, :], B, 1e-24, None, ALU.max).then_inc(sg("norm_read"), 1)
                dve.wait_ge(sg("norm_made"), j + 1)
                dve.wait_ge(sg("kk_made"), j + 1)
                nc.vector.tensor_tensor(kk[:, :], kk[:, :], kn[:, :], ALU.mult).then_inc(sg("kk_normed"), 1)
                dve.wait_ge(sg("kk_normed"), j + 1)
                nc.vector.tensor_tensor(t3[:, :], kk[:, :], sig_a[:, :], ALU.mult).then_inc(sg("kka_made"), 1)
                dve.wait_ge(sg("eprev_made"), j + 1)
                dve.wait_ge(sg("stored_A"), 16 * j)
                nc.vector.tensor_tensor(out["A"][:, :], kk[:, :], eprev[:, :], ALU.mult).then_inc(sg("made_A"), 1)
                dve.wait_ge(sg("kka_made"), j + 1)
                dve.wait_ge(sg("stored_B"), 16 * j)
                nc.vector.tensor_tensor(out["B"][:, :], t3[:, :], em[:, :], ALU.mult).then_inc(sg("made_B"), 1)
                dve.wait_ge(sg("stored_K"), 16 * j)
                nc.vector.tensor_tensor(out["K"][:, :], kp[:, :], em[:, :], ALU.mult).then_inc(sg("made_K"), 1)
                dve.wait_ge(sg("stored_R"), 16 * j)
                nc.vector.tensor_tensor(out["R"][:, :], mix["r"][:, :], ep[:, :], ALU.mult).then_inc(sg("made_R"), 1)
                ends(c["decay_end"], j, bass.ds(j, 1))
                dve.wait_ge(sg("stored_W"), 16 * j)
                nc.vector.tensor_scalar(out["W"][:, :], gate[:, :], col("lw", j), None, ALU.mult).then_inc(sg("made_W"), 1)
                dve.wait_ge(sg("v_read"), 2 * j + 2)
                dve.wait_ge(sg("v_before"), j + 1)
                dve.wait_ge(sg("stored_V"), 16 * j)
                token_mix("v", mix["v"], col("mu", j + 8), "v_mixed", bass.ds(8 + j, 1), 3 * j + 3)
                dve.wait_ge(sg("v_mixed"), 2 * j + 2)
                dve.wait_ge(sg("bonus_done"), j + 1)
                nc.vector.tensor_tensor(t3[:, :], B, mix["v"][:, :], ALU.mult).then_inc(sg("bonus_used"), 1)
                dve.wait_ge(sg("bonus_used"), j + 1)
                dve.wait_ge(sg("stored_G"), 16 * j)
                nc.vector.scalar_tensor_tensor(out["G"][:, :], t3[:, :], col("lb", j), gate[:, :], ALU.add, ALU.mult).then_inc(sg("made_G"), 1)
            with dve.Fori(0, 2) as p:
                i = NJ + p
                dve.wait_ge(sg("z_read"), 2 * p + 1)
                nc.vector.tensor_scalar(df[:, :], B, col("bg", p), 0.0, ALU.add, ALU.min).then_inc(sg("z_read"), 1)
                dve.wait_ge(sg("z_read"), 2 * p + 2)
                dve.wait_ge(sg("z_log"), p + 1)
                nc.vector.tensor_tensor(df[:, :], df[:, :], sig_a[:, :], ALU.subtract).then_inc(sg("la_made"), 1)
                dve.wait_ge(sg("la_made"), p + 1)
                nc.vector.tensor_scalar(df[:, :], df[:, :], 1.0 / 16.0, None, ALU.mult).then_inc(sg("la_scaled"), 1)
                dve.wait_ge(sg("la_scaled"), p + 1)
                dve.wait_ge(sg("em_made"), i)
                dve.wait_ge(sg("eprev_made"), NJ)
                nc.vector.tensor_tensor_scan(b[:, :], reset[:, :], df[:, :], 0.0, ALU.mult, ALU.add).then_inc(sg("b_summed"), 1)
                centre(i)
                dve.wait_ge(sg("k_done"), NJ + 1 + 2 * p)
                dve.wait_ge(sg("ep_made"), i + 1)
                dve.wait_ge(sg("stored_R"), 16 * i)
                nc.vector.scalar_tensor_tensor(out["R"][:, :], A, 0.125, ep[:, :], ALU.mult, ALU.mult).then_inc(sg("made_R"), 1)
                dve.wait_ge(sg("r_done"), NJ + 1 + 2 * p)
                dve.wait_ge(sg("em_made"), i + 1)
                dve.wait_ge(sg("stored_K"), 16 * i)
                nc.vector.tensor_tensor(out["K"][:, :], B, em[:, :], ALU.mult).then_inc(sg("made_K"), 1)
                ends(c["gla_end"], i, bass.ds(p, 1))
                dve.wait_ge(sg("og0_sig"), p + 1)
                dve.wait_ge(sg("stored_W"), 16 * i)
                nc.vector.scalar_tensor_tensor(out["W"][:, :], A, col("gn", 2 * p), t1[:, :], ALU.mult, ALU.mult).then_inc(sg("made_W"), 1)
                dve.wait_ge(sg("og1_sig"), p + 1)
                dve.wait_ge(sg("stored_G"), 16 * i)
                nc.vector.scalar_tensor_tensor(out["G"][:, :], B, col("gn", 2 * p + 1), t2[:, :], ALU.mult, ALU.mult).then_inc(sg("made_G"), 1)
            dve.wait_ge(sg("shifts_made"), 26)
            dve.wait_ge(sg("end_made"), 12)


def recurrence_block(nc, a, o, d, c, psum):
    with nc.cleanup_on_exit(), ExitStack() as ctx:
        sems = {}

        def sg(name):
            if name not in sems:
                sems[name] = nc.alloc_semaphore(name=name)
            return sems[name]

        def sb(name, shape, dt=F32):
            return ctx.enter_context(nc.sbuf_tensor("mixer_" + name, shape, dt))

        ident, ones, headones = c["ident"], c["ones"], c["headones"]
        feats = [sb(f"feats{u}", [P, F_TILES, P]) for u in range(2)]
        LT, TI, TT, XX, MT, RBT, RKT = [sb(n, [P, 2, 512]) for n in ("LT", "TI", "TT", "XX", "MT", "RBT", "RKT")]
        LTm = sb("LTm", [P, 2, 2, 512])
        ATT, tB, tK, tV, tGV, Gn, SA = [sb(n, [P, 512]) for n in ("ATT", "tB", "tK", "tV", "tGV", "Gn", "SA")]
        tKI = sb("tKI", [P, 256])
        S, Ss = sb("S", [P, NJ, 64]), sb("Ss", [P, NJ, P])
        G, Gs = sb("G", [P, 2, P]), sb("Gs", [P, 4, P])
        Ys, yrs, Os, ors = [sb(n, [P, NJ, P]) for n in ("Ys", "yrs", "Os", "ors")]
        yT = sb("yT", [P, KT, P])
        w_out = sb("w_out", [P, KT, D])
        wr = sb("wr", [P, KT, NG + NE])
        rbias = sb("rbias", [P, NG + NE])
        rows = sb("rows", [P, 2, 3, D])
        x, x1, h2 = [sb(n, [P, D]) for n in ("x", "x1", "h2")]
        h2T = sb("h2T", [P, KT, P])
        eps = sb("eps", [P, 2])
        state_in, gin = sb("state_in", [64, 512]), sb("gin", [P, 2, P])
        wkv, gkeep = sb("wkv", [64, 2, 512]), sb("gkeep", [P, 2, 2, P])
        st = sb("st", [P, 4])

        x_all = [a["x_prompt"].rearrange("a t d -> (a t) d"), a["x_sample"].rearrange("a t d -> (a t) d")]
        feat = d["feat"].rearrange("(f p) t -> p f t", p=P)
        GATE, SCALE, SHIFT = 0, 1, 2
        block = ctx.enter_context(nc.Block())

        def w(eng, name, value):
            if not isinstance(value, int) or value > 0:
                eng.wait_ge(sg(name), value)

        COUNT = {"X_done": (6, 0), "X_read": (6, 0), "C_made": (6, 0), "T_made": (6, 1), "TT_made": (7, 1),
                 "Y_done": (5, 0), "YT_done": (6, 0)}

        def level_of(what, g):
            kind, event = what.split("_")
            return sg(f"{kind}lv{g}_{event}")

        def wl(eng, what, k, g, n):
            per, off = COUNT[what]
            value = per * n + (k + off)
            if not isinstance(value, int) or value > 0:
                eng.wait_ge(level_of(what, g), value)

        def wl_before(eng, what, g, n):
            per, off = COUNT[what]
            if not isinstance(n, int) or n > 0:
                eng.wait_ge(level_of(what, g), per * n)

        def four(buf, g, m):
            return buf[0:m, g, :].rearrange("p (a b) -> p a b", a=4)[:, :, 0:m]

        def four_b(bank, m):
            return bank[0:m, :].rearrange("p (a b) -> p a b", a=4)[:, :, 0:m]

        def mask(name, m):
            return over4(c[name][0:m, 0:m])

        def level(k, m):
            return c["level"][0:m, k:k + 1, 0:m].to_broadcast([m, 4, m])

        def head(h):
            return h // 2, slice(64 * (h % 2), 64 * (h % 2) + 64)

        def last(m):
            return 6 if m == P else 5

        def steps(eng, front, back):
            front(0, 0, P, 0, 1)
            with eng.Fori(0, 3) as k:
                for u in (1, 0):
                    n = 2 * k + (2 - u)
                    front(n, u, P, eng.to_reg(n + 0), eng.to_reg(n + 1))
            front(7, 1, P, 7, 8)

        @block.sync
        def _(sp):
            sp.dma_start(w_out[:, :, :], a["w_out"].rearrange("l (k p) n -> p (l k) n", p=P)).then_inc(sg("w_out_loaded"), 16)
            for r in range(2):
                for i, at in ((GATE, 2), (SCALE, 4), (SHIFT, 3)):
                    sp.dma_start(rows[:, r, i, :], d["mod"][r:r + 1, at * D:(at + 1) * D].to_broadcast([P, D])).then_inc(sg("rows_loaded"), 16)
            sp.dma_start(h2[:, :], a["norm2_g"].to_broadcast([P, D])).then_inc(sg("rows_loaded"), 16)
            sp.dma_start(wr[:, :, 0:NG], a["w_router_group"].rearrange("l (k p) n -> p (l k) n", p=P)).then_inc(sg("router_loaded"), 16)
            sp.dma_start(wr[:, :, NG:], a["w_router_expert"].rearrange("l (k p) n -> p (l k) n", p=P)).then_inc(sg("router_loaded"), 16)
            sp.dma_start(rbias[:, 0:NG], a["b_router_group"].to_broadcast([P, NG])).then_inc(sg("router_loaded"), 16)
            sp.dma_start(rbias[:, NG:], a["b_router_expert"].to_broadcast([P, NE])).then_inc(sg("router_loaded"), 16)

            sp.dma_start(state_in[0:64, :].rearrange("v (h k) -> v h k", h=8), a["state_rwkv_wkv"].rearrange("l b h v k -> v (l b h) k")).then_inc(sg("state_loaded"), 16)
            gla_in = a["state_gla_kv"].rearrange("l b (p q) k v -> q k (l b p) v", q=2)
            for q in range(2):
                sp.dma_start(gin[64 * q:64 * q + 64, :, :], gla_in[q]).then_inc(sg("state_loaded"), 16)

            def store(n, m):
                w(sp, "x1_made", 2 * (n + 1))
                sp.dma_start(d["x1"][bass.ds(n * P, m), :], x1[0:m, :]).then_inc(sg("x1_stored"), 16)
                w(sp, "h2_made", n + 1)
                sp.dma_start(d["h2"][bass.ds(n * P, m), :], h2[0:m, :]).then_inc(sg("h2_stored"), 16)

            def front(n, u, m, n0, n1, x_src=x_all[0]):
                before = n - 1 if isinstance(n, int) else sp.to_reg(n - 1)
                for name in ("O_done", "Y_done", "yg_made", "yr_made"):
                    w(sp, name, before)
                cols = bass.ds(n * P, m)
                for lo, hi in ((0, 16), (16, 28), (28, 40)):
                    sp.dma_start(feats[u][:, lo:hi, 0:m], feat[:, lo:hi, cols]).then_inc(sg(f"feats{u}_loaded"), 16)
                w(sp, "x1_made", 2 * n)
                sp.dma_start(x[0:m, :], x_src[bass.ds(0 if m < P else n * P, m), :]).then_inc(sg("x_loaded"), 16)
                if not (isinstance(n, int) and n == 0):
                    store(n - 1, P)

            steps(sp, front, None)
            front(8, 0, DEC, 8, 9, x_all[1])
            store(8, DEC)
            for i, (wkv_out, gla_out) in enumerate(((o[3], o[4]), (o[6], o[7]))):
                sp.wait_ge(sg("wkv_turned"), i + 1)
                sp.dma_start(wkv_out.rearrange("l b h v k -> v (l b h) k"), wkv[0:64, i, :].rearrange("v (h k) -> v h k", h=8)).then_inc(sg("states_out"), 16)
                sp.wait_ge(sg("G_kept"), i + 1)
                g_out = gla_out.rearrange("l b (p q) k v -> q k (l b p) v", q=2)
                for q in range(2):
                    sp.dma_start(g_out[q], gkeep[64 * q:64 * q + 64, i, :, :]).then_inc(sg("states_out"), 16)
            sp.wait_ge(sg("states_out"), 96)
            sp.wait_ge(sg("x1_stored"), 144)
            sp.wait_ge(sg("h2_stored"), 144)

        @block.tensor
        def _(pe):
            def turn(bank, src, m, n1, name):
                for j in range(src.shape[1]):
                    mm = pe.transpose(bank[0:m, j * P:(j + 1) * P], src[:, j, 0:m], ident[:, :])
                mm.then_inc(sg(name), 1)

            def scores(bank, lhs, rhs, g, m, name):
                for i in range(4):
                    j, q = head(2 * i + g)
                    mm = pe.matmul(bank[0:m, i * P:i * P + m], lhs[q, j, 0:m], rhs[q, j, 0:m], start=True, stop=True)
                mm.then_inc(sg(name), 1)

            def product(bank, lhs, rhs, m, done):
                for i in range(4):
                    mm = pe.matmul(bank[0:m, i * P:i * P + m], lhs[0:m, i * P:i * P + m], rhs[0:m, i * P:i * P + m], start=True, stop=True)
                mm.then_inc(done, 1)

            def back(n0, nm, m):
                def mu():
                    w(pe, "SA_read", n0)
                    w(pe, "Y_read", n0)
                    pe.matmul(psum[7][:, :], headones[:, :], Ys[:, :, :].rearrange("p a b -> p (a b)"), start=True, stop=True).then_inc(sg("mu_done"), 1)

                def gvar():
                    w(pe, "O_squared", n0)
                    w(pe, "mu_read", n0)
                    pe.matmul(psum[7][:, :], ones[:, :], ors[:, :, :].rearrange("p a b -> p (a b)"), start=True, stop=True).then_inc(sg("gvar_done"), 1)

                def var():
                    w(pe, "yc_squared", n0)
                    w(pe, "gvar_read", n0)
                    pe.matmul(psum[7][:, :], headones[:, :], yrs[:, :, :].rearrange("p a b -> p (a b)"), start=True, stop=True).then_inc(sg("var_done"), 1)

                def wo(half):
                    def run():
                        w(pe, ("RBT0_read", "RBT1_read")[half], back.n1)
                        w(pe, ("G_read", "var_read")[half], n0)
                        w(pe, "yr_made", n0)
                        w(pe, "yg_made", n0)
                        pe.wait_ge(sg("w_out_loaded"), 16)
                        for q in range(KT):
                            mm = pe.matmul(psum[6 + half][0:m, :], yT[:, q, 0:m], w_out[:, q, 512 * half:512 * half + 512],
                                           start=q == 0, stop=q == KT - 1)
                        mm.then_inc(sg(f"wo{half}_done"), 1)
                    return run

                def ht(half):
                    def run():
                        w(pe, ("TGV_read", "TKI_read")[half], back.n1)
                        w(pe, "h2_made", n0)
                        b_ = psum[7 - half]
                        for q in range(4):
                            mm = pe.transpose(b_[:, q * P:q * P + m], h2[0:m, (4 * half + q) * P:(4 * half + q + 1) * P], ident[0:m, 0:m])
                        mm.then_inc(sg(f"ht{half}_done"), 1)
                    return run

                def rt():
                    w(pe, "ht0_read", n0)
                    w(pe, "ht1_read", n0)
                    pe.wait_ge(sg("router_loaded"), 64)
                    for q in range(KT):
                        mm = pe.matmul(psum[7][0:m, 0:NG + NE], h2T[:, q, 0:m], wr[:, q, :], start=q == 0, stop=q == KT - 1)
                    mm.then_inc(sg("rt_done"), 1)

                return {"mu": mu, "gvar": gvar, "var": var, "wo0": wo(0), "wo1": wo(1), "ht0": ht(0), "ht1": ht(1), "rt": rt}

            def front(n, u, m, n0, n1):
                F = feats[u]
                fA, fB, fK, fR, fV = [F[:, f:f + NJ, :] for f in (F_A, F_B, F_K, F_R, F_V)]
                fQD, fKI, fGV = F[:, F_QD:F_QD + 2, :], F[:, F_KI:F_KI + 2, :], F[:, F_GV:F_GV + 4, :]
                back.n1 = n1
                bk = back(n0, None, P) if not (isinstance(n, int) and n == 0) else {}
                w(pe, f"feats{u}_loaded", 24 * (n + 2 - u))
                w(pe, "S_made", n0)
                scores(psum[0], fB, fA, 0, m, "LT0_done")
                w(pe, "Y_read", n0)
                scores(psum[1], fB, fA, 1, m, "LT1_done")
                w(pe, "G_made", n0)
                scores(psum[2], fA, fB, 0, m, "L0_done")
                w(pe, "O_squared", n0)
                scores(psum[3], fA, fB, 1, m, "L1_done")

                def filler(name):
                    if name in bk:
                        bk[name]()
                    elif name == "TB":
                        w(pe, "G_read", n0)
                        turn(psum[6], fB, m, n1, "TB_done")
                    elif name == "TV":
                        w(pe, "TB_read", n1)
                        turn(psum[6], fV, m, n1, "TV_done")
                    elif name == "TK":
                        w(pe, "TV_read", n1)
                        turn(psum[6], fK, m, n1, "TK_done")
                    elif name == "MT0":
                        w(pe, "TK_read", n1)
                        scores(psum[6], fK, fA, 0, m, "MT0_done")
                    elif name == "MT1":
                        w(pe, "var_read", n0)
                        scores(psum[7], fK, fA, 1, m, "MT1_done")
                    elif name == "RBT0":
                        w(pe, "MT0_read", n1)
                        scores(psum[6], fB, fR, 0, m, "RBT0_done")
                    elif name == "RBT1":
                        w(pe, "MT1_read", n1)
                        scores(psum[7], fB, fR, 1, m, "RBT1_done")
                    elif name == "RKT0":
                        w(pe, "RBT0_read", n1)
                        w(pe, "x1_made", 2 * n)
                        scores(psum[6], fK, fR, 0, m, "RKT0_done")
                    elif name == "RKT1":
                        w(pe, "RBT1_read", n1)
                        scores(psum[7], fK, fR, 1, m, "RKT1_done")
                    elif name == "ATT":
                        w(pe, "RKT0_read", n1)
                        for hh in (0, 2, 1, 3):
                            j, q = head(hh)
                            if hh == 1:
                                w(pe, "ATT_half", n1)
                            mm = pe.matmul(psum[6][0:m, hh * P:hh * P + m], fKI[q, j, 0:m], fQD[q, j, 0:m], start=True, stop=True)
                            if hh == 2:
                                mm.then_inc(sg("ATT_half"), 1)
                        mm.then_inc(sg("ATT_done"), 1)
                    elif name == "TGV":
                        w(pe, "RKT1_read", n1)
                        turn(psum[7], fGV, m, n1, "TGV_done")
                    elif name == "TKI":
                        w(pe, "ATT_read", n1)
                        turn(psum[6], fKI, m, n1, "TKI_done")

                fill = [["TB", "mu"], ["TV", "gvar"], ["TK", "var"], ["MT0", "MT1"], ["RBT0", "RBT1"], ["wo0"],
                        ["wo1"], ["RKT0", "RKT1"], ["ATT", "TGV"], ["TKI", "ht0"], ["ht1"], ["rt"]]
                for k in range(1, 7):
                    if m == DEC and k == 6:
                        for names in fill[2 * k - 2:]:
                            for name in names:
                                filler(name)
                        continue
                    for g in range(2):
                        wl(pe, "T_made", k - 1, g, n)
                        wl(pe, "C_made", k, g, n)
                        product(psum[g], LTm[:, k % 2, g, :], TI[:, g, :], m, level_of("X_done", g))
                    for name in fill[2 * k - 2]:
                        filler(name)
                    for g in range(2):
                        wl(pe, "X_read", k, g, n)
                        wl(pe, "TT_made", k - 1, g, n)
                        if k < last(m):
                            product(psum[2 + 2 * g], TT[:, g, :], XX[:, g, :], m, level_of("Y_done", g))
                        if k == 1 and g == 0:
                            wl(pe, "T_made", 0, 1, n)
                        product(psum[3 + 2 * g], XX[:, g, :], TT[:, g, :], m, level_of("YT_done", g))
                    for name in fill[2 * k - 1]:
                        filler(name)
                w(pe, "Ss_made", 2 * n + 2)
                w(pe, "MT0_read", n1)
                w(pe, "MT1_read", n1)
                w(pe, "TV_read", n1)
                w(pe, "TKI_read", n1)
                w(pe, "ht1_read", n0)
                for h in range(8):
                    j, q = head(h)
                    g, i = h % 2, h // 2
                    if h % 2 == 0:
                        pe.matmul(psum[6][0:m, P * j:P * j + P], fA[:, j, 0:m], Ss[:, j, :], start=True, stop=False)
                    mm = pe.matmul(psum[6][0:m, 64 * h:64 * h + 64], MT[0:m, g, i * P:i * P + m], tV[0:m, 64 * h:64 * h + 64], start=False, stop=g == 1)
                mm.then_inc(sg("G_done"), 1)
                w(pe, "TGV_read", n1)
                wl(pe, "T_made", last(m) - 1, 0, n)
                for hh in range(4):
                    j, q = head(hh)
                    mm = pe.matmul(psum[2][q, j * P:(j + 1) * P], tKI[0:m, hh * 64:hh * 64 + 64], tGV[0:m, hh * P:(hh + 1) * P], start=True, stop=True)
                mm.then_inc(sg("U_done"), 1)
                w(pe, "ATT_read", n1)
                w(pe, "Gs_made", 2 * n + 2)
                wl(pe, "TT_made", last(m), 0, n)
                for hh in range(4):
                    j, q = head(hh)
                    pe.matmul(psum[3][:, hh * P:hh * P + m], Gs[:, hh, :], fQD[:, j, 0:m], start=True, stop=False)
                    mm = pe.matmul(psum[3][:, hh * P:hh * P + m], tGV[0:m, hh * P:(hh + 1) * P], ATT[0:m, hh * P:hh * P + m], start=False, stop=True)
                mm.then_inc(sg("O_done"), 1)
                w(pe, "G_read", n1)
                wl(pe, "TT_made", last(m), 1, n)
                w(pe, "rt_read", n0)
                for h in range(8):
                    g, i = h % 2, h // 2
                    mm = pe.matmul(psum[7][0:m, 64 * h:64 * h + 64], TT[0:m, g, i * P:i * P + m], Gn[0:m, 64 * h:64 * h + 64], start=True, stop=True)
                mm.then_inc(sg("SA_done"), 1)
                w(pe, "TB_read", n1)
                w(pe, "TK_read", n1)
                w(pe, "SA_read", n1)
                for h in range(8):
                    j, q = head(h)
                    pe.matmul(psum[0][q, 64 * j:64 * j + 64], tB[0:m, 64 * h:64 * h + 64], SA[0:m, 64 * h:64 * h + 64], start=True, stop=False)
                    mm = pe.matmul(psum[0][q, 64 * j:64 * j + 64], tK[0:m, 64 * h:64 * h + 64], tV[0:m, 64 * h:64 * h + 64], start=False, stop=True)
                mm.then_inc(sg("SU_done"), 1)
                pe.wait_ge(sg("w_out_loaded"), 16)
                for g in range(2):
                    w(pe, f"RBT{g}_read", n1)
                w(pe, "RKT0_read", n1)
                w(pe, "RKT1_read", n1)
                for h in range(8):
                    j, q = head(h)
                    g, i = h % 2, h // 2
                    y = psum[1][q, P * j:P * j + m]
                    if h % 2 == 0:
                        pe.matmul(psum[1][:, P * j:P * j + m], Ss[:, j, :], fR[:, j, 0:m], start=True, stop=False)
                    pe.matmul(y, SA[0:m, 64 * h:64 * h + 64], RBT[0:m, g, i * P:i * P + m], start=False, stop=False)
                    mm = pe.matmul(y, tV[0:m, 64 * h:64 * h + 64], RKT[0:m, g, i * P:i * P + m], start=False, stop=True)
                mm.then_inc(sg("Y_done"), 1)

            def turn_state(i):
                pe.wait_ge(sg("S_made"), 8 + i)
                if i == 0:
                    wl(pe, "T_made", 5, 1, 7)
                for j in range(NJ):
                    mm = pe.transpose(psum[4][0:64, j * P:(j + 1) * P], S[:, j, :], ident[:, :])
                mm.then_inc(sg("S_turned"), 1)

            steps(pe, front, back)
            turn_state(0)
            pe.wait_ge(sg("state_loaded"), 48)
            wl(pe, "TT_made", 6, 1, 7)
            for j in range(NJ):
                mm = pe.transpose(psum[5][:, j * 64:(j + 1) * 64], state_in[0:64, j * P:(j + 1) * P], ident[0:64, 0:64])
            mm.then_inc(sg("state_turned"), 1)
            pe.wait_ge(sg("wkv_turned"), 1)
            pe.wait_ge(sg("state_taken"), 2)
            front(8, 0, DEC, 8, 9)
            turn_state(1)
            back.n1 = 9
            bk = back(9, None, DEC)
            for name in ("mu", "gvar", "var", "wo0", "wo1", "ht0", "ht1", "rt"):
                bk[name]()

        @block.gpsimd
        def _(pool):
            nc.gpsimd.memset(eps[:, 0:1], LNX_EPS).then_inc(sg("eps_made"), 1)
            nc.gpsimd.memset(eps[:, 1:2], RMS_EPS).then_inc(sg("eps_made"), 1)
            nc.gpsimd.memset(S[:, :, :], 0.0).then_inc(sg("zero_states"), 1)
            nc.gpsimd.memset(G[:, :, :], 0.0).then_inc(sg("zero_states"), 1)
            nc.gpsimd.memset(Ss[:, :, :], 0.0).then_inc(sg("zero_states"), 1)
            nc.gpsimd.memset(Gs[:, :, :], 0.0).then_inc(sg("zero_states"), 1)

            def front(n, u, m, n0, n1):
                for k in range(1, last(m) + 1):
                    for g in range(2):
                        w(pool, f"LT{g}_read", n1)
                        if k > 2:
                            wl(pool, "X_done", k - 2, g, n)
                        else:
                            wl(pool, "X_done", k - 2, g, n)
                        nc.gpsimd.tensor_tensor(four(LTm[:, k % 2], g, m), four(LT, g, m), level(k, m), ALU.mult).then_inc(level_of("C_made", g), 1)

            steps(pool, front, None)
            front(8, 0, DEC, 8, 9)

        @block.scalar
        def _(act):
            nc.scalar.preload_act_table_set("natural_log_exp_and_others")
            act.wait_ge(sg("eps_made"), 2)

            def flat(t):
                return t[:, :, :].rearrange("p a b -> p (a b)")

            def rsqrt(out, src, scale, e, m, ready, name, count):
                nc.scalar.activation(out, src, ACT.Ln, scale=scale, bias=eps[0:m, e:e + 1]).then_inc(sg(ready), 1)
                w(act, ready, count)
                nc.scalar.activation(out, out, ACT.Exp, scale=-0.5).then_inc(sg(name), 1)

            def back(n0, m):
                def yc():
                    w(act, "mu_read", n0)
                    w(act, "yr_made", n0 - 1 if isinstance(n0, int) else back.nm)
                    nc.scalar.activation(flat(yrs), flat(Ys), ACT.Square).then_inc(sg("yc_squared"), 1)

                def gvar():
                    w(act, "gvar_done", n0)
                    rsqrt(flat(ors), psum[7][:, :], 1.0 / P, 1, P, "gvar_read", "gr_made", n0)

                def var():
                    w(act, "var_done", n0)
                    rsqrt(flat(yrs), psum[7][:, :], 1.0 / 64, 0, P, "var_read", "yrs_made", n0)

                def norm():
                    w(act, "x1_made", 2 * n0 if isinstance(n0, int) else back.n2)
                    w(act, "rt_done", n0 - 1 if isinstance(n0, int) else back.nm)
                    nc.scalar.activation(h2T[0:m, :, :].rearrange("p a b -> p (a b)"), x1[0:m, :], ACT.Square, accum_out=st[0:m, 0:1]).then_inc(sg("x1_squared"), 1)
                    w(act, "x1_squared", n0)
                    rsqrt(st[0:m, 1:2], st[0:m, 0:1], 1.0 / D, 1, m, "x1_log", "x1_rstd", n0)

                def ht(half):
                    w(act, f"ht{half}_done", n0)
                    nc.scalar.copy(h2T[:, 4 * half:4 * half + 4, 0:m], psum[7 - half][:, :].rearrange("p (a b) -> p a b", a=4)[:, :, 0:m]).then_inc(sg(f"ht{half}_read"), 1)

                return yc, gvar, var, norm, ht

            def front(n, u, m, n0, n1):
                first = isinstance(n, int) and n == 0
                if not isinstance(n, int):
                    back.nm = act.to_reg(n - 1)
                    back.n2 = act.to_reg(2 * n)
                yc, gvar, var, norm, ht = back(n0, P)

                def take(bank, dst, name, free=None, scale=1.0):
                    if free:
                        w(act, free, n0)
                    w(act, name + "_done", n1)
                    nc.scalar.activation(dst, bank, ACT.Copy, scale=scale).then_inc(sg(name + "_read"), 1)

                def xk(k):
                    for g in range(2):
                        wl(act, "X_done", k, g, n)
                        if k > 1:
                            wl(act, "YT_done", k - 1, g, n)
                        else:
                            wl_before(act, "YT_done", g, n)
                        nc.scalar.copy(four(XX, g, m), four_b(psum[g], m)).then_inc(level_of("X_read", g), 1)

                xk(1)
                take(psum[6][0:m, :], tB[0:m, :], "TB", "SU_done")
                first or yc()
                take(psum[6][0:m, :], tV[0:m, :], "TV", "Y_done")
                first or gvar()
                xk(2)
                take(psum[6][0:m, :], tK[0:m, :], "TK", "SU_done")
                first or var()
                xk(3)
                xk(4)
                xk(5)
                first or norm()
                take(psum[7][0:m, :], tGV[0:m, :], "TGV", "O_done")
                take(psum[6][0:m, 0:256], tKI[0:m, :], "TKI", "U_done")
                first or ht(0)
                if m == P:
                    xk(6)
                first or ht(1)
                w(act, "SA_done", n0)
                take(psum[6][0:m, :], Gn[0:m, :], "G", None, -1.0)
                w(act, "SU_done", n0)
                w(act, "yg_made", n0)
                take(psum[3][:, :].rearrange("p (a b) -> p a b", a=4)[:, :, 0:m], Os[:, :, 0:m], "O")
                w(act, "O_read", n1)
                nc.scalar.activation(ors[:, :, 0:m], Os[:, :, 0:m], ACT.Square).then_inc(sg("O_squared"), 1)
                take(psum[7][0:m, :], SA[0:m, :], "SA", "Y_done")
                w(act, "yr_made", n0)
                take(psum[1][:, :].rearrange("p (a b) -> p a b", a=4)[:, :, 0:m], Ys[:, :, 0:m], "Y")

            def turned(i):
                act.wait_ge(sg("S_turned"), i + 1)
                nc.scalar.copy(wkv[:, i, :], psum[4][0:64, :]).then_inc(sg("wkv_turned"), 1)

            steps(act, front, None)
            turned(0)
            front(8, 0, DEC, 8, 9)
            turned(1)
            yc, gvar, var, norm, ht = back(9, DEC)
            for stage in (yc, gvar, var, norm):
                stage()
            ht(0)
            ht(1)

        @block.vector
        def _(dve):
            dve.wait_ge(sg("rows_loaded"), 112)
            for r in range(2):
                nc.vector.scalar_tensor_tensor(rows[:, r, SCALE, :], rows[:, r, SCALE, :], 1.0, h2[:, :], ALU.add, ALU.mult).then_inc(sg("rows_made"), 1)
            dve.wait_ge(sg("rows_made"), 2)
            dve.wait_ge(sg("zero_states"), 4)
            dve.wait_ge(sg("router_loaded"), 64)

            def masked(name, bank, dst, g, mk, m, n0, n1, free):
                w(dve, name + "_done", n1)
                w(dve, free, n0) if isinstance(free, str) else wl_before(dve, "C_made", g, free[0])
                nc.vector.tensor_tensor(four(dst, g, m), four_b(bank, m), mask(mk, m), ALU.mult).then_inc(sg(name + "_read"), 1)

            def back(n, u, m, r, n0):
                F = feats[1 - u]

                def mu():
                    w(dve, "mu_done", n0)
                    nc.vector.scalar_tensor_tensor(Ys[:, :, :], psum[7][:, :].rearrange("p (a b) -> p a b", a=4), -1.0 / 64, Ys[:, :, :], ALU.mult, ALU.add).then_inc(sg("mu_read"), 1)

                def yg():
                    w(dve, "gr_made", n0)
                    nc.vector.tensor_tensor(Os[:, :, :], Os[:, :, :], ors[:, :, :], ALU.mult).then_inc(sg("yg_normed"), 1)
                    w(dve, "yg_normed", n0)
                    nc.vector.tensor_tensor(yT[:, 4:8, :], Os[:, :, :], F[:, F_SG:F_SG + 4, :], ALU.mult).then_inc(sg("yg_made"), 1)

                def yr():
                    w(dve, "yrs_made", n0)
                    nc.vector.tensor_tensor(Ys[:, :, :], Ys[:, :, :], yrs[:, :, :], ALU.mult).then_inc(sg("yr_normed"), 1)
                    w(dve, "yr_normed", n0)
                    nc.vector.tensor_tensor(Ys[:, :, :], Ys[:, :, :], F[:, F_WG:F_WG + 4, :], ALU.mult).then_inc(sg("yr_gated"), 1)
                    w(dve, "yr_gated", n0)
                    nc.vector.tensor_tensor(yT[:, 0:4, :], Ys[:, :, :], F[:, F_BG:F_BG + 4, :], ALU.add).then_inc(sg("yr_made"), 1)

                def add(half):
                    cols = slice(512 * half, 512 * half + 512)
                    w(dve, f"wo{half}_done", n0)
                    w(dve, "x1_stored", 16 * (n - 1))
                    nc.vector.tensor_tensor(x1[0:m, cols], psum[6 + half][0:m, :], rows[0:m, r, GATE, cols], ALU.mult).then_inc(sg(f"gated{half}"), 1)
                    w(dve, f"gated{half}", n0)
                    w(dve, "x_loaded", 16 * n)
                    nc.vector.tensor_tensor(x1[0:m, cols], x1[0:m, cols], x[0:m, cols], ALU.add).then_inc(sg("x1_made"), 1)

                def norm():
                    w(dve, "x1_rstd", n0)
                    w(dve, "h2_stored", 16 * (n - 1))
                    nc.vector.scalar_tensor_tensor(h2[0:m, :], x1[0:m, :], st[0:m, 1:2], rows[0:m, r, SCALE, :], ALU.mult, ALU.mult).then_inc(sg("h2_scaled"), 1)
                    w(dve, "h2_scaled", n0)
                    nc.vector.tensor_tensor(h2[0:m, :], h2[0:m, :], rows[0:m, r, SHIFT, :], ALU.add).then_inc(sg("h2_made"), 1)

                def rt():
                    w(dve, "rt_done", n0)
                    nc.vector.tensor_tensor(c["logits"][0:m, bass.ds(n - 1, 1), :].rearrange("p a b -> p (a b)"), psum[7][0:m, 0:NG + NE], rbias[0:m, :], ALU.add).then_inc(sg("rt_read"), 1)

                return mu, yg, yr, add, norm, rt

            def front(n, u, m, n0, n1):
                first = isinstance(n, int) and n == 0
                mu, yg, yr, add, norm, rt = back(n, u, P, 0, n0)
                at = bass.ds(n, 1)
                for g in range(2):
                    masked(f"LT{g}", psum[g], LT, g, "after", m, n0, n1, (n,))
                for g in range(2):
                    w(dve, f"L{g}_done", n1)
                    wl_before(dve, "X_done", g, n)
                    nc.vector.tensor_tensor(four(TI, g, m), four_b(psum[2 + g], m), mask("below", m), ALU.mult).then_inc(sg(f"L{g}_masked"), 1)
                    w(dve, f"LT{g}_read", n1)
                    w(dve, "SA_done", n0)
                    nc.vector.tensor_tensor(four(TT, g, m), four(LT, g, m), level(0, m), ALU.mult).then_inc(sg(f"LT{g}_masked"), 1)
                    w(dve, f"L{g}_masked", n1)
                    nc.vector.tensor_tensor(four(TI, g, m), mask("ident", m), four(TI, g, m), ALU.subtract).then_inc(level_of("T_made", g), 1)
                    w(dve, f"LT{g}_masked", n1)
                    nc.vector.tensor_tensor(four(TT, g, m), mask("ident", m), four(TT, g, m), ALU.subtract).then_inc(level_of("TT_made", g), 1)
                w(dve, "Y_done", n0)
                w(dve, "S_made", n0)
                for v in range(2):
                    q = slice(64 * v, 64 * v + 64)
                    nc.vector.tensor_tensor(Ss[q, :, q], S[q, :, :], c["decay_mid"][q, :, at].to_broadcast([64, NJ, 64]), ALU.mult).then_inc(sg("Ss_made"), 1)
                w(dve, "O_done", n0)
                w(dve, "G_made", n0)
                for v in range(2):
                    q = slice(64 * v, 64 * v + 64)
                    nc.vector.tensor_tensor(Gs[q, v::2, :], G[q, :, :], c["gla_mid"][q, :, at].to_broadcast([64, 2, P]), ALU.mult).then_inc(sg("Gs_made"), 1)
                first or mu()

                def update(k):
                    for g in range(2):
                        if k < last(m):
                            wl(dve, "Y_done", k, g, n)
                            wl(dve, "T_made", k - 1, g, n)
                            nc.vector.tensor_tensor(four(TI, g, m), four(TI, g, m), four_b(psum[2 + 2 * g], m), ALU.subtract).then_inc(level_of("T_made", g), 1)
                        wl(dve, "YT_done", k, g, n)
                        wl(dve, "TT_made", k - 1, g, n)
                        nc.vector.tensor_tensor(four(TT, g, m), four(TT, g, m), four_b(psum[3 + 2 * g], m), ALU.subtract).then_inc(level_of("TT_made", g), 1)

                update(1)
                first or yg()
                update(2)
                masked("MT0", psum[6], MT, 0, "after", m, n0, n1, "G_done")
                masked("MT1", psum[7], MT, 1, "after", m, n0, n1, "G_done")
                first or yr()
                masked("RBT0", psum[6], RBT, 0, "upto", m, n0, n1, "Y_done")
                masked("RBT1", psum[7], RBT, 1, "upto", m, n0, n1, "Y_done")
                update(3)
                first or add(0)
                first or add(1)
                update(4)
                masked("RKT0", psum[6], RKT, 0, "upto", m, n0, n1, "Y_done")
                masked("RKT1", psum[7], RKT, 1, "upto", m, n0, n1, "Y_done")
                w(dve, "ATT_done", n1)
                w(dve, "O_done", n0)
                nc.vector.tensor_tensor(ATT[0:m, :].rearrange("p (a b) -> p a b", a=4)[:, :, 0:m], four_b(psum[6], m), mask("upto", m), ALU.mult).then_inc(sg("ATT_read"), 1)
                update(5)
                first or norm()
                if m == P:
                    update(6)
                first or rt()
                w(dve, "U_done", n1)
                for v in range(2):
                    q = slice(64 * v, 64 * v + 64)
                    nc.vector.tensor_tensor(G[q, :, :], Gs[q, v::2, :], psum[2][q, 0:256].rearrange("p (a b) -> p a b", a=2), ALU.add).then_inc(sg("G_added"), 1)
                w(dve, "G_added", 2 * n + 2)
                nc.vector.tensor_tensor(G[:, :, :], G[:, :, :], c["gla_end"][:, :, at].to_broadcast([P, 2, P]), ALU.mult).then_inc(sg("G_made"), 1)
                w(dve, "SU_done", n1)
                for v in range(2):
                    q = slice(64 * v, 64 * v + 64)
                    nc.vector.tensor_tensor(S[q, :, :], Ss[q, :, q], psum[0][q, 0:256].rearrange("p (a b) -> p a b", a=4), ALU.add).then_inc(sg("S_added"), 1)
                w(dve, "S_added", 2 * n + 2)
                nc.vector.tensor_tensor(S[:, :, :], S[:, :, :], c["decay_end"][:, :, at].to_broadcast([P, NJ, 64]), ALU.mult).then_inc(sg("S_made"), 1)

            def keep(i):
                dve.wait_ge(sg("G_made"), 8 + i)
                nc.vector.tensor_copy(gkeep[:, i, :, :], G[:, :, :]).then_inc(sg("G_kept"), 1)

            steps(dve, front, None)
            keep(0)
            dve.wait_ge(sg("state_loaded"), 48)
            dve.wait_ge(sg("S_turned"), 1)
            dve.wait_ge(sg("state_turned"), 1)
            dve.wait_ge(sg("G_kept"), 1)
            nc.vector.tensor_copy(S[:, :, :], psum[5][:, 0:256].rearrange("p (a b) -> p a b", a=4)).then_inc(sg("state_taken"), 1)
            nc.vector.tensor_copy(G[:, :, :], gin[:, :, :]).then_inc(sg("state_taken"), 1)
            dve.wait_ge(sg("state_taken"), 2)
            front(8, 0, DEC, 8, 9)
            keep(1)
            mu, yg, yr, add, norm, rt = back(9, 1, DEC, 1, 9)
            for stage in (mu, yg, yr):
                stage()
            add(0)
            add(1)
            norm()
            rt()
            dve.wait_ge(sg("G_kept"), 2)
            dve.wait_ge(sg("rt_read"), 9)


def experts_block(nc, a, d, c, psum):
    with nc.cleanup_on_exit(), ExitStack() as ctx:
        sems = {}

        def sg(name):
            if name not in sems:
                sems[name] = nc.alloc_semaphore(name="moe_" + name)
            return sems[name]

        def sb(name, shape, dt=F32):
            return ctx.enter_context(nc.sbuf_tensor("moe_" + name, shape, dt))

        ident, ones, after, logits = c["ident"], c["ones"], c["after"], c["logits"]
        E4 = [P, NT, 4]
        E16 = [P, NT, NG, EG]
        lg, ex, eq, group = [sb(n, E4) for n in ("lg", "ex", "eq", "group")]
        le, prob, prob2 = [sb(n, E4) for n in ("le", "prob", "prob2")]
        picked = [sb(f"picked{i}", E4) for i in range(2)]
        tmp16 = sb("tmp16", E16)
        chosen = [sb(f"chosen{i}", E16) for i in range(2)]
        either = sb("either", E16)
        gmax, first, pg, emax, v1, v2 = [sb(n, [P, NT]) for n in ("gmax", "first", "pg", "emax", "v1", "v2")]
        count_i = sb("count_i", [P, 64], I32)
        count = sb("count", [P, 64])
        token = sb("token", [P, NT], I32)
        rank, counts, carry, slot = [sb(n, [P, NT, NE]) for n in ("rank", "counts", "carry", "slot")]
        total, nblk, end, start = [sb(n, [P, NE]) for n in ("total", "nblk", "end", "start")]
        over = sb("over", [P, NE, NT])
        tri, prod = sb("tri", [P, NE, NE]), sb("prod", [P, NE, NE])
        ended = sb("ended", [P, NB, NE])
        be, slot_f = sb("be", [P, NB]), sb("slot_f", [P, NT, 2])
        blk_i, row_f, row_i = sb("blk_i", [P, NT, 2], I32), sb("row_f", [P, NT, 2]), sb("row_i", [P, NT, 2], I32)
        blk_f = sb("blk_f", [P, NT, 2])
        sent = sb("sent", [P, NT, 2, 2], I32)
        zero = sb("zero", [P, NB * 2], I32)
        plan = sb("plan", [P, NB, 2], I32)

        wg, wu = [sb(n, [P, 2, KT, DE]) for n in ("wg", "wu")]
        wd = sb("wd", [P, 2, DE // P, D])
        idx = sb("idx", [P, 2], I32)
        xg = sb("xg", [P, 2, D])
        xT = sb("xT", [P, 2, KT, P])
        sil, hid = sb("sil", [P, DE]), sb("hid", [P, DE])
        hT = sb("hT", [P, DE // P, P])
        yrow = sb("yrow", [P, 2, D])
        slots, block_expert = c["slots"], c["block_expert"]

        gate = a["w_expert_gate"].rearrange("l e (k p) n -> p (l e) k n", p=P)
        up = a["w_expert_up"].rearrange("l e (k p) n -> p (l e) k n", p=P)
        down = a["w_expert_down"].rearrange("l e (k p) n -> p (l e) k n", p=P)
        plan_rows = d["tok"].rearrange("(p b) c -> p (b c)", p=P)

        block = ctx.enter_context(nc.Block())

        def w(eng, name, value):
            if not isinstance(value, int) or value > 0:
                eng.wait_ge(sg(name), value)

        def blocks(eng, step):
            step(0, 0)
            with eng.Fori(0, NB // 2 - 1) as k:
                for u in (1, 0):
                    step(2 * k + (2 - u), u)
            step(NB - 1, 1)

        @block.sync
        def _(sp):
            sp.wait_ge(sg("zero_made"), 1)
            sp.dma_start(plan_rows, zero[:, :]).then_inc(sg("plan_zeroed"), 16)
            sp.wait_ge(sg("block_expert_made"), 1)

            def step(b, u):
                e = sp.value_load(block_expert[0:1, bass.ds(b, 1)], min_val=0, max_val=NE - 1)
                before = b - 1 if isinstance(b, int) else sp.to_reg(b - 1)
                w(sp, "gate_done", before)
                sp.dma_start(wg[:, u], gate[:, bass.ds(e, 1)].rearrange("p e k n -> p (e k) n")).then_inc(sg(f"gate{u}_loaded"), 16)
                w(sp, "up_done", before)
                sp.dma_start(wu[:, u], up[:, bass.ds(e, 1)].rearrange("p e k n -> p (e k) n")).then_inc(sg(f"up{u}_loaded"), 16)
                w(sp, "down1_done", before)
                sp.dma_start(wd[:, u], down[:, bass.ds(e, 1)].rearrange("p e k n -> p (e k) n")).then_inc(sg(f"down{u}_loaded"), 16)

            blocks(sp, step)

        @block.gpsimd
        def _(pool):
            nc.gpsimd.memset(zero[:, :], 0).then_inc(sg("zero_made"), 1)
            nc.gpsimd.memset(carry[:, 0, :], 0.0).then_inc(sg("carry_zeroed"), 1)
            nc.gpsimd.iota(count_i[:, :], [[1, 64]], base=0, channel_multiplier=0).then_inc(sg("iotas_made"), 1)
            nc.gpsimd.iota(token[:, :], [[P, NT]], base=0, channel_multiplier=1).then_inc(sg("iotas_made"), 1)
            pool.wait_ge(sg("sent_made"), 5)
            pool.wait_ge(sg("plan_zeroed"), 16)
            for n in range(NT):
                m = P if n < NP else DEC
                for i in range(2):
                    pool.indirect_dma_start(out=d["tok"], out_offset=bass.IndirectOffsetOnAxis(ap=row_i[0:m, n, i:i + 1], axis=0),
                                            in_=sent[0:m, n, i, :], in_offset=None).then_inc(sg("plan_sent"), 16)
            pool.wait_ge(sg("plan_sent"), 16 * 2 * NT)
            pool.dma_start(plan[:, :, :].rearrange("p b c -> p (b c)"), plan_rows).then_inc(sg("plan_loaded"), 16)
            pool.wait_ge(sg("plan_loaded"), 16)

            def step(b, u):
                before = b - 1 if isinstance(b, int) else pool.to_reg(b - 1)
                w(pool, "xT1_done", before)
                nc.gpsimd.tensor_copy(idx[:, u:u + 1], plan[:, bass.ds(b, 1), 0]).then_inc(sg("idx_made"), 1)
                now = b + 1 if isinstance(b, int) else pool.to_reg(b + 1)
                pool.wait_ge(sg("plan_loaded"), 16)
                pool.wait_ge(sg("idx_made"), now)
                pool.indirect_dma_start(out=xg[:, u, :], out_offset=None, in_=d["h2"],
                                        in_offset=bass.IndirectOffsetOnAxis(ap=idx[:, u:u + 1], axis=0)).then_inc(sg(f"x{u}_loaded"), 16)

            blocks(pool, step)

        @block.tensor
        def _(pe):
            pe.wait_ge(sg("either_made"), 1)
            flat = either[:, :, :, :].rearrange("p n g e -> p (n g e)")
            pe.matmul(psum[0][:, 0:NT * NE], after[:, :], flat, start=True, stop=True).then_inc(sg("ranked"), 1)
            pe.matmul(psum[1][:, 0:NT * NE], ones[:, :], flat, start=True, stop=True).then_inc(sg("counted"), 1)

            def turn_x(b, u, b1):
                pe.wait_ge(sg(f"x{u}_loaded"), 8 * (b + 2 - u))
                for h in range(2):
                    w(pe, f"xT{h}_read", b)
                    for q in range(4):
                        mm = pe.transpose(psum[3 + h][:, q * P:(q + 1) * P], xg[:, u, (4 * h + q) * P:(4 * h + q + 1) * P], ident[:, :])
                    mm.then_inc(sg(f"xT{h}_done"), 1)

            def gate_up(b, u, b1):
                pe.wait_ge(sg("xT0_read"), b1)
                pe.wait_ge(sg("xT1_read"), b1)
                for name, wt, bank, used in (("gate", wg, psum[0], "gate_read"), ("up", wu, psum[1], "hid_made")):
                    pe.wait_ge(sg(f"{name}{u}_loaded"), 8 * (b + 2 - u))
                    w(pe, used, b)
                    for q in range(KT):
                        mm = pe.matmul(bank[:, :], xT[:, u, q, :], wt[:, u, q, :], start=q == 0, stop=q == KT - 1)
                    mm.then_inc(sg(f"{name}_done"), 1)

            def turn_hid(b, b1):
                w(pe, "hid_made", b1)
                w(pe, "hT_read", b)
                for q in range(4):
                    mm = pe.transpose(psum[2][:, q * P:(q + 1) * P], hid[:, q * P:(q + 1) * P], ident[:, :])
                mm.then_inc(sg("hT_done"), 1)

            def down_rows(b, u, b1):
                pe.wait_ge(sg("hT_read"), b1)
                pe.wait_ge(sg(f"down{u}_loaded"), 8 * (b + 2 - u))
                for h in range(2):
                    w(pe, f"down{h}_read", b)
                    for q in range(DE // P):
                        mm = pe.matmul(psum[5 + h][:, :], hT[:, q, :], wd[:, u, q, 512 * h:512 * h + 512], start=q == 0, stop=q == DE // P - 1)
                    mm.then_inc(sg(f"down{h}_done"), 1)

            def step(b, u):
                first, final = isinstance(b, int) and b == 0, isinstance(b, int) and b == NB - 1
                now, nxt, nxt2 = (b, b + 1, b + 2) if isinstance(b, int) else (pe.to_reg(b + 0), pe.to_reg(b + 1), pe.to_reg(b + 2))
                before = b - 1 if isinstance(b, int) else pe.to_reg(b - 1)
                if first:
                    turn_x(0, 0, 1)
                gate_up(b, u, nxt)
                first or turn_hid(before, now)
                final or turn_x(nxt if isinstance(b, int) else b + 1, 1 - u, nxt2)
                first or down_rows(before if isinstance(b, int) else b - 1, 1 - u, now)

            pe.wait_ge(sg("rank_read"), 2)
            blocks(pe, step)
            turn_hid(NB - 1, NB)
            down_rows(NB - 1, 1, NB)

        @block.scalar
        def _(act):
            nc.scalar.preload_act_table_set("natural_log_exp_and_others")
            act.wait_ge(sg("lg_shifted"), 1)
            nc.scalar.activation(ex[:, :, :], lg[:, :, :], ACT.Exp).then_inc(sg("ex_made"), 1)
            act.wait_ge(sg("le_shifted"), 1)
            nc.scalar.activation(prob[:, :, :], le[:, :, :], ACT.Exp).then_inc(sg("ex_made"), 1)

            def down_read(b, u, b1):
                w(act, f"y{u}_stored", 8 * (b - u))
                for h in range(2):
                    act.wait_ge(sg("plan_loaded"), 16)
                    act.wait_ge(sg(f"down{h}_done"), b1)
                    nc.scalar.activation(yrow[:, u, 512 * h:512 * h + 512], psum[5 + h][:, :], ACT.Copy,
                                         scale=plan[:, bass.ds(b, 1), 1].bitcast(F32)).then_inc(sg(f"down{h}_read"), 1)
                act.wait_ge(sg("down0_read"), b1)
                act.wait_ge(sg("down1_read"), b1)
                act.dma_start(d["y"][bass.ds(b * P, P), :], yrow[:, u, :]).then_inc(sg(f"y{u}_stored"), 16)

            def step(b, u):
                first, final = isinstance(b, int) and b == 0, isinstance(b, int) and b == NB - 1
                now, nxt, nxt2 = (b, b + 1, b + 2) if isinstance(b, int) else (act.to_reg(b + 0), act.to_reg(b + 1), act.to_reg(b + 2))
                if first:
                    x_read(0, 0, 1)
                act.wait_ge(sg("gate_done"), nxt)
                w(act, "hid_made", now)
                nc.scalar.activation(sil[:, :], psum[0][:, :], ACT.Silu).then_inc(sg("gate_read"), 1)
                final or x_read(b + 1, 1 - u, nxt2)
                first or down_read(b - 1, 1 - u, now)

            def x_read(b, u, b1):
                act.wait_ge(sg("xT0_done"), b1)
                w(act, "up_done", b - 1 if isinstance(b, int) else act.to_reg(b - 1))
                nc.scalar.copy(xT[:, u, 0:4, :], psum[3][:, :].rearrange("p (a b) -> p a b", a=4)).then_inc(sg("xT0_read"), 1)

            act.wait_ge(sg("plan_loaded"), 16)
            blocks(act, step)
            down_read(NB - 1, 1, NB)
            for u in range(2):
                act.wait_ge(sg(f"y{u}_stored"), 8 * NB)

        @block.vector
        def _(dve):
            done = [0]

            def then(op):
                done[0] += 1
                op.then_inc(sg("route_step"), 1)
                dve.wait_ge(sg("route_step"), done[0])

            def wide(v, shape):
                return v.unsqueeze(2).to_broadcast(shape)

            V = nc.vector
            def reduce(out, in_, op):
                return V.tensor_reduce(out=out, in_=in_, axis=AX_X, op=op)

            dve.wait_ge(sg("iotas_made"), 2)
            then(V.tensor_copy(count[:, :], count_i[:, :]))
            c4 = count[:, 0:4].unsqueeze(1).to_broadcast(E4)

            def one_hot_of_max(out, v, top):
                then(V.tensor_tensor(eq[:, :, :], v, wide(top, E4), ALU.is_equal))
                then(V.scalar_tensor_tensor(eq[:, :, :], c4, -4.0, eq[:, :, :], ALU.add, ALU.mult))
                then(reduce(first[:, :], eq[:, :, :], ALU.min))
                then(V.tensor_scalar(first[:, :], first[:, :], 4.0, None, ALU.add))
                then(V.tensor_tensor(out, c4, wide(first[:, :], E4), ALU.is_equal))

            then(reduce(gmax[:, :], logits[:, :, 0:NG], ALU.max))
            V.tensor_tensor(lg[:, :, :], logits[:, :, 0:NG], wide(gmax[:, :], E4), ALU.subtract).then_inc(sg("lg_shifted"), 1)
            one_hot_of_max(group[:, :, :], logits[:, :, 0:NG], gmax[:, :])
            then(V.tensor_tensor(tmp16[:, :, :, :], logits[:, :, NG:].rearrange("p n (g e) -> p n g e", g=NG),
                                 group[:, :, :].unsqueeze(3).to_broadcast(E16), ALU.mult))
            then(reduce(le[:, :, :], tmp16[:, :, :, :].rearrange("p n g e -> p n e g"), ALU.add))
            then(reduce(emax[:, :], le[:, :, :], ALU.max))
            V.tensor_tensor(le[:, :, :], le[:, :, :], wide(emax[:, :], E4), ALU.subtract).then_inc(sg("le_shifted"), 1)
            dve.wait_ge(sg("ex_made"), 1)
            then(reduce(pg[:, :], ex[:, :, :], ALU.add))
            then(V.reciprocal(pg[:, :], pg[:, :]))
            dve.wait_ge(sg("ex_made"), 2)
            then(reduce(emax[:, :], prob[:, :, :], ALU.add))
            then(V.reciprocal(emax[:, :], emax[:, :]))
            then(V.tensor_tensor(prob[:, :, :], prob[:, :, :], wide(emax[:, :], E4), ALU.mult))
            then(reduce(v1[:, :], prob[:, :, :], ALU.max))
            one_hot_of_max(picked[0][:, :, :], prob[:, :, :], v1[:, :])
            then(V.scalar_tensor_tensor(prob2[:, :, :], picked[0][:, :, :], -2.0, prob[:, :, :], ALU.mult, ALU.add))
            then(reduce(v2[:, :], prob2[:, :, :], ALU.max))
            one_hot_of_max(picked[1][:, :, :], prob2[:, :, :], v2[:, :])
            for i in range(2):
                then(V.tensor_tensor(chosen[i][:, :, :, :], group[:, :, :].unsqueeze(3).to_broadcast(E16),
                                     picked[i][:, :, :].unsqueeze(2).to_broadcast(E16), ALU.mult))
            then(V.tensor_tensor(either[:, :, :, :], chosen[0][:, :, :, :], chosen[1][:, :, :, :], ALU.add))
            V.memset(either[DEC:P, NP, :, :], 0.0).then_inc(sg("either_made"), 1)
            then(V.tensor_tensor(emax[:, :], v1[:, :], v2[:, :], ALU.add))
            then(V.reciprocal(emax[:, :], emax[:, :]))
            then(V.tensor_tensor(pg[:, :], pg[:, :], emax[:, :], ALU.mult))
            for i, v in enumerate((v1, v2)):
                V.tensor_tensor(sent[:, :, i, 1].bitcast(F32), pg[:, :], v[:, :], ALU.mult).then_inc(sg("sent_made"), 1)
                V.tensor_copy(sent[:, :, i, 0], token[:, :]).then_inc(sg("sent_made"), 1)
            dve.wait_ge(sg("ranked"), 1)
            V.tensor_copy(rank[:, :, :].rearrange("p n e -> p (n e)"), psum[0][:, 0:NT * NE]).then_inc(sg("rank_read"), 1)
            dve.wait_ge(sg("counted"), 1)
            V.tensor_copy(counts[:, :, :].rearrange("p n e -> p (n e)"), psum[1][:, 0:NT * NE]).then_inc(sg("rank_read"), 1)
            dve.wait_ge(sg("rank_read"), 2)
            dve.wait_ge(sg("carry_zeroed"), 1)
            for n in range(1, NT):
                then(V.tensor_tensor(carry[:, n, :], carry[:, n - 1, :], counts[:, n - 1, :], ALU.add))
            then(V.tensor_tensor(total[:, :], carry[:, NP, :], counts[:, NP, :], ALU.add))
            then(V.tensor_scalar(first[:, :], count[:, 0:NT], float(P), None, ALU.mult))
            then(V.tensor_tensor(over[:, :, :], total[:, :].unsqueeze(2).to_broadcast([P, NE, NT]),
                                 first[:, :].unsqueeze(1).to_broadcast([P, NE, NT]), ALU.is_gt))
            then(reduce(nblk[:, :], over[:, :, :], ALU.add))
            then(V.tensor_tensor(tri[:, :, :], count[:, 0:NE].unsqueeze(1).to_broadcast([P, NE, NE]),
                                 count[:, 0:NE].unsqueeze(2).to_broadcast([P, NE, NE]), ALU.is_le))
            then(V.tensor_tensor(prod[:, :, :], tri[:, :, :], nblk[:, :].unsqueeze(1).to_broadcast([P, NE, NE]), ALU.mult))
            then(reduce(end[:, :], prod[:, :, :], ALU.add))
            then(V.tensor_tensor(ended[:, :, :], end[:, :].unsqueeze(1).to_broadcast([P, NB, NE]),
                                 count[:, 0:NB].unsqueeze(2).to_broadcast([P, NB, NE]), ALU.is_le))
            then(reduce(be[:, :], ended[:, :, :], ALU.add))
            V.tensor_scalar(block_expert[0:1, :], be[0:1, :], float(NE - 1), None, ALU.min).then_inc(sg("block_expert_made"), 1)
            then(V.tensor_tensor(start[:, :], end[:, :], nblk[:, :], ALU.subtract))
            then(V.scalar_tensor_tensor(slot[:, :, :], start[:, :].unsqueeze(1).to_broadcast([P, NT, NE]), float(P),
                                        carry[:, :, :], ALU.mult, ALU.add))
            then(V.tensor_tensor(slot[:, :, :], slot[:, :, :], rank[:, :, :], ALU.add))
            for i in range(2):
                then(V.tensor_tensor(rank[:, :, :], slot[:, :, :], chosen[i][:, :, :, :].rearrange("p n g e -> p n (g e)"), ALU.mult))
                then(reduce(slot_f[:, :, i], rank[:, :, :], ALU.add))
            then(V.tensor_copy(slots[:, :, :], slot_f[:, :, :]))
            then(V.tensor_scalar(blk_i[:, :, :], slots[:, :, :], 7, None, ALU.logical_shift_right))
            then(V.tensor_copy(blk_f[:, :, :], blk_i[:, :, :]))
            then(V.tensor_scalar(blk_f[:, :, :], blk_f[:, :, :], float(1 - P * NB), None, ALU.mult))
            then(V.scalar_tensor_tensor(row_f[:, :, :], slot_f[:, :, :], float(NB), blk_f[:, :, :], ALU.mult, ALU.add))
            V.tensor_copy(row_i[:, :, :], row_f[:, :, :]).then_inc(sg("sent_made"), 1)

            def step(b, u):
                first_, final = isinstance(b, int) and b == 0, isinstance(b, int) and b == NB - 1
                now, nxt, nxt2 = (b, b + 1, b + 2) if isinstance(b, int) else (dve.to_reg(b + 0), dve.to_reg(b + 1), dve.to_reg(b + 2))
                if first_:
                    x_read(0, 0, 1)
                dve.wait_ge(sg("up_done"), nxt)
                dve.wait_ge(sg("gate_read"), nxt)
                w(dve, "hT_done", now)
                V.tensor_tensor(hid[:, :], sil[:, :], psum[1][:, :], ALU.mult).then_inc(sg("hid_made"), 1)
                if not first_:
                    h_read(b - 1 if isinstance(b, int) else dve.to_reg(b - 1), now)
                final or x_read(b + 1, 1 - u, nxt2)

            def x_read(b, u, b1):
                dve.wait_ge(sg("xT1_done"), b1)
                w(dve, "up_done", b - 1 if isinstance(b, int) else dve.to_reg(b - 1))
                V.tensor_copy(xT[:, u, 4:8, :], psum[4][:, :].rearrange("p (a b) -> p a b", a=4)).then_inc(sg("xT1_read"), 1)

            def h_read(b, b1):
                dve.wait_ge(sg("hT_done"), b1)
                w(dve, "down1_done", b)
                V.tensor_copy(hT[:, :, :], psum[2][:, :].rearrange("p (a b) -> p a b", a=4)).then_inc(sg("hT_read"), 1)

            blocks(dve, step)
            h_read(NB - 1, NB)


def combine_block(nc, a, o, d, c):
    with nc.cleanup_on_exit(), ExitStack() as ctx:
        sems = {}

        def sg(name):
            if name not in sems:
                sems[name] = nc.alloc_semaphore(name="final_" + name)
            return sems[name]

        def sb(name, shape, dt=F32):
            return ctx.enter_context(nc.sbuf_tensor("final_" + name, shape, dt))

        rows = sb("rows", [P, 2, 3, D])
        normf = sb("normf", [P, D])
        y1, y2, x, sq, out = [sb(n, [P, 2, D]) for n in ("y1", "y2", "x", "sq", "out")]
        idx = sb("idx", [P, 2, 2], I32)
        st = sb("st", [P, 2, 2])
        eps = sb("eps", [P, 1])
        slots = c["slots"]
        GATE, SCALE, SHIFT = 0, 1, 2
        yp = o[0].rearrange("a t d -> (a t) d")
        ys = o[1].rearrange("a t d -> (a t) d")
        block = ctx.enter_context(nc.Block())

        def w(eng, name, value):
            if not isinstance(value, int) or value > 0:
                eng.wait_ge(sg(name), value)

        def tiles(eng, step):
            step(0, 0, P, 0, 1)
            with eng.Fori(0, 3) as k:
                for u in (1, 0):
                    n = 2 * k + (2 - u)
                    step(n, u, P, eng.to_reg(n + 0), eng.to_reg(n + 1))
            step(7, 1, P, 7, 8)
            step(8, 0, DEC, 8, 9)

        @block.sync
        def _(sp):
            for r in range(2):
                for i, at in ((GATE, 5), (SCALE, 7), (SHIFT, 6)):
                    sp.dma_start(rows[:, r, i, :], d["mod"][r:r + 1, at * D:(at + 1) * D].to_broadcast([P, D])).then_inc(sg("rows_loaded"), 16)
            sp.dma_start(normf[:, :], a["normf_g"].rearrange("(l n) -> l n", l=1).to_broadcast([P, D])).then_inc(sg("rows_loaded"), 16)
            for r, i in ((0, 2), (1, 5)):
                with nc.allow_non_contiguous_dma("a row of 13 x 128 from its columns"):
                    sp.dma_start(o[i].rearrange("a b (n p) -> p (a b n)", p=P), c["shifts"][:, :, r]).then_inc(sg("shifts_out"), 16)

            def step(n, u, m, n0, n1):
                before = n - 1 if isinstance(n, int) else sp.to_reg(n - 1)
                w(sp, "out_scaled", before)
                sp.dma_start(x[0:m, u, :], d["x1"][bass.ds(n * P, m), :]).then_inc(sg(f"x{u}_loaded"), 16)

            tiles(sp, step)
            sp.wait_ge(sg("shifts_out"), 32)

        @block.gpsimd
        def _(pool):
            nc.gpsimd.memset(eps[:, :], RMS_EPS).then_inc(sg("eps_made"), 1)

            def step(n, u, m, n0, n1):
                before = n - 1 if isinstance(n, int) else pool.to_reg(n - 1)
                w(pool, "x2_made", before)
                nc.gpsimd.tensor_copy(idx[:, u, :], slots[:, bass.ds(n, 1), :].rearrange("p a b -> p (a b)")).then_inc(sg("idx_made"), 1)
                for i, y in enumerate((y1, y2)):
                    pool.wait_ge(sg("eps_made"), 1)
                    pool.wait_ge(sg("idx_made"), n1)
                    pool.indirect_dma_start(out=y[0:m, u, :], out_offset=None, in_=d["y"],
                                            in_offset=bass.IndirectOffsetOnAxis(ap=idx[0:m, u, i:i + 1], axis=0)).then_inc(sg(f"y{u}_loaded"), 16)

            tiles(pool, step)

        @block.scalar
        def _(act):
            nc.scalar.preload_act_table_set("natural_log_exp_and_others")
            act.wait_ge(sg("eps_made"), 1)

            def step(n, u, m, n0, n1):
                before = n - 1 if isinstance(n, int) else act.to_reg(n - 1)
                w(act, "out_scaled", before)
                w(act, "x2_made", n1)
                nc.scalar.activation(sq[0:m, u, :], x[0:m, u, :], ACT.Square, accum_out=st[0:m, u, 0:1]).then_inc(sg("squared"), 1)
                w(act, "squared", n1)
                nc.scalar.activation(st[0:m, u, 1:2], st[0:m, u, 0:1], ACT.Ln, scale=1.0 / D, bias=eps[0:m, :]).then_inc(sg("log_made"), 1)
                w(act, "log_made", n1)
                nc.scalar.activation(st[0:m, u, 1:2], st[0:m, u, 1:2], ACT.Exp, scale=-0.5).then_inc(sg("rstd_made"), 1)
                act.wait_ge(sg("out_made"), n1)
                dst = yp[bass.ds(n * P, m), :] if m == P else ys
                act.dma_start(dst, out[0:m, u, :]).then_inc(sg(f"out{u}_stored"), 16)

            tiles(act, step)
            act.wait_ge(sg("out0_stored"), 80)
            act.wait_ge(sg("out1_stored"), 64)

        @block.vector
        def _(dve):
            V = nc.vector
            dve.wait_ge(sg("rows_loaded"), 112)
            for r in range(2):
                V.scalar_tensor_tensor(rows[:, r, SCALE, :], rows[:, r, SCALE, :], 1.0, normf[:, :], ALU.add, ALU.mult).then_inc(sg("rows_made"), 1)
            dve.wait_ge(sg("rows_made"), 2)

            def head(n, u, m, n0, n1):
                r = 0 if m == P else 1
                dve.wait_ge(sg(f"y{u}_loaded"), 16 * (n + 2 - u))
                V.tensor_tensor(y1[0:m, u, :], y1[0:m, u, :], y2[0:m, u, :], ALU.add).then_inc(sg("y_summed"), 1)
                dve.wait_ge(sg("y_summed"), n1)
                V.tensor_tensor(y1[0:m, u, :], y1[0:m, u, :], rows[0:m, r, GATE, :], ALU.mult).then_inc(sg("y_gated"), 1)
                dve.wait_ge(sg(f"x{u}_loaded"), 8 * (n + 2 - u))
                dve.wait_ge(sg("y_gated"), n1)
                V.tensor_tensor(x[0:m, u, :], x[0:m, u, :], y1[0:m, u, :], ALU.add).then_inc(sg("x2_made"), 1)

            def tail(n, u, m, n0, n1):
                r = 0 if m == P else 1
                dve.wait_ge(sg("rstd_made"), n1)
                w(dve, f"out{u}_stored", 8 * (n - u))
                V.scalar_tensor_tensor(out[0:m, u, :], x[0:m, u, :], st[0:m, u, 1:2], rows[0:m, r, SCALE, :], ALU.mult, ALU.mult).then_inc(sg("out_scaled"), 1)
                dve.wait_ge(sg("out_scaled"), n1)
                V.tensor_tensor(out[0:m, u, :], out[0:m, u, :], rows[0:m, r, SHIFT, :], ALU.add).then_inc(sg("out_made"), 1)

            def step(n, u, m, n0, n1):
                head(n, u, m, n0, n1)
                tail(n, u, m, n0, n1)

            tiles(dve, step)


INPUTS = ["x_prompt", "x_sample", "c_prompt", "c_sample", "state_rwkv_shift", "state_rwkv_wkv", "state_gla_kv",
          "w_ada", "b_ada", "norm1_g", "norm2_g", "w_in", "mu_shift", "w0", "w_decay_up", "a0", "w_a_up", "w_g_up",
          "k_k", "k_a", "r_k", "lnx_w", "lnx_b", "w_gla_gate_up", "b_gla_gate", "gla_norm_g", "w_out",
          "w_router_group", "b_router_group", "w_router_expert", "b_router_expert",
          "w_expert_gate", "w_expert_up", "w_expert_down", "w_ada_final", "b_ada_final", "normf_g"]
OUTPUTS = [(1, SEQ, D), (1, DEC, D), (1, 1, RP), (1, 1, 8, 64, 64), (1, 1, 4, 64, 128),
           (1, 1, RP), (1, 1, 8, 64, 64), (1, 1, 4, 64, 128)]


def kernel(**inputs):
    import numpy as np
    import concourse.bacc as bacc
    from concourse.bass_utils import run_bass_kernel_spmd

    nc = bacc.Bacc("TRN2", target_bir_lowering=False, num_devices=1)
    arrays, a = {}, {}
    for name in INPUTS:
        arrays[name] = np.ascontiguousarray(inputs[name])
        a[name] = nc.dram_tensor(name, arrays[name].shape, F32, kind="ExternalInput").ap()
    o = [nc.dram_tensor(f"out_{i}", s, F32, kind="ExternalOutput").ap() for i, s in enumerate(OUTPUTS)]
    build(nc, a, o)
    r = run_bass_kernel_spmd(nc, [arrays], core_ids=[0])
    return tuple(r.results[0][f"out_{i}"] for i in range(len(OUTPUTS)))
```

```python
from contextlib import ExitStack

import concourse.bass as bass
from concourse import mybir

F32 = mybir.dt.float32
I32 = mybir.dt.int32
ALU = mybir.AluOpType
ACT = mybir.ActivationFunctionType
AX_X = mybir.AxisListType.X

P = 128
D = 1024
KT = D // P
SEQ = 1024
DEC = 64
T = SEQ + DEC
NP = SEQ // P
NT = NP + 1
RW = 512
NJ = RW // P
RP = 3 * RW + 128
GK, GV, GR = 256, 512, 16
NE, NG, EG = 16, 4, 4
DE = 512
NB = (2 * T + NE * (P - 1)) // P
RMS_EPS, LNX_EPS = 1e-6, 64e-5
DECAY_SCALE = -0.6065306597126334

F_A, F_B, F_K, F_R, F_V, F_WG, F_BG = [NJ * i for i in range(7)]
F_QD, F_KI, F_GV, F_SG = 28, 30, 32, 36
F_TILES = 40
PC = {}
_rows = 0
for _name, _n in (("mu", 13), ("w0", 4), ("a0", 4), ("kk", 4), ("ka", 4), ("rk", 4), ("lw", 4), ("lb", 4),
                  ("bg", 2), ("gn", 4), ("n1", 8), ("sh", 13)):
    PC[_name] = _rows
    _rows += _n
NPAR = _rows


def build(nc, a, o):
    ctx = ExitStack()
    with ctx:
        def sb(name, shape, dt=F32):
            return ctx.enter_context(nc.sbuf_tensor(name, shape, dt))

        def dram(name, shape, dt=F32):
            return nc.dram_tensor(name, shape, dt, kind="Internal").ap()

        d = {
            "mod": dram("mod_rows", (2, 8 * D)),
            "feat": dram("feature_major", (F_TILES * P, T)),
            "x1": dram("x_after_mixer", (T, D)),
            "h2": dram("moe_input", (T, D)),
            "y": dram("expert_rows", (NB * P, D)),
        }
        banks = ctx.enter_context(nc.psum_tensor("banks", [P, 8 * 512], F32))
        psum = [banks[:, 512 * i:512 * i + 512] for i in range(8)]
        c = {
            "ident": sb("ident", [P, P]), "ones": sb("ones", [P, P]), "headones": sb("headones", [P, P]),
            "after": sb("after", [P, P]),
            "upto": sb("upto", [P, P]),
            "below": sb("below", [P, P]),
            "level": sb("level", [P, 7, P]),
            "par": sb("par", [P, NPAR]),
            "modT": sb("modT", [P, 8 * KT, 2]),
            "hscale": sb("hscale", [P, KT, 2]),
            "decay_mid": sb("decay_mid", [P, NJ, NT]),
            "decay_end": sb("decay_end", [P, NJ, NT]),
            "gla_mid": sb("gla_mid", [P, 2, NT]),
            "gla_end": sb("gla_end", [P, 2, NT]),
            "logits": sb("logits", [P, NT, NG + NE]),
            "slots": sb("slots", [P, NT, 2], I32),
            "block_expert": sb("block_expert", [1, NB + 1], I32),
            "shifts": sb("shifts", [P, 13, 2]),
        }
        with nc.sbuf_tensor("xT", [P, KT, T], F32) as xT:
            c["xT"] = xT
            modulation_block(nc, a, d, c, psum)
            projection_block(nc, a, d, c, banks)
        recurrence_block(nc, a, o, d, c, psum)
        with nc.sbuf_tensor("final_rows", [P, 2, 3, D], F32) as final_rows:
            experts_block(nc, a, d, c, psum, final_rows)
            combine_block(nc, a, o, d, c, final_rows)


def bank4(bank):
    return bank[:, :].rearrange("p (a b) -> p a b", a=4)


def over4(mask):
    return mask.unsqueeze(1).to_broadcast([mask.shape[0], 4, mask.shape[1]])


def need(eng, sem, value):
    if not isinstance(value, int) or value > 0:
        eng.wait_ge(sem, value)


def reg(eng, value):
    return value if isinstance(value, int) else eng.to_reg(value)


def modulation_block(nc, a, d, c, psum):
    with nc.cleanup_on_exit(), ExitStack() as ctx:
        def sem(name):
            return nc.alloc_semaphore(name=name)

        def sb(name, shape, dt=F32):
            return ctx.enter_context(nc.sbuf_tensor(name, shape, dt))

        W = sb("wada", [P, 2, KT, 1024])
        brow = sb("brow", [P, 2, 256])
        modrow = sb("modrow", [P, 2, 256])
        cs = sb("cs", [2, D])
        ce = sb("ce", [2, D])
        cT = sb("cT", [P, KT, 32])
        prow = sb("prow", [P, P])
        xin = sb("xin", [P, 2, D])
        xn = sb("xn", [P, 2, D])
        sq = sb("sq", [P, D])
        ss = sb("ss", [P, 2])
        ms = sb("ms", [P, 2])
        rstd = sb("rstd", [P, 2])
        ri = sb("ri", [P, P], I32)
        fi = sb("fi", [P, P], I32)
        xi = sb("xi", [P, P], I32)
        xf = sb("xf", [P, P])
        odd = sb("odd", [P, P])
        odi = sb("odi", [P, P], I32)
        ge = sb("ge", [P, 8, P])
        xT = c["xT"]

        w_loaded = [sem(f"w_loaded{i}") for i in range(2)]
        x_loaded = [sem(f"x_loaded{i}") for i in range(2)]
        c_loaded = sem("c_loaded")
        p_loaded = sem("p_loaded")
        consts_made = sem("consts_made")
        ident_made = sem("ident_made")
        mask_step = sem("mask_step")
        c_step = sem("c_step")
        c_turned = sem("c_turned")
        cT_ready = sem("cT_ready")
        p_turned = sem("p_turned")
        p_read = sem("p_read")
        mod_done = sem("mod_done")
        row_ready = sem("row_ready")
        row_turned = sem("row_turned")
        modT_read = sem("modT_read")
        row_stored = [sem(f"row_stored{i}") for i in range(2)]
        squared = sem("squared")
        rstd_ready = sem("rstd_ready")
        mean_ready = sem("mean_ready")
        log_ready = sem("log_ready")
        xn_ready = sem("xn_ready")
        x_turned = [sem(f"x_turned{i}") for i in range(2)]
        x_read = [sem(f"x_read{i}") for i in range(2)]
        scale_ready = sem("scale_ready")

        xp = a["x_prompt"].rearrange("a t d -> (a t) d")
        xs = a["x_sample"].rearrange("a t d -> (a t) d")
        wa = a["w_ada"].rearrange("l (k p) n -> p (l k) n", p=P)
        wf = a["w_ada_final"].rearrange("(k p) n -> p k n", p=P)
        mod_b = [psum[0], psum[1]]
        x_b = [psum[2], psum[3]]
        row_b = [psum[4], psum[5]]

        cT_zeroed = sem("cT_zeroed")
        block = ctx.enter_context(nc.Block())

        def groups(eng, step):
            step(0, 0)
            step(1, 1)
            with eng.Fori(1, 4) as k:
                for u in range(2):
                    step(2 * k + u, u)

        @block.sync
        def _(sp):
            sp.dma_start(cs[0:1, :], a["c_prompt"]).then_inc(c_loaded, 16)
            sp.dma_start(cs[1:2, :], a["c_sample"]).then_inc(c_loaded, 16)

            def columns(u, src, bias, at):
                sp.dma_start(W[:, u], src[:, :, bass.ds(at, 1024)]).then_inc(w_loaded[u], 16)
                for q in range(4):
                    sp.dma_start(brow[32 * q:32 * q + 32, u, :], bias[:, bass.ds(at + 256 * q, 256)].to_broadcast([32, 256])).then_inc(w_loaded[u], 16)

            def x_tile(n, u):
                sp.dma_start(xin[:, u, :], xp[bass.ds(n * P, P), :]).then_inc(x_loaded[u], 16)

            x_tile(0, 0)
            x_tile(1, 1)
            for name, src in (("mu", a["mu_shift"]), ("w0", a["w0"]), ("a0", a["a0"]), ("kk", a["k_k"]),
                              ("ka", a["k_a"]), ("lw", a["lnx_w"]), ("lb", a["lnx_b"]), ("bg", a["b_gla_gate"]),
                              ("gn", a["gla_norm_g"]), ("n1", a["norm1_g"]), ("sh", a["state_rwkv_shift"])):
                v = src.rearrange("l b (n p) -> (l b n) p", p=P) if name == "sh" else src.rearrange("l (n p) -> (l n) p", p=P)
                sp.dma_start(prow[PC[name]:PC[name] + v.shape[0], :], v).then_inc(p_loaded, 16)
            sp.dma_start(prow[PC["rk"]:PC["rk"] + 4, :],
                         a["r_k"].rearrange("l (n h) k -> (l n) (h k)", h=2)).then_inc(p_loaded, 16)
            for u in range(2):
                columns(u, wa, a["b_ada"], u * 1024)
            b_final = a["b_ada_final"].rearrange("(l n) -> l n", l=1)

            def group(g, u, src, bias, at):
                need(sp, mod_done, g - 1)
                need(sp, row_ready, g - 1)
                columns(u, src, bias, at)
                need(sp, xn_ready, g - 1)
                x_tile(g, u)

            with sp.Fori(1, 3) as k:
                for u in range(2):
                    group(2 * k + u, u, wa, a["b_ada"], 2048 * k + 1024 * u)
            for u in range(2):
                group(6 + u, u, wf, b_final, 1024 * u)
            sp.wait_ge(xn_ready, 7)
            sp.dma_start(xin[0:DEC, 0, :], xs).then_inc(x_loaded[0], 16)

        @block.gpsimd
        def _(pool):
            nc.gpsimd.memset(cT[:, :, :], 0.0).then_inc(cT_zeroed, 1)
            nc.gpsimd.memset(c["ones"][:, :], 1.0).then_inc(consts_made, 1)
            nc.gpsimd.memset(c["headones"][:, :], 0.0).then_inc(consts_made, 1)
            nc.gpsimd.memset(c["logits"][:, :, :], 0.0).then_inc(consts_made, 1)
            nc.gpsimd.iota(ri[:, :], [[0, P]], base=0, channel_multiplier=1).then_inc(consts_made, 1)
            nc.gpsimd.iota(fi[:, :], [[1, P]], base=0, channel_multiplier=0).then_inc(consts_made, 1)
            pool.wait_ge(consts_made, 5)
            nc.gpsimd.memset(c["headones"][0:64, 0:64], 1.0).then_inc(consts_made, 1)
            nc.gpsimd.memset(c["headones"][64:128, 64:128], 1.0).then_inc(consts_made, 1)
            pool.wait_ge(consts_made, 7)
            nc.gpsimd.affine_select(out=c["ident"][:, :], in_=c["ones"][:, :], pattern=[[1, P]], compare_op=ALU.is_equal,
                                    fill=0.0, base=0, channel_multiplier=-1).then_inc(ident_made, 1)
            nc.gpsimd.affine_select(out=c["after"][:, :], in_=c["ones"][:, :], pattern=[[1, P]], compare_op=ALU.is_gt,
                                    fill=0.0, base=0, channel_multiplier=-1).then_inc(ident_made, 1)
            nc.gpsimd.affine_select(out=c["upto"][:, :], in_=c["ones"][:, :], pattern=[[1, P]], compare_op=ALU.is_ge,
                                    fill=0.0, base=0, channel_multiplier=-1).then_inc(ident_made, 1)
            nc.gpsimd.affine_select(out=c["below"][:, :], in_=c["ones"][:, :], pattern=[[1, P]], compare_op=ALU.is_equal,
                                    fill=0.0, base=1, channel_multiplier=-1).then_inc(ident_made, 1)
            pool.wait_ge(consts_made, 7)
            pool.wait_ge(ident_made, 4)
            def store(g, u):
                need(pool, row_ready, g + 1)
                for q in range(4):
                    pool.dma_start(d["mod"][:, bass.ds(1024 * g + 256 * q, 256)], modrow[32 * q:32 * q + 2, u, :]).then_inc(row_stored[u], 16)

            groups(pool, store)
            for u in range(2):
                pool.wait_ge(row_stored[u], 64 * 4)

        @block.tensor
        def _(pe):
            pe.wait_ge(ident_made, 1)
            pe.wait_ge(c_step, 4)
            for k in range(KT):
                mm = pe.transpose(psum[6][:, 2 * k:2 * k + 2], cs[:, k * P:(k + 1) * P], c["ident"][0:2, 0:2])
            mm.then_inc(c_turned, 1)
            pe.wait_ge(p_loaded, 16 * 12)
            pe.transpose(psum[7][:, 0:NPAR], prow[0:NPAR, :], c["ident"][0:NPAR, 0:NPAR]).then_inc(p_turned, 1)
            pe.wait_ge(cT_ready, 1)

            def x_tile(n, u, m):
                need(pe, xn_ready, n + 1)
                for h in range(2):
                    need(pe, x_read[h], n)
                    for q in range(4):
                        mm = pe.transpose(x_b[h][:, q * P:q * P + m], xn[0:m, u, (4 * h + q) * P:(4 * h + q + 1) * P],
                                          c["ident"][0:m, 0:m])
                    mm.then_inc(x_turned[h], 1)

            def turn_row(g, u):
                now = reg(pe, g + 1)
                pe.wait_ge(ident_made, 1)
                pe.wait_ge(row_ready, now)
                need(pe, modT_read, g)
                for h in range(2):
                    mm = pe.transpose(row_b[u][:, P * h:P * h + P], modrow[:, u, P * h:P * h + P], c["ident"][:, :])
                mm.then_inc(row_turned, 1)

            def step(g, u):
                before = reg(pe, g - 1)
                pe.wait_ge(ident_made, 1)
                pe.wait_ge(w_loaded[u], reg(pe, 40 * (g - u) + 80))
                need(pe, row_ready, before)
                for q in range(KT):
                    for r in range(4):
                        mm = pe.matmul(mod_b[u][32 * r:32 * r + 32, 0:256], cT[:, q, :], W[:, u, q, 256 * r:256 * r + 256],
                                       start=q == 0, stop=q == KT - 1)
                mm.then_inc(mod_done, 1)
                x_tile(g, u, P)
                turn_row(g, u)

            groups(pe, step)
            x_tile(NP, 0, DEC)

        @block.scalar
        def _(act):
            nc.scalar.preload_act_table_set("natural_log_exp_and_others")
            act.wait_ge(c_loaded, 32)
            nc.scalar.activation(ce[:, :], cs[:, :], ACT.Exp, scale=-1.0).then_inc(c_step, 1)
            act.wait_ge(c_step, 1)
            nc.scalar.activation(ce[:, :], ce[:, :], ACT.Ln, bias=1.0).then_inc(c_step, 1)
            act.wait_ge(c_step, 2)
            nc.scalar.activation(ce[:, :], ce[:, :], ACT.Exp, scale=-1.0).then_inc(c_step, 1)
            act.wait_ge(p_turned, 1)
            nc.scalar.copy(c["par"][:, :], psum[7][:, 0:NPAR]).then_inc(p_read, 1)

            def rstd_of(n, u, m):
                need(act, mean_ready, n + 1)
                nc.scalar.activation(rstd[0:m, u:u + 1], ms[0:m, u:u + 1], ACT.Ln).then_inc(log_ready, 1)
                need(act, log_ready, n + 1)
                nc.scalar.activation(rstd[0:m, u:u + 1], rstd[0:m, u:u + 1], ACT.Exp, scale=-0.5).then_inc(rstd_ready, 1)

            def evacuate(n, m):
                need(act, x_turned[0], n + 1)
                nc.scalar.copy(xT[:, 0:4, bass.ds(n * P, m)], bank4(x_b[0])[:, :, 0:m]).then_inc(x_read[0], 1)

            def step(g, u):
                need(act, x_loaded[u], 8 * (g - u) + 16)
                need(act, xn_ready, g)
                need(act, squared, g)
                nc.scalar.activation(sq[:, :], xin[:, u, :], ACT.Square, accum_out=ss[:, u:u + 1]).then_inc(squared, 1)
                rstd_of(g, u, P)
                evacuate(g, P)
                need(act, row_turned, g + 1)
                nc.scalar.copy(c["modT"][:, bass.ds(8 * g, 8), :].rearrange("p (q h) r -> p q h r", h=2),
                               row_b[u][:, 0:256].rearrange("p (h q r) -> p q h r", h=2, q=4)[:, :, :, 0:2]).then_inc(modT_read, 1)

            groups(act, step)
            act.wait_ge(x_loaded[0], 16 * 5)
            act.wait_ge(xn_ready, NP)
            act.wait_ge(squared, NP)
            nc.scalar.activation(sq[0:DEC, :], xin[0:DEC, 0, :], ACT.Square, accum_out=ss[0:DEC, 0:1]).then_inc(squared, 1)
            rstd_of(NP, 0, DEC)
            evacuate(NP, DEC)

        @block.vector
        def _(dve):
            dve.wait_ge(c_step, 3)
            nc.vector.tensor_tensor(cs[:, :], cs[:, :], ce[:, :], ALU.mult).then_inc(c_step, 1)
            dve.wait_ge(c_turned, 1)
            dve.wait_ge(cT_zeroed, 1)
            nc.vector.tensor_copy(cT[:, :, 0:2], psum[6][:, 0:2 * KT].rearrange("p (k b) -> p k b", b=2)).then_inc(cT_ready, 1)
            dve.wait_ge(consts_made, 7)
            nc.vector.tensor_tensor(xi[:, :], ri[:, :], fi[:, :], ALU.bitwise_xor).then_inc(mask_step, 1)
            nc.vector.tensor_scalar(odi[:, :], ri[:, :], 1, None, ALU.bitwise_and).then_inc(mask_step, 1)
            dve.wait_ge(mask_step, 2)
            nc.vector.tensor_copy(xf[:, :], xi[:, :]).then_inc(mask_step, 1)
            nc.vector.tensor_copy(odd[:, :], odi[:, :]).then_inc(mask_step, 1)
            dve.wait_ge(mask_step, 4)
            for k in range(8):
                nc.vector.tensor_scalar(ge[:, k, :], xf[:, :], float(2 ** k), None, ALU.is_ge).then_inc(mask_step, 1)
            dve.wait_ge(mask_step, 12)
            dve.wait_ge(ident_made, 4)
            for k in range(7):
                nc.vector.tensor_tensor(c["level"][:, k, :], ge[:, k, :], ge[:, k + 1, :], ALU.subtract).then_inc(mask_step, 1)
            nc.vector.tensor_tensor(c["below"][:, :], c["below"][:, :], odd[:, :], ALU.mult).then_inc(mask_step, 1)
            dve.wait_ge(mask_step, 20)

            def x_tile(n, u, m):
                need(dve, squared, n + 1)
                nc.vector.tensor_scalar(ms[0:m, u:u + 1], ss[0:m, u:u + 1], 1.0 / D, RMS_EPS, ALU.mult, ALU.add).then_inc(mean_ready, 1)
                need(dve, rstd_ready, n + 1)
                nc.vector.tensor_scalar(xn[0:m, u, :], xin[0:m, u, :], rstd[0:m, u:u + 1], None, ALU.mult).then_inc(xn_ready, 1)
                need(dve, x_turned[1], n + 1)
                nc.vector.tensor_copy(xT[:, 4:8, bass.ds(n * P, m)], bank4(x_b[1])[:, :, 0:m]).then_inc(x_read[1], 1)

            def step(g, u):
                need(dve, mod_done, g + 1)
                need(dve, row_stored[u], 32 * (g - u))
                nc.vector.tensor_tensor(modrow[:, u, :], mod_b[u][:, 0:256], brow[:, u, :], ALU.add).then_inc(row_ready, 1)
                x_tile(g, u, P)

            groups(dve, step)
            x_tile(NP, 0, DEC)
            dve.wait_ge(modT_read, 8)
            dve.wait_ge(p_read, 1)
            nc.vector.tensor_scalar(c["hscale"][:, :, :], c["modT"][:, KT:2 * KT, :], 1.0, None, ALU.add).then_inc(scale_ready, 1)
            dve.wait_ge(scale_ready, 1)
            for b in range(2):
                nc.vector.tensor_tensor(c["hscale"][:, :, b], c["hscale"][:, :, b], c["par"][:, PC["n1"]:PC["n1"] + 8], ALU.mult).then_inc(scale_ready, 1)
            dve.wait_ge(scale_ready, 3)


def projection_block(nc, a, d, c, banks):
    with nc.cleanup_on_exit(), ExitStack() as ctx:
        sems = {}

        def sg(name):
            if name not in sems:
                sems[name] = nc.alloc_semaphore(name=name)
            return sems[name]

        def sb(name, shape, dt=F32):
            return ctx.enter_context(nc.sbuf_tensor(name, shape, dt))

        hT = c["xT"]
        par, shifts = c["par"], c["shifts"]
        W = {n: sb("w_" + n, [P, KT, P]) for n in "rkv"}
        up = sb("up", [P, P])
        raw = {n: sb("raw_" + n, [P, T + 2]) for n in "rkv"}
        df = sb("df", [P, T])
        t3, kp, kn = [sb(n, [P, T]) for n in ("t3", "kp", "kn")]
        mid = sb("mid", [P, NT])
        mix = {n: sb("mix_" + n, [P, T]) for n in "rkv"}
        lora = sb("lora", [P, T])
        reset = sb("reset", [P, T])
        sig_w, sig_a, gate, b, t1, t2, kk = [sb(n, [P, T]) for n in ("sig_w", "sig_a", "gate", "b", "t1", "t2", "kkn")]
        ep, em, eprev = [sb(n, [P, T]) for n in ("ep", "em", "eprev")]
        out = {n: sb("out_" + n, [P, T]) for n in "ABKRWG"}
        dg = sb("dg", [GR, T])
        omka = sb("omka", [P, NJ])
        sh = sb("sh_state", [P, 13])
        A, B = banks[:, 0:T], banks[:, 3 * 512:3 * 512 + T]
        X1 = slice(0, SEQ)
        X2 = slice(SEQ, T)
        w_in = a["w_in"].rearrange("l (k p) n -> p (l k) n", p=P)
        feat = d["feat"]
        block = ctx.enter_context(nc.Block())

        def tiles(ap):
            return ap[:, X1].rearrange("p (n t) -> p n t", t=P)

        def col(name, j):
            return par[:, bass.ds(PC[name] + j, 1)]

        @block.sync
        def _(sp):
            def w_load(n, at, m=P):
                sp.dma_start(W[n][:, :, 0:m], w_in[:, :, bass.ds(at, m)]).then_inc(sg("w_loaded_" + n), 16)

            w_load("v", 3 * RW)
            sp.dma_start(sh[:, :], par[:, PC["sh"]:PC["sh"] + 13]).then_inc(sg("sh_loaded"), 16)
            def features(j):
                need(sp, sg("g_done"), j)
                for lo, hi, name in ((0, 32, "w_decay_up"), (32, 64, "w_a_up"), (64, 128, "w_g_up")):
                    sp.dma_start(up[lo:hi, :], a[name][0][:, bass.ds(j * P, P)]).then_inc(sg("up_loaded"), 16)
                need(sp, sg("k_done"), j)
                w_load("k", RW + j * P)
                need(sp, sg("r_done"), j)
                w_load("r", j * P)
                need(sp, sg("v_done"), j + 1)
                w_load("v", 2 * RW + j * P)

            features(0)
            with sp.Fori(1, NJ) as j:
                features(j)
            q0, k0, v0, r0 = RP, RP + GK, RP + 2 * GK, RP + 2 * GK + GV
            g0 = r0 + GR
            sp.wait_ge(sg("v_done"), NJ + 1)
            w_load("v", r0, GR)
            sp.wait_ge(sg("g_done"), NJ)
            def pair_of_heads(p):
                need(sp, sg("z_done"), p)
                sp.dma_start(up[0:GR, :], a["w_gla_gate_up"][0][:, bass.ds(p * P, P)]).then_inc(sg("gate_up_loaded"), 16)
                need(sp, sg("k_done"), NJ + 2 * p)
                w_load("k", q0 + p * P)
                need(sp, sg("r_done"), NJ + 2 * p)
                w_load("r", k0 + p * P)
                need(sp, sg("v_done"), NJ + 2 + 2 * p)
                w_load("v", v0 + 2 * p * P)
                need(sp, sg("k_done"), NJ + 1 + 2 * p)
                w_load("k", v0 + P + 2 * p * P)
                need(sp, sg("r_done"), NJ + 1 + 2 * p)
                w_load("r", g0 + 2 * p * P)
                need(sp, sg("v_done"), NJ + 3 + 2 * p)
                w_load("v", g0 + P + 2 * p * P)

            for p in range(2):
                pair_of_heads(p)

        @block.gpsimd
        def _(pool):
            nc.gpsimd.memset(reset[:, :], 1.0).then_inc(sg("reset_filled"), 1)
            for n in "rkv":
                nc.gpsimd.memset(raw[n][:, 0:1], 0.0).then_inc(sg("reset_filled"), 1)
            pool.wait_ge(sg("reset_filled"), 4)
            nc.gpsimd.memset(tiles(reset)[:, :, 0:1], 0.0).then_inc(sg("reset_made"), 1)
            nc.gpsimd.memset(reset[:, SEQ:SEQ + 1], 0.0).then_inc(sg("reset_made"), 1)

            def store(n, row, src, ready):
                need(pool, sg("made_" + n), ready)
                pool.dma_start(feat[bass.ds(row * P, P), :], src[:, :]).then_inc(sg("stored_" + n), 16)

            def features(j):
                for n, f in (("R", F_R), ("K", F_K), ("A", F_A), ("B", F_B), ("W", F_WG)):
                    store(n, f + j, out[n], j + 1)
                need(pool, sg("v_mixed"), 2 * j + 2)
                pool.dma_start(feat[bass.ds((F_V + j) * P, P), :], mix["v"][:, :]).then_inc(sg("stored_V"), 16)
                store("G", F_BG + j, out["G"], j + 1)

            features(0)
            with pool.Fori(1, NJ) as j:
                features(j)
            def pair_of_heads(p):
                for n, f in (("R", F_QD + p), ("K", F_KI + p), ("A", F_GV + 2 * p), ("B", F_GV + 2 * p + 1),
                             ("W", F_SG + 2 * p), ("G", F_SG + 2 * p + 1)):
                    store(n, f, out[n], NJ + p + 1)

            for p in range(2):
                pair_of_heads(p)
            for n in "ABKRWG":
                need(pool, sg("stored_" + n), 16 * (NJ + 2))
            pool.wait_ge(sg("stored_V"), 16 * NJ)

        def project(pe, dst, w, m=P):
            for lo in (0, 512, 1024):
                hi = min(lo + 512, T)
                for q in range(KT):
                    mm = pe.matmul(dst[0:m, lo:hi], w[:, q, 0:m], hT[:, q, lo:hi], start=q == 0, stop=q == KT - 1)
            return mm

        def raise_rank(pe, dst, lo_row, hi_row, src):
            for lo in (0, 512, 1024):
                hi = min(lo + 512, T)
                mm = pe.matmul(dst[:, lo:hi], up[lo_row:hi_row, :], src[lo_row:hi_row, lo:hi], start=True, stop=True)
            return mm

        def head_sums(pe, dst, src):
            for lo in (0, 512, 1024):
                hi = min(lo + 512, T)
                mm = pe.matmul(dst[:, lo:hi], c["headones"][:, :], src[:, lo:hi], start=True, stop=True)
            return mm

        @block.tensor
        def _(pe):
            pe.wait_ge(sg("h_made"), 2 * KT)
            pe.wait_ge(sg("w_loaded_v"), 16)
            project(pe, B, W["v"]).then_inc(sg("v_done"), 1)
            pe.wait_ge(sg("lora_read"), 2)
            def features(j):
                j0, j1, j3 = reg(pe, j + 0), reg(pe, j + 1), reg(pe, (j + 1) * 48)
                need(pe, sg("v_read"), 2 * j)
                pe.wait_ge(sg("lora_made"), 3)
                need(pe, sg("up_loaded"), j3)
                raise_rank(pe, A, 0, 32, lora).then_inc(sg("w_done"), 1)
                pe.wait_ge(sg("lora_made"), 3)
                need(pe, sg("bonus_used"), j0)
                raise_rank(pe, B, 32, 64, lora).then_inc(sg("a_done"), 1)
                pe.wait_ge(sg("lora_made"), 3)
                need(pe, sg("w_read"), j1)
                raise_rank(pe, A, 64, 128, lora).then_inc(sg("g_done"), 1)
                need(pe, sg("w_loaded_k"), 16 * (j + 1))
                need(pe, sg("a_read"), j1)
                project(pe, B, W["k"]).then_inc(sg("k_done"), 1)
                need(pe, sg("w_loaded_r"), 16 * (j + 1))
                need(pe, sg("g_read"), j1)
                project(pe, A, W["r"]).then_inc(sg("r_done"), 1)
                need(pe, sg("k_read"), 2 * j + 2)
                need(pe, sg("k_squared"), j1)
                head_sums(pe, B, t2).then_inc(sg("norm_done"), 1)
                need(pe, sg("w_loaded_v"), 16 * (j + 2))
                need(pe, sg("r_read"), 2 * j + 2)
                project(pe, A, W["v"]).then_inc(sg("v_done"), 1)
                need(pe, sg("norm_read"), j1)
                need(pe, sg("rk_made"), j1)
                head_sums(pe, B, t1).then_inc(sg("bonus_done"), 1)

            features(0)
            with pe.Fori(1, NJ) as j:
                features(j)
            need(pe, sg("w_loaded_v"), 16 * (NJ + 2))
            pe.wait_ge(sg("v_read"), 2 * NJ)
            project(pe, A, W["v"], GR).then_inc(sg("v_done"), 1)
            def pair_of_heads(p):
                pe.wait_ge(sg("bonus_used"), NJ)
                need(pe, sg("made_G"), NJ + p)
                pe.wait_ge(sg("dg_made"), 1)
                need(pe, sg("gate_up_loaded"), reg(pe, 16 * (p + 1)))
                for lo in (0, 512, 1024):
                    hi = min(lo + 512, T)
                    mm = pe.matmul(B[:, lo:hi], up[0:GR, :], dg[:, lo:hi], start=True, stop=True)
                mm.then_inc(sg("z_done"), 1)
                for dst, slot, count, read, reads in (
                        (A, "k", NJ + 1 + 2 * p, "made_W", NJ + p), (B, "r", NJ + 1 + 2 * p, "z_read", 2 * p + 2),
                        (A, "v", NJ + 3 + 2 * p, "made_R", NJ + p + 1), (B, "k", NJ + 2 + 2 * p, "made_K", NJ + p + 1),
                        (A, "r", NJ + 2 + 2 * p, "made_A", NJ + p + 1), (B, "v", NJ + 4 + 2 * p, "made_B", NJ + p + 1)):
                    need(pe, sg("w_loaded_" + slot), 16 * count)
                    need(pe, sg(read), reads)
                    project(pe, dst, W[slot]).then_inc(sg(slot + "_done"), 1)

            for p in range(2):
                pair_of_heads(p)

        @block.scalar
        def _(act):
            for q in range(0, KT, 2):
                for r, span in ((0, X1), (1, X2)):
                    nc.scalar.activation(hT[:, q, span], hT[:, q, span], ACT.Identity, scale=c["hscale"][:, q, r:r + 1],
                                         bias=c["modT"][:, q, r:r + 1]).then_inc(sg("h_made"), 1)
            act.wait_ge(sg("sh_loaded"), 16)

            def take(n, src, done, index):
                need(act, sg(n + "_mixed"), done * 2)
                nc.scalar.copy(raw[n][:, 1:SEQ + 1], src[:, X1]).then_inc(sg(n + "_read"), 1)
                nc.scalar.copy(raw[n][:, SEQ + 2:], src[:, X2]).then_inc(sg(n + "_read"), 1)
                nc.scalar.copy(raw[n][:, SEQ + 1:SEQ + 2], sh[:, index]).then_inc(sg(n + "_before"), 1)

            act.wait_ge(sg("v_done"), 1)
            nc.scalar.copy(raw["v"][:, 1:SEQ + 1], B[:, X1]).then_inc(sg("lora_read"), 1)
            nc.scalar.copy(raw["v"][:, SEQ + 2:], B[:, X2]).then_inc(sg("lora_read"), 1)
            nc.scalar.copy(raw["v"][:, SEQ + 1:SEQ + 2], sh[:, 12:13]).then_inc(sg("lora_read"), 1)
            act.wait_ge(sg("lora_mixed"), 2)
            nc.scalar.activation(lora[0:32, :], kk[0:32, :], ACT.Tanh).then_inc(sg("lora_made"), 1)
            nc.scalar.copy(lora[32:64, :], kk[32:64, :]).then_inc(sg("lora_made"), 1)
            nc.scalar.activation(lora[64:128, :], kk[64:128, :], ACT.Sigmoid).then_inc(sg("lora_made"), 1)
            def features(j):
                need(act, sg("w_done"), j + 1)
                need(act, sg("prev_made"), j)
                nc.scalar.activation(sig_w[:, :], A, ACT.Sigmoid, bias=col("w0", j)).then_inc(sg("w_read"), 1)
                need(act, sg("a_done"), j + 1)
                need(act, sg("kka_made"), j)
                nc.scalar.activation(sig_a[:, :], B, ACT.Sigmoid, bias=col("a0", j)).then_inc(sg("a_read"), 1)
                need(act, sg("g_done"), j + 1)
                need(act, sg("made_G"), j)
                need(act, sg("made_W"), j)
                nc.scalar.copy(gate[:, :], A).then_inc(sg("g_read"), 1)
                nc.scalar.preload_act_table_set("natural_log_exp_and_others")
                need(act, sg("k_done"), j + 1)
                take("k", B, j, bass.ds(4 + j, 1))
                need(act, sg("prev_made"), j + 1)
                need(act, sg("made_R"), j)
                need(act, sg("made_K"), j)
                need(act, sg("made_A"), j)
                need(act, sg("made_B"), j)
                need(act, sg("end_made"), 2 * j)
                nc.scalar.activation(ep[:, :], b[:, :], ACT.Exp).then_inc(sg("ep_made"), 1)
                nc.scalar.activation(em[:, :], b[:, :], ACT.Exp, scale=-1.0).then_inc(sg("em_made"), 1)
                nc.scalar.activation(eprev[:, :], sig_w[:, :], ACT.Exp).then_inc(sg("eprev_made"), 1)
                nc.scalar.activation(c["decay_mid"][:, bass.ds(j, 1), :].rearrange("p a n -> p (a n)"), mid[:, :], ACT.Exp).then_inc(sg("mid_made"), 1)
                need(act, sg("k_mixed"), 2 * j + 2)
                need(act, sg("norm_done"), j)
                nc.scalar.activation(t2[:, :], mix["k"][:, :], ACT.Square, scale=col("kk", j)).then_inc(sg("k_squared"), 1)
                need(act, sg("r_done"), j + 1)
                take("r", A, j, bass.ds(j, 1))
                need(act, sg("norm_read"), j + 1)
                nc.scalar.activation(kn[:, :], kn[:, :], ACT.Ln).then_inc(sg("norm_log"), 1)
                need(act, sg("norm_log"), j + 1)
                nc.scalar.activation(kn[:, :], kn[:, :], ACT.Exp, scale=-0.5).then_inc(sg("norm_made"), 1)
                need(act, sg("v_done"), j + 2)
                take("v", A, j, bass.ds(8 + j, 1))

            features(0)
            with act.Fori(1, NJ) as j:
                features(j)
            act.wait_ge(sg("v_done"), NJ + 2)
            nc.scalar.copy(dg[:, :], A[0:GR, :]).then_inc(sg("dg_made"), 1)
            def pair_of_heads(p):
                need(act, sg("z_done"), p + 1)
                need(act, sg("la_made"), p)
                act.wait_ge(sg("kka_made"), NJ)
                nc.scalar.activation(sig_a[:, :], B, ACT.Abs, bias=col("bg", p)).then_inc(sg("z_read"), 1)
                need(act, sg("z_read"), 2 * p + 1)
                need(act, sg("z_abs"), p)
                nc.scalar.activation(sig_a[:, :], sig_a[:, :], ACT.Exp, scale=-1.0).then_inc(sg("z_abs"), 1)
                need(act, sg("z_abs"), p + 1)
                nc.scalar.activation(sig_a[:, :], sig_a[:, :], ACT.Ln, bias=1.0).then_inc(sg("z_log"), 1)
                need(act, sg("b_centred"), 2 * (NJ + p) + 2)
                need(act, sg("made_R"), NJ + p)
                need(act, sg("made_K"), NJ + p)
                need(act, sg("end_made"), 2 * (NJ + p))
                nc.scalar.activation(ep[:, :], b[:, :], ACT.Exp).then_inc(sg("ep_made"), 1)
                nc.scalar.activation(em[:, :], b[:, :], ACT.Exp, scale=-1.0).then_inc(sg("em_made"), 1)
                nc.scalar.activation(c["gla_mid"][:, bass.ds(p, 1), :].rearrange("p a n -> p (a n)"), mid[:, :], ACT.Exp).then_inc(sg("mid_made"), 1)
                need(act, sg("v_done"), NJ + 3 + 2 * p)
                need(act, sg("stored_A"), 16 * (NJ + p))
                nc.scalar.copy(out["A"][:, :], A).then_inc(sg("made_A"), 1)
                need(act, sg("k_done"), NJ + 2 + 2 * p)
                need(act, sg("stored_B"), 16 * (NJ + p))
                nc.scalar.copy(out["B"][:, :], B).then_inc(sg("made_B"), 1)
                for i, (src, done, buf, name, before) in enumerate(((A, sg("r_done"), t1, "og0", "made_W"), (B, sg("v_done"), t2, "og1", "made_G"))):
                    need(act, done, NJ + 2 + 2 * p if i == 0 else NJ + 4 + 2 * p)
                    need(act, sg(before), NJ + p)
                    act.wait_ge(sg("bonus_done"), NJ)
                    nc.scalar.activation(buf[:, :], src, ACT.Exp, scale=-1.0).then_inc(sg(name + "_exp"), 1)
                    need(act, sg(name + "_exp"), p + 1)
                    nc.scalar.activation(buf[:, :], buf[:, :], ACT.Ln, bias=1.0).then_inc(sg(name + "_log"), 1)
                    need(act, sg(name + "_log"), p + 1)
                    nc.scalar.activation(buf[:, :], buf[:, :], ACT.Exp, scale=-1.0).then_inc(sg(name + "_sig"), 1)

            for p in range(2):
                pair_of_heads(p)

        @block.vector
        def _(dve):
            for q in range(1, KT, 2):
                for r, span in ((0, X1), (1, X2)):
                    nc.vector.tensor_scalar(hT[:, q, span], hT[:, q, span], c["hscale"][:, q, r:r + 1], c["modT"][:, q, r:r + 1],
                                            ALU.mult, ALU.add).then_inc(sg("h_made"), 1)
            nc.vector.tensor_scalar(omka[:, :], par[:, PC["ka"]:PC["ka"] + NJ], -1.0, 1.0, ALU.mult, ALU.add).then_inc(sg("omka_made"), 1)
            dve.wait_ge(sg("reset_made"), 2)
            dve.wait_ge(sg("omka_made"), 1)

            def token_mix(n, dst, mu, done, index, step):
                r = raw[n]
                nc.vector.tensor_tensor(df[:, X1], r[:, 0:SEQ], r[:, 1:SEQ + 1], ALU.subtract).then_inc(sg("df_made"), 1)
                nc.vector.tensor_tensor(df[:, X2], r[:, SEQ + 1:T + 1], r[:, SEQ + 2:T + 2], ALU.subtract).then_inc(sg("df_made"), 1)
                nc.vector.tensor_copy(shifts[:, index, 0:1], r[:, SEQ:SEQ + 1].unsqueeze(1)).then_inc(sg("shifts_made"), 1)
                nc.vector.tensor_copy(shifts[:, index, 1:2], r[:, T + 1:T + 2].unsqueeze(1)).then_inc(sg("shifts_made"), 1)
                need(dve, sg("df_made"), 2 * step + 2)
                nc.vector.scalar_tensor_tensor(dst[:, X1], df[:, X1], mu, r[:, 1:SEQ + 1], ALU.mult, ALU.add).then_inc(sg(done), 1)
                nc.vector.scalar_tensor_tensor(dst[:, X2], df[:, X2], mu, r[:, SEQ + 2:], ALU.mult, ALU.add).then_inc(sg(done), 1)

            def centre(i):
                need(dve, sg("b_summed"), i + 1)
                need(dve, sg("mid_made"), i)
                nc.vector.tensor_copy(mid[:, 0:NP], tiles(b)[:, :, 63]).then_inc(sg("mid_taken"), 1)
                nc.vector.tensor_copy(mid[:, NP:NT], b[:, SEQ + 63:SEQ + 64]).then_inc(sg("mid_taken"), 1)
                need(dve, sg("mid_taken"), 2 * i + 2)
                nc.vector.tensor_tensor(tiles(b), tiles(b), mid[:, 0:NP].unsqueeze(2).to_broadcast([P, NP, P]), ALU.subtract).then_inc(sg("b_centred"), 1)
                nc.vector.tensor_scalar(b[:, X2], b[:, X2], mid[:, NP:NT], None, ALU.subtract).then_inc(sg("b_centred"), 1)
                need(dve, sg("b_centred"), 2 * i + 2)

            def ends(dst, i, at):
                need(dve, sg("ep_made"), i + 1)
                d2 = dst[:, at, :].rearrange("p a n -> p (a n)")
                nc.vector.tensor_copy(d2[:, 0:NP], tiles(ep)[:, :, P - 1]).then_inc(sg("end_made"), 1)
                nc.vector.tensor_copy(d2[:, NP:NT], ep[:, T - 1:T]).then_inc(sg("end_made"), 1)

            dve.wait_ge(sg("lora_read"), 3)
            token_mix("v", kk, par[:, PC["mu"] + 12:PC["mu"] + 13], "lora_mixed", slice(12, 13), 0)
            dve.wait_ge(sg("lora_made"), 3)
            def features(j):
                need(dve, sg("w_read"), j + 1)
                nc.vector.tensor_scalar(sig_w[:, :], sig_w[:, :], DECAY_SCALE, None, ALU.mult).then_inc(sg("ld_made"), 1)
                need(dve, sg("ld_made"), j + 1)
                need(dve, sg("em_made"), j)
                nc.vector.tensor_tensor_scan(b[:, :], reset[:, :], sig_w[:, :], 0.0, ALU.mult, ALU.add).then_inc(sg("b_summed"), 1)
                centre(j)
                nc.vector.tensor_tensor(sig_w[:, :], b[:, :], sig_w[:, :], ALU.subtract).then_inc(sg("prev_made"), 1)
                need(dve, sg("a_read"), j + 1)
                need(dve, sg("bonus_used"), j)
                nc.vector.tensor_scalar(t3[:, :], sig_a[:, :], col("ka", j), omka[:, bass.ds(j, 1)], ALU.mult, ALU.add).then_inc(sg("ka_made"), 1)
                need(dve, sg("k_read"), 2 * j + 2)
                need(dve, sg("k_before"), j + 1)
                need(dve, sg("k_squared"), j)
                token_mix("k", mix["k"], col("mu", j + 4), "k_mixed", bass.ds(4 + j, 1), 3 * j + 1)
                need(dve, sg("k_mixed"), 2 * j + 2)
                need(dve, sg("ka_made"), j + 1)
                nc.vector.tensor_tensor(kp[:, :], mix["k"][:, :], t3[:, :], ALU.mult).then_inc(sg("kp_made"), 1)
                nc.vector.tensor_scalar(kk[:, :], mix["k"][:, :], col("kk", j), None, ALU.mult).then_inc(sg("kk_made"), 1)
                need(dve, sg("r_read"), 2 * j + 2)
                need(dve, sg("r_before"), j + 1)
                token_mix("r", mix["r"], col("mu", j), "r_mixed", bass.ds(j, 1), 3 * j + 2)
                need(dve, sg("r_mixed"), 2 * j + 2)
                need(dve, sg("kp_made"), j + 1)
                need(dve, sg("bonus_done"), j)
                nc.vector.scalar_tensor_tensor(t1[:, :], mix["r"][:, :], col("rk", j), kp[:, :], ALU.mult, ALU.mult).then_inc(sg("rk_made"), 1)
                need(dve, sg("norm_done"), j + 1)
                nc.vector.tensor_scalar(kn[:, :], B, 1e-24, None, ALU.max).then_inc(sg("norm_read"), 1)
                need(dve, sg("norm_made"), j + 1)
                need(dve, sg("kk_made"), j + 1)
                nc.vector.tensor_tensor(kk[:, :], kk[:, :], kn[:, :], ALU.mult).then_inc(sg("kk_normed"), 1)
                need(dve, sg("kk_normed"), j + 1)
                nc.vector.tensor_tensor(t3[:, :], kk[:, :], sig_a[:, :], ALU.mult).then_inc(sg("kka_made"), 1)
                need(dve, sg("eprev_made"), j + 1)
                need(dve, sg("stored_A"), 16 * j)
                nc.vector.tensor_tensor(out["A"][:, :], kk[:, :], eprev[:, :], ALU.mult).then_inc(sg("made_A"), 1)
                need(dve, sg("kka_made"), j + 1)
                need(dve, sg("stored_B"), 16 * j)
                nc.vector.tensor_tensor(out["B"][:, :], t3[:, :], em[:, :], ALU.mult).then_inc(sg("made_B"), 1)
                need(dve, sg("stored_K"), 16 * j)
                nc.vector.tensor_tensor(out["K"][:, :], kp[:, :], em[:, :], ALU.mult).then_inc(sg("made_K"), 1)
                need(dve, sg("stored_R"), 16 * j)
                nc.vector.tensor_tensor(out["R"][:, :], mix["r"][:, :], ep[:, :], ALU.mult).then_inc(sg("made_R"), 1)
                ends(c["decay_end"], j, bass.ds(j, 1))
                need(dve, sg("stored_W"), 16 * j)
                nc.vector.tensor_scalar(out["W"][:, :], gate[:, :], col("lw", j), None, ALU.mult).then_inc(sg("made_W"), 1)
                need(dve, sg("v_read"), 2 * j + 2)
                need(dve, sg("v_before"), j + 1)
                need(dve, sg("stored_V"), 16 * j)
                token_mix("v", mix["v"], col("mu", j + 8), "v_mixed", bass.ds(8 + j, 1), 3 * j + 3)
                need(dve, sg("v_mixed"), 2 * j + 2)
                need(dve, sg("bonus_done"), j + 1)
                nc.vector.tensor_tensor(t3[:, :], B, mix["v"][:, :], ALU.mult).then_inc(sg("bonus_used"), 1)
                need(dve, sg("bonus_used"), j + 1)
                need(dve, sg("stored_G"), 16 * j)
                nc.vector.scalar_tensor_tensor(out["G"][:, :], t3[:, :], col("lb", j), gate[:, :], ALU.add, ALU.mult).then_inc(sg("made_G"), 1)

            features(0)
            with dve.Fori(1, NJ) as j:
                features(j)
            def pair_of_heads(p):
                i = NJ + p
                need(dve, sg("z_read"), 2 * p + 1)
                nc.vector.tensor_scalar(df[:, :], B, col("bg", p), 0.0, ALU.add, ALU.min).then_inc(sg("z_read"), 1)
                need(dve, sg("z_read"), 2 * p + 2)
                need(dve, sg("z_log"), p + 1)
                nc.vector.tensor_tensor(df[:, :], df[:, :], sig_a[:, :], ALU.subtract).then_inc(sg("la_made"), 1)
                need(dve, sg("la_made"), p + 1)
                nc.vector.tensor_scalar(df[:, :], df[:, :], 1.0 / 16.0, None, ALU.mult).then_inc(sg("la_scaled"), 1)
                need(dve, sg("la_scaled"), p + 1)
                need(dve, sg("em_made"), i)
                dve.wait_ge(sg("eprev_made"), NJ)
                nc.vector.tensor_tensor_scan(b[:, :], reset[:, :], df[:, :], 0.0, ALU.mult, ALU.add).then_inc(sg("b_summed"), 1)
                centre(i)
                need(dve, sg("k_done"), NJ + 1 + 2 * p)
                need(dve, sg("ep_made"), i + 1)
                need(dve, sg("stored_R"), 16 * i)
                nc.vector.scalar_tensor_tensor(out["R"][:, :], A, 0.125, ep[:, :], ALU.mult, ALU.mult).then_inc(sg("made_R"), 1)
                need(dve, sg("r_done"), NJ + 1 + 2 * p)
                need(dve, sg("em_made"), i + 1)
                need(dve, sg("stored_K"), 16 * i)
                nc.vector.tensor_tensor(out["K"][:, :], B, em[:, :], ALU.mult).then_inc(sg("made_K"), 1)
                ends(c["gla_end"], i, bass.ds(p, 1))
                need(dve, sg("og0_sig"), p + 1)
                need(dve, sg("stored_W"), 16 * i)
                nc.vector.scalar_tensor_tensor(out["W"][:, :], A, col("gn", 2 * p), t1[:, :], ALU.mult, ALU.mult).then_inc(sg("made_W"), 1)
                need(dve, sg("og1_sig"), p + 1)
                need(dve, sg("stored_G"), 16 * i)
                nc.vector.scalar_tensor_tensor(out["G"][:, :], B, col("gn", 2 * p + 1), t2[:, :], ALU.mult, ALU.mult).then_inc(sg("made_G"), 1)

            for p in range(2):
                pair_of_heads(p)
            dve.wait_ge(sg("shifts_made"), 26)
            dve.wait_ge(sg("end_made"), 12)


def recurrence_block(nc, a, o, d, c, psum):
    with nc.cleanup_on_exit(), ExitStack() as ctx:
        sems = {}

        def sg(name):
            if name not in sems:
                sems[name] = nc.alloc_semaphore(name=name)
            return sems[name]

        def sb(name, shape, dt=F32):
            return ctx.enter_context(nc.sbuf_tensor("mixer_" + name, shape, dt))

        ident, ones, headones = c["ident"], c["ones"], c["headones"]
        feats = [sb(f"feats{u}", [P, F_TILES, P]) for u in range(2)]
        LT, TI, TT, XX, MT, RBT, RKT = [sb(n, [P, 2, 512]) for n in ("LT", "TI", "TT", "XX", "MT", "RBT", "RKT")]
        LTm = sb("LTm", [P, 2, 2, 512])
        ATT, tB, tK, tV, tGV, Gn, SA = [sb(n, [P, 512]) for n in ("ATT", "tB", "tK", "tV", "tGV", "Gn", "SA")]
        tKI = sb("tKI", [P, 256])
        S, Ss = sb("S", [P, NJ, 64]), sb("Ss", [P, NJ, P])
        G, Gs = sb("G", [P, 2, P]), sb("Gs", [P, 4, P])
        Ys, yrs, Os, ors = [sb(n, [P, NJ, P]) for n in ("Ys", "yrs", "Os", "ors")]
        yT = sb("yT", [P, KT, P])
        w_out = sb("w_out", [P, KT, D])
        wr = sb("wr", [P, KT, NG + NE])
        rbias = sb("rbias", [P, NG + NE])
        rows = sb("rows", [P, 2, 3, D])
        x, x1, h2 = [sb(n, [P, D]) for n in ("x", "x1", "h2")]
        h2T = sb("h2T", [P, KT, P])
        eps = sb("eps", [P, 2])
        state_in, gin = sb("state_in", [64, 512]), sb("gin", [P, 2, P])
        wkv, gkeep = sb("wkv", [64, 2, 512]), sb("gkeep", [P, 2, 2, P])
        st = sb("st", [P, 4])

        x_all = [a["x_prompt"].rearrange("a t d -> (a t) d"), a["x_sample"].rearrange("a t d -> (a t) d")]
        feat = d["feat"].rearrange("(f p) t -> p f t", p=P)
        GATE, SCALE, SHIFT = 0, 1, 2
        block = ctx.enter_context(nc.Block())

        def w(eng, name, value):
            need(eng, sg(name), value)

        COUNT = {"X_done": (6, 0), "X_read": (6, 0), "C_made": (5, 0), "T_made": (6, 1), "TT_made": (7, 1),
                 "Y_done": (5, 0), "YT_done": (6, 0)}

        def level_of(what, g):
            kind, event = what.split("_")
            return sg(f"{kind}lv{g}_{event}")

        def wl(eng, what, k, g, n):
            per, off = COUNT[what]
            value = per * n + (k + off)
            if not isinstance(value, int) or value > 0:
                eng.wait_ge(level_of(what, g), value)

        def lv(what, k, g, n):
            per, off = COUNT[what]
            return level_of(what, g), per * n + (k + off)

        def wl_before(eng, what, g, n):
            per, off = COUNT[what]
            if not isinstance(n, int) or n > 0:
                eng.wait_ge(level_of(what, g), per * n)

        def four(buf, g, m):
            return buf[0:m, g, :].rearrange("p (a b) -> p a b", a=4)[:, :, 0:m]

        def four_b(bank, m):
            return bank[0:m, :].rearrange("p (a b) -> p a b", a=4)[:, :, 0:m]

        def mask(name, m):
            return over4(c[name][0:m, 0:m])

        def level(k, m):
            return c["level"][0:m, k:k + 1, 0:m].to_broadcast([m, 4, m])

        def head(h):
            return h // 2, slice(64 * (h % 2), 64 * (h % 2) + 64)

        def last(m):
            return 6 if m == P else 5

        def steps(eng, front, after_first=None):
            front(0, 0, P, 0, 1)
            if after_first:
                after_first()
            with eng.Fori(0, 3) as k:
                for u in (1, 0):
                    n = 2 * k + (2 - u)
                    front(n, u, P, eng.to_reg(n + 0), eng.to_reg(n + 1))
            front(7, 1, P, 7, 8)

        @block.sync
        def _(sp):
            def store(n, m):
                w(sp, "x1_made", 2 * (n + 1))
                sp.dma_start(d["x1"][bass.ds(n * P, m), :], x1[0:m, :]).then_inc(sg("x1_stored"), 16)
                w(sp, "h2_made", n + 1)
                sp.dma_start(d["h2"][bass.ds(n * P, m), :], h2[0:m, :]).then_inc(sg("h2_stored"), 16)

            def front(n, u, m, n0, n1, x_src=x_all[0]):
                before = reg(sp, n - 1)
                for name in ("O_done", "Y_done", "yg_made", "yr_made"):
                    w(sp, name, before)
                cols = bass.ds(n * P, m)
                for lo, hi in ((0, 16), (16, 28), (28, 40)):
                    sp.dma_start(feats[u][:, lo:hi, 0:m], feat[:, lo:hi, cols]).then_inc(sg(f"feats{u}_loaded"), 16)
                w(sp, "x1_made", 2 * n)
                sp.dma_start(x[0:m, :], x_src[bass.ds(0 if m < P else n * P, m), :]).then_inc(sg("x_loaded"), 16)
                if not (isinstance(n, int) and n == 0):
                    store(n - 1, P)

            def constants():
                sp.dma_start(w_out[:, :, :], a["w_out"].rearrange("l (k p) n -> p (l k) n", p=P)).then_inc(sg("w_out_loaded"), 16)
                for r in range(2):
                    for i, at in ((GATE, 2), (SCALE, 4), (SHIFT, 3)):
                        sp.dma_start(rows[:, r, i, :], d["mod"][r:r + 1, at * D:(at + 1) * D].to_broadcast([P, D])).then_inc(sg("rows_loaded"), 16)
                sp.dma_start(h2[:, :], a["norm2_g"].to_broadcast([P, D])).then_inc(sg("rows_loaded"), 16)
                sp.dma_start(wr[:, :, 0:NG], a["w_router_group"].rearrange("l (k p) n -> p (l k) n", p=P)).then_inc(sg("router_loaded"), 16)
                sp.dma_start(wr[:, :, NG:], a["w_router_expert"].rearrange("l (k p) n -> p (l k) n", p=P)).then_inc(sg("router_loaded"), 16)
                sp.dma_start(rbias[:, 0:NG], a["b_router_group"].to_broadcast([P, NG])).then_inc(sg("router_loaded"), 16)
                sp.dma_start(rbias[:, NG:], a["b_router_expert"].to_broadcast([P, NE])).then_inc(sg("router_loaded"), 16)

                sp.dma_start(state_in[0:64, :].rearrange("v (h k) -> v h k", h=8), a["state_rwkv_wkv"].rearrange("l b h v k -> v (l b h) k")).then_inc(sg("state_loaded"), 16)
                gla_in = a["state_gla_kv"].rearrange("l b (p q) k v -> q k (l b p) v", q=2)
                for q in range(2):
                    sp.dma_start(gin[64 * q:64 * q + 64, :, :], gla_in[q]).then_inc(sg("state_loaded"), 16)

            front(0, 0, P, 0, 1)
            constants()
            front(1, 1, P, 1, 2)
            with sp.Fori(1, 4) as k:
                for u in range(2):
                    front(2 * k + u, u, P, None, None)
            front(8, 0, DEC, 8, 9, x_all[1])
            store(8, DEC)
            for i, (wkv_out, gla_out) in enumerate(((o[3], o[4]), (o[6], o[7]))):
                sp.wait_ge(sg("wkv_turned"), i + 1)
                sp.dma_start(wkv_out.rearrange("l b h v k -> v (l b h) k"), wkv[0:64, i, :].rearrange("v (h k) -> v h k", h=8)).then_inc(sg("states_out"), 16)
                sp.wait_ge(sg("G_kept"), i + 1)
                g_out = gla_out.rearrange("l b (p q) k v -> q k (l b p) v", q=2)
                for q in range(2):
                    sp.dma_start(g_out[q], gkeep[64 * q:64 * q + 64, i, :, :]).then_inc(sg("states_out"), 16)
            sp.wait_ge(sg("states_out"), 96)
            sp.wait_ge(sg("x1_stored"), 145)
            sp.wait_ge(sg("h2_stored"), 145)

        @block.tensor
        def _(pe):
            def turn(bank, src, m, n1, name):
                for j in range(src.shape[1]):
                    mm = pe.transpose(bank[0:m, j * P:(j + 1) * P], src[:, j, 0:m], ident[:, :])
                mm.then_inc(sg(name), 1)

            def scores(bank, lhs, rhs, g, m, name):
                for i in range(4):
                    j, q = head(2 * i + g)
                    mm = pe.matmul(bank[0:m, i * P:i * P + m], lhs[q, j, 0:m], rhs[q, j, 0:m], start=True, stop=True)
                mm.then_inc(sg(name), 1)

            def product(bank, lhs, rhs, m, done):
                for i in range(4):
                    mm = pe.matmul(bank[0:m, i * P:i * P + m], lhs[0:m, i * P:i * P + m], rhs[0:m, i * P:i * P + m], start=True, stop=True)
                mm.then_inc(done, 1)

            FIRST, SECOND = slice(0, 64), slice(64, P)

            def quarter(bank, rows_out, cols_out, lhs, rows_in, lhs_cols, rhs, rhs_cols, done):
                for i in range(4):
                    at = lambda v: slice(i * P + v.start, i * P + v.stop)
                    mm = pe.matmul(bank[rows_out, at(cols_out)], lhs[rows_in, at(lhs_cols)], rhs[rows_in, at(rhs_cols)], start=True, stop=True)
                mm.then_inc(done, 1)

            def ready(*waits):
                waits = [(s_, reg(pe, value)) for s_, value in waits]
                pe.wait_ge(sg("eps_made"), 2)
                for s_, value in waits:
                    pe.wait_ge(s_, value)

            def back(n0, m):
                def mu():
                    w(pe, "SA_read", n0)
                    w(pe, "Y_read", n0)
                    pe.matmul(psum[7][:, :], headones[:, :], Ys[:, :, :].rearrange("p a b -> p (a b)"), start=True, stop=True).then_inc(sg("mu_done"), 1)

                def gvar():
                    w(pe, "O_squared", n0)
                    w(pe, "mu_read", n0)
                    pe.matmul(psum[7][:, :], ones[:, :], ors[:, :, :].rearrange("p a b -> p (a b)"), start=True, stop=True).then_inc(sg("gvar_done"), 1)

                def var():
                    w(pe, "yc_squared", n0)
                    w(pe, "gvar_read", n0)
                    pe.matmul(psum[7][:, :], headones[:, :], yrs[:, :, :].rearrange("p a b -> p (a b)"), start=True, stop=True).then_inc(sg("var_done"), 1)

                def wo(half):
                    def run():
                        w(pe, ("RBT0_read", "RBT1_read")[half], back.n1)
                        w(pe, ("G_read", "var_read")[half], n0)
                        w(pe, "yr_made", n0)
                        w(pe, "yg_made", n0)
                        pe.wait_ge(sg("w_out_loaded"), 16)
                        for q in range(KT):
                            mm = pe.matmul(psum[6 + half][0:m, :], yT[:, q, 0:m], w_out[:, q, 512 * half:512 * half + 512],
                                           start=q == 0, stop=q == KT - 1)
                        mm.then_inc(sg(f"wo{half}_done"), 1)
                    return run

                def ht(half):
                    def run():
                        w(pe, ("TGV_read", "TKI_read")[half], back.n1)
                        w(pe, "h2_made", n0)
                        b_ = psum[7 - half]
                        for q in range(4):
                            mm = pe.transpose(b_[:, q * P:q * P + m], h2[0:m, (4 * half + q) * P:(4 * half + q + 1) * P], ident[0:m, 0:m])
                        mm.then_inc(sg(f"ht{half}_done"), 1)
                    return run

                def rt():
                    w(pe, "ht0_read", n0)
                    w(pe, "ht1_read", n0)
                    pe.wait_ge(sg("router_loaded"), 64)
                    for q in range(KT):
                        mm = pe.matmul(psum[7][0:m, 0:NG + NE], h2T[:, q, 0:m], wr[:, q, :], start=q == 0, stop=q == KT - 1)
                    mm.then_inc(sg("rt_done"), 1)

                return {"mu": mu, "gvar": gvar, "var": var, "wo0": wo(0), "wo1": wo(1), "ht0": ht(0), "ht1": ht(1), "rt": rt}

            def front(n, u, m, n0, n1):
                F = feats[u]
                fA, fB, fK, fR, fV = [F[:, f:f + NJ, :] for f in (F_A, F_B, F_K, F_R, F_V)]
                fQD, fKI, fGV = F[:, F_QD:F_QD + 2, :], F[:, F_KI:F_KI + 2, :], F[:, F_GV:F_GV + 4, :]
                back.n1 = n1
                bk = back(n0, P) if not (isinstance(n, int) and n == 0) else {}
                w(pe, f"feats{u}_loaded", 24 * (n + 2 - u))
                w(pe, "S_made", n0)
                scores(psum[0], fB, fA, 0, m, "LT0_done")
                w(pe, "Y_read", n0)
                scores(psum[1], fB, fA, 1, m, "LT1_done")
                w(pe, "G_made", n0)
                scores(psum[2], fA, fB, 0, m, "L0_done")
                w(pe, "O_squared", n0)
                scores(psum[3], fA, fB, 1, m, "L1_done")

                def filler(name):
                    if name in bk:
                        bk[name]()
                    elif name == "TB":
                        w(pe, "G_read", n0)
                        turn(psum[6], fB, m, n1, "TB_done")
                    elif name == "TV":
                        w(pe, "TB_read", n1)
                        turn(psum[6], fV, m, n1, "TV_done")
                    elif name == "TK":
                        w(pe, "TV_read", n1)
                        turn(psum[6], fK, m, n1, "TK_done")
                    elif name == "MT0":
                        w(pe, "TK_read", n1)
                        scores(psum[6], fK, fA, 0, m, "MT0_done")
                    elif name == "MT1":
                        w(pe, "var_read", n0)
                        scores(psum[7], fK, fA, 1, m, "MT1_done")
                    elif name == "RBT0":
                        w(pe, "MT0_read", n1)
                        scores(psum[6], fB, fR, 0, m, "RBT0_done")
                    elif name == "RBT1":
                        w(pe, "MT1_read", n1)
                        scores(psum[7], fB, fR, 1, m, "RBT1_done")
                    elif name == "RKT0":
                        w(pe, "RBT0_read", n1)
                        w(pe, "x1_made", 2 * n)
                        scores(psum[6], fK, fR, 0, m, "RKT0_done")
                    elif name == "RKT1":
                        w(pe, "RBT1_read", n1)
                        scores(psum[7], fK, fR, 1, m, "RKT1_done")
                    elif name == "ATT":
                        w(pe, "RKT0_read", n1)
                        for hh in (0, 2, 1, 3):
                            j, q = head(hh)
                            if hh == 1:
                                w(pe, "ATT_half", n1)
                            mm = pe.matmul(psum[6][0:m, hh * P:hh * P + m], fKI[q, j, 0:m], fQD[q, j, 0:m], start=True, stop=True)
                            if hh == 2:
                                mm.then_inc(sg("ATT_half"), 1)
                        mm.then_inc(sg("ATT_done"), 1)
                    elif name == "TGV":
                        w(pe, "RKT1_read", n1)
                        turn(psum[7], fGV, m, n1, "TGV_done")
                    elif name == "TKI":
                        w(pe, "ATT_read", n1)
                        turn(psum[6], fKI, m, n1, "TKI_done")

                filler("TB")
                if "mu" in bk:
                    bk["mu"]()
                fill = [["TV"], ["TK", "gvar"], ["MT0"], ["var"], ["MT1", "RBT0"], ["RBT1", "wo0"],
                        ["wo1"], ["RKT0", "RKT1"], ["ATT", "TGV"], ["TKI"], ["ht0"], ["ht1"]]
                for k in range(1, 7):
                    if m == DEC and k == 6:
                        for names in fill[2 * k - 2:]:
                            for name in names:
                                filler(name)
                        continue
                    for g in range(2):
                        if k < 6:
                            wl(pe, "T_made", k - 1, g, n)
                            wl(pe, "C_made", k, g, n)
                            product(psum[g], LTm[:, k % 2, g, :], TI[:, g, :], m, level_of("X_done", g))
                        else:
                            ready(lv("T_made", 5, g, n))
                            quarter(psum[g], SECOND, FIRST, LT[:, g, :], FIRST, SECOND, TI[:, g, :], FIRST, level_of("X_done", g))
                    for name in fill[2 * k - 2]:
                        filler(name)
                    for g in range(2):
                        if k == 6:
                            ready(lv("X_read", 6, g, n), lv("TT_made", 5, g, n))
                            quarter(psum[3 + 2 * g], FIRST, SECOND, XX[:, g, :], SECOND, FIRST, TT[:, g, :], SECOND, level_of("YT_done", g))
                            continue
                        wl(pe, "X_read", k, g, n)
                        wl(pe, "TT_made", k - 1, g, n)
                        if k < last(m):
                            product(psum[2 + 2 * g], TT[:, g, :], XX[:, g, :], m, level_of("Y_done", g))
                        if k == 1 and g == 0:
                            wl(pe, "T_made", 0, 1, n)
                        product(psum[3 + 2 * g], XX[:, g, :], TT[:, g, :], m, level_of("YT_done", g))
                    for name in fill[2 * k - 1]:
                        filler(name)
                w(pe, "TGV_read", n1)
                w(pe, "TKI_read", n1)
                wl(pe, "T_made", last(m) - 1, 0, n)
                for hh in range(4):
                    j, q = head(hh)
                    mm = pe.matmul(psum[2][q, j * P:(j + 1) * P], tKI[0:m, hh * 64:hh * 64 + 64], tGV[0:m, hh * P:(hh + 1) * P], start=True, stop=True)
                mm.then_inc(sg("U_done"), 1)
                w(pe, "Ss_made", 2 * n + 2)
                w(pe, "MT0_read", n1)
                w(pe, "MT1_read", n1)
                w(pe, "TV_read", n1)
                w(pe, "ht1_read", n0)
                for h in range(8):
                    j, q = head(h)
                    g, i = h % 2, h // 2
                    if h % 2 == 0:
                        pe.matmul(psum[6][0:m, P * j:P * j + P], fA[:, j, 0:m], Ss[:, j, :], start=True, stop=False)
                    mm = pe.matmul(psum[6][0:m, 64 * h:64 * h + 64], MT[0:m, g, i * P:i * P + m], tV[0:m, 64 * h:64 * h + 64], start=False, stop=g == 1)
                mm.then_inc(sg("G_done"), 1)
                if "rt" in bk:
                    bk["rt"]()
                def gla_rows(heads):
                    for hh in heads:
                        j, q = head(hh)
                        pe.matmul(psum[3][:, hh * P:hh * P + m], Gs[:, hh, :], fQD[:, j, 0:m], start=True, stop=False)
                        mm = pe.matmul(psum[3][:, hh * P:hh * P + m], tGV[0:m, hh * P:(hh + 1) * P], ATT[0:m, hh * P:hh * P + m], start=False, stop=True)
                    return mm

                w(pe, "ATT_read", n1)
                w(pe, "Gs_made", 2 * n + 2)
                wl(pe, "TT_made", last(m), 0, n)
                gla_rows((0, 1))
                w(pe, "G_read", n1)
                wl(pe, "TT_made", last(m), 1, n)
                w(pe, "rt_read", n0)
                for h in range(8):
                    g, i = h % 2, h // 2
                    mm = pe.matmul(psum[7][0:m, 64 * h:64 * h + 64], TT[0:m, g, i * P:i * P + m], Gn[0:m, 64 * h:64 * h + 64], start=True, stop=True)
                mm.then_inc(sg("SA_done"), 1)
                gla_rows((2, 3)).then_inc(sg("O_done"), 1)
                w(pe, "TB_read", n1)
                w(pe, "TK_read", n1)
                w(pe, "SA_read", n1)
                for h in range(8):
                    j, q = head(h)
                    pe.matmul(psum[0][q, 64 * j:64 * j + 64], tB[0:m, 64 * h:64 * h + 64], SA[0:m, 64 * h:64 * h + 64], start=True, stop=False)
                    mm = pe.matmul(psum[0][q, 64 * j:64 * j + 64], tK[0:m, 64 * h:64 * h + 64], tV[0:m, 64 * h:64 * h + 64], start=False, stop=True)
                mm.then_inc(sg("SU_done"), 1)
                for g in range(2):
                    w(pe, f"RBT{g}_read", n1)
                w(pe, "RKT0_read", n1)
                w(pe, "RKT1_read", n1)
                for h in range(8):
                    j, q = head(h)
                    g, i = h % 2, h // 2
                    y = psum[1][q, P * j:P * j + m]
                    if h % 2 == 0:
                        pe.matmul(psum[1][:, P * j:P * j + m], Ss[:, j, :], fR[:, j, 0:m], start=True, stop=False)
                    pe.matmul(y, SA[0:m, 64 * h:64 * h + 64], RBT[0:m, g, i * P:i * P + m], start=False, stop=False)
                    mm = pe.matmul(y, tV[0:m, 64 * h:64 * h + 64], RKT[0:m, g, i * P:i * P + m], start=False, stop=True)
                mm.then_inc(sg("Y_done"), 1)

            def turn_state(i):
                pe.wait_ge(sg("S_made"), 8 + i)
                if i == 0:
                    wl(pe, "T_made", 5, 1, 7)
                for j in range(NJ):
                    mm = pe.transpose(psum[4][0:64, j * P:(j + 1) * P], S[:, j, :], ident[:, :])
                mm.then_inc(sg("S_turned"), 1)

            steps(pe, front)
            turn_state(0)
            pe.wait_ge(sg("state_loaded"), 48)
            wl(pe, "TT_made", 6, 1, 7)
            for j in range(NJ):
                mm = pe.transpose(psum[5][:, j * 64:(j + 1) * 64], state_in[0:64, j * P:(j + 1) * P], ident[0:64, 0:64])
            mm.then_inc(sg("state_turned"), 1)
            pe.wait_ge(sg("wkv_turned"), 1)
            pe.wait_ge(sg("state_taken"), 2)
            front(8, 0, DEC, 8, 9)
            turn_state(1)
            back.n1 = 9
            bk = back(9, DEC)
            for name in ("mu", "gvar", "var", "wo0", "wo1", "ht0", "ht1", "rt"):
                bk[name]()

        @block.gpsimd
        def _(pool):
            nc.gpsimd.memset(eps[:, 0:1], LNX_EPS).then_inc(sg("eps_made"), 1)
            nc.gpsimd.memset(eps[:, 1:2], RMS_EPS).then_inc(sg("eps_made"), 1)
            nc.gpsimd.memset(S[:, :, :], 0.0).then_inc(sg("zero_states"), 1)
            nc.gpsimd.memset(G[:, :, :], 0.0).then_inc(sg("zero_states"), 1)
            nc.gpsimd.memset(Ss[:, :, :], 0.0).then_inc(sg("zero_states"), 1)
            nc.gpsimd.memset(Gs[:, :, :], 0.0).then_inc(sg("zero_states"), 1)

            def front(n, u, m, n0, n1):
                for k in range(1, 6):
                    for g in range(2):
                        w(pool, f"LT{g}_read", n1)
                        wl(pool, "X_done", k - 2, g, n)
                        nc.gpsimd.tensor_tensor(four(LTm[:, k % 2], g, m), four(LT, g, m), level(k, m), ALU.mult).then_inc(level_of("C_made", g), 1)

            steps(pool, front)
            front(8, 0, DEC, 8, 9)

        @block.scalar
        def _(act):
            nc.scalar.preload_act_table_set("natural_log_exp_and_others")
            act.wait_ge(sg("eps_made"), 2)

            def flat(t):
                return t[:, :, :].rearrange("p a b -> p (a b)")

            def rsqrt(out, src, scale, e, m, ready, name, count):
                nc.scalar.activation(out, src, ACT.Ln, scale=scale, bias=eps[0:m, e:e + 1]).then_inc(sg(ready), 1)
                w(act, ready, count)
                nc.scalar.activation(out, out, ACT.Exp, scale=-0.5).then_inc(sg(name), 1)

            def back(n0, m):
                def yc():
                    w(act, "mu_read", n0)
                    nc.scalar.activation(flat(yrs), flat(Ys), ACT.Square).then_inc(sg("yc_squared"), 1)

                def gvar():
                    w(act, "gvar_done", n0)
                    rsqrt(flat(ors), psum[7][:, :], 1.0 / P, 1, P, "gvar_read", "gr_made", n0)

                def var():
                    w(act, "var_done", n0)
                    rsqrt(flat(yrs), psum[7][:, :], 1.0 / 64, 0, P, "var_read", "yrs_made", n0)

                def norm():
                    w(act, "x1_made", 2 * n0 if isinstance(n0, int) else back.n2)
                    nc.scalar.activation(h2T[0:m, :, :].rearrange("p a b -> p (a b)"), x1[0:m, :], ACT.Square, accum_out=st[0:m, 0:1]).then_inc(sg("x1_squared"), 1)
                    w(act, "x1_squared", n0)
                    rsqrt(st[0:m, 1:2], st[0:m, 0:1], 1.0 / D, 1, m, "x1_log", "x1_rstd", n0)

                def ht(half):
                    w(act, f"ht{half}_done", n0)
                    nc.scalar.copy(h2T[:, 4 * half:4 * half + 4, 0:m], psum[7 - half][:, :].rearrange("p (a b) -> p a b", a=4)[:, :, 0:m]).then_inc(sg(f"ht{half}_read"), 1)

                return yc, gvar, var, norm, ht

            def front(n, u, m, n0, n1):
                first = isinstance(n, int) and n == 0
                back.n2 = reg(act, 2 * n)
                yc, gvar, var, norm, ht = back(n0, P)

                def take(bank, dst, name, free=None, scale=1.0):
                    if free:
                        w(act, free, n0)
                    w(act, name + "_done", n1)
                    nc.scalar.activation(dst, bank, ACT.Copy, scale=scale).then_inc(sg(name + "_read"), 1)

                def xk(k):
                    for g in range(2):
                        wl(act, "X_done", k, g, n)
                        if k > 1:
                            wl(act, "YT_done", k - 1, g, n)
                        else:
                            wl_before(act, "YT_done", g, n)
                        part = (slice(0, m), slice(None), slice(0, m)) if k < 6 else (slice(64, P), slice(None), slice(0, 64))
                        nc.scalar.copy(four(XX, g, m)[part], four_b(psum[g], m)[part]).then_inc(level_of("X_read", g), 1)

                take(psum[6][0:m, :], tB[0:m, :], "TB", "SU_done")
                xk(1)
                take(psum[6][0:m, :], tV[0:m, :], "TV", "Y_done")
                first or yc()
                take(psum[6][0:m, :], tK[0:m, :], "TK", "SU_done")
                first or gvar()
                xk(2)
                first or var()
                xk(3)
                xk(4)
                first or norm()
                xk(5)
                take(psum[7][0:m, :], tGV[0:m, :], "TGV", "O_done")
                take(psum[6][0:m, 0:256], tKI[0:m, :], "TKI", "U_done")
                if m == P:
                    xk(6)
                first or ht(0)
                first or ht(1)
                w(act, "SA_done", n0)
                take(psum[6][0:m, :], Gn[0:m, :], "G", None, -1.0)
                take(psum[7][0:m, :], SA[0:m, :], "SA", "Y_done")
                w(act, "SU_done", n0)
                w(act, "yg_made", n0)
                take(psum[3][:, :].rearrange("p (a b) -> p a b", a=4)[:, :, 0:m], Os[:, :, 0:m], "O")
                w(act, "O_read", n1)
                nc.scalar.activation(ors[:, :, 0:m], Os[:, :, 0:m], ACT.Square).then_inc(sg("O_squared"), 1)
                w(act, "yr_made", n0)
                take(psum[1][:, :].rearrange("p (a b) -> p a b", a=4)[:, :, 0:m], Ys[:, :, 0:m], "Y")

            def turned(i):
                act.wait_ge(sg("S_turned"), i + 1)
                nc.scalar.copy(wkv[:, i, :], psum[4][0:64, :]).then_inc(sg("wkv_turned"), 1)

            steps(act, front)
            turned(0)
            front(8, 0, DEC, 8, 9)
            turned(1)
            yc, gvar, var, norm, ht = back(9, DEC)
            for stage in (yc, gvar, var, norm):
                stage()
            ht(0)
            ht(1)

        @block.vector
        def _(dve):
            dve.sem_inc(sg("x1_stored"), 1)
            dve.sem_inc(sg("h2_stored"), 1)
            dve.wait_ge(sg("zero_states"), 4)

            def constants():
                dve.wait_ge(sg("rows_loaded"), 112)
                for r in range(2):
                    nc.vector.scalar_tensor_tensor(rows[:, r, SCALE, :], rows[:, r, SCALE, :], 1.0, h2[:, :], ALU.add, ALU.mult).then_inc(sg("rows_made"), 1)
                dve.wait_ge(sg("rows_made"), 2)
                dve.wait_ge(sg("router_loaded"), 64)


            def masked(name, bank, dst, g, mk, m, n0, n1, free):
                w(dve, name + "_done", n1)
                if free:
                    w(dve, free, n0)
                nc.vector.tensor_tensor(four(dst, g, m), four_b(bank, m), mask(mk, m), ALU.mult).then_inc(sg(name + "_read"), 1)

            def back(n, u, m, r, n0):
                F = feats[1 - u]

                def mu():
                    w(dve, "mu_done", n0)
                    nc.vector.scalar_tensor_tensor(Ys[:, :, :], psum[7][:, :].rearrange("p (a b) -> p a b", a=4), -1.0 / 64, Ys[:, :, :], ALU.mult, ALU.add).then_inc(sg("mu_read"), 1)

                def yg():
                    w(dve, "gr_made", n0)
                    nc.vector.tensor_tensor(Os[:, :, :], Os[:, :, :], ors[:, :, :], ALU.mult).then_inc(sg("yg_normed"), 1)
                    w(dve, "yg_normed", n0)
                    nc.vector.tensor_tensor(yT[:, 4:8, :], Os[:, :, :], F[:, F_SG:F_SG + 4, :], ALU.mult).then_inc(sg("yg_made"), 1)

                def yr():
                    w(dve, "yrs_made", n0)
                    nc.vector.tensor_tensor(Ys[:, :, :], Ys[:, :, :], yrs[:, :, :], ALU.mult).then_inc(sg("yr_normed"), 1)
                    w(dve, "yr_normed", n0)
                    nc.vector.tensor_tensor(Ys[:, :, :], Ys[:, :, :], F[:, F_WG:F_WG + 4, :], ALU.mult).then_inc(sg("yr_gated"), 1)
                    w(dve, "yr_gated", n0)
                    nc.vector.tensor_tensor(yT[:, 0:4, :], Ys[:, :, :], F[:, F_BG:F_BG + 4, :], ALU.add).then_inc(sg("yr_made"), 1)

                def add(half):
                    cols = slice(512 * half, 512 * half + 512)
                    w(dve, f"wo{half}_done", n0)
                    w(dve, "x1_stored", 16 * (n - 1) + 1)
                    nc.vector.tensor_tensor(x1[0:m, cols], psum[6 + half][0:m, :], rows[0:m, r, GATE, cols], ALU.mult).then_inc(sg(f"gated{half}"), 1)
                    w(dve, f"gated{half}", n0)
                    w(dve, "x_loaded", 16 * n)
                    nc.vector.tensor_tensor(x1[0:m, cols], x1[0:m, cols], x[0:m, cols], ALU.add).then_inc(sg("x1_made"), 1)

                def norm():
                    w(dve, "x1_rstd", n0)
                    w(dve, "h2_stored", 16 * (n - 1) + 1)
                    nc.vector.scalar_tensor_tensor(h2[0:m, :], x1[0:m, :], st[0:m, 1:2], rows[0:m, r, SCALE, :], ALU.mult, ALU.mult).then_inc(sg("h2_scaled"), 1)
                    w(dve, "h2_scaled", n0)
                    nc.vector.tensor_tensor(h2[0:m, :], h2[0:m, :], rows[0:m, r, SHIFT, :], ALU.add).then_inc(sg("h2_made"), 1)

                def rt():
                    w(dve, "rt_done", n0)
                    nc.vector.tensor_tensor(c["logits"][0:m, bass.ds(n - 1, 1), :].rearrange("p a b -> p (a b)"), psum[7][0:m, 0:NG + NE], rbias[0:m, :], ALU.add).then_inc(sg("rt_read"), 1)

                return mu, yg, yr, add, norm, rt

            def front(n, u, m, n0, n1):
                first = isinstance(n, int) and n == 0
                mu, yg, yr, add, norm, rt = back(n, u, P, 0, n0)
                at = bass.ds(n, 1)
                for g in range(2):
                    wl_before(dve, "C_made", g, n)
                    wl_before(dve, "X_done", g, n)
                    masked(f"LT{g}", psum[g], LT, g, "after", m, n0, n1, None)
                for g in range(2):
                    w(dve, f"L{g}_done", n1)
                    wl_before(dve, "X_done", g, n)
                    nc.vector.tensor_tensor(four(TI, g, m), four_b(psum[2 + g], m), mask("below", m), ALU.mult).then_inc(sg(f"L{g}_masked"), 1)
                    w(dve, f"L{g}_masked", n1)
                    nc.vector.tensor_tensor(four(TI, g, m), mask("ident", m), four(TI, g, m), ALU.subtract).then_inc(level_of("T_made", g), 1)
                for g in range(2):
                    w(dve, f"LT{g}_read", n1)
                    w(dve, "SA_done", n0)
                    nc.vector.tensor_tensor(four(TT, g, m), four(LT, g, m), level(0, m), ALU.mult).then_inc(sg(f"LT{g}_masked"), 1)
                    w(dve, f"LT{g}_masked", n1)
                    nc.vector.tensor_tensor(four(TT, g, m), mask("ident", m), four(TT, g, m), ALU.subtract).then_inc(level_of("TT_made", g), 1)
                w(dve, "Y_done", n0)
                w(dve, "S_made", n0)
                for v in range(2):
                    q = slice(64 * v, 64 * v + 64)
                    nc.vector.tensor_tensor(Ss[q, :, q], S[q, :, :], c["decay_mid"][q, :, at].to_broadcast([64, NJ, 64]), ALU.mult).then_inc(sg("Ss_made"), 1)
                w(dve, "O_done", n0)
                w(dve, "G_made", n0)
                for v in range(2):
                    q = slice(64 * v, 64 * v + 64)
                    nc.vector.tensor_tensor(Gs[q, v::2, :], G[q, :, :], c["gla_mid"][q, :, at].to_broadcast([64, 2, P]), ALU.mult).then_inc(sg("Gs_made"), 1)
                first or mu()

                def update(k):
                    for g in range(2):
                        if k < last(m):
                            wl(dve, "Y_done", k, g, n)
                            wl(dve, "T_made", k - 1, g, n)
                            nc.vector.tensor_tensor(four(TI, g, m), four(TI, g, m), four_b(psum[2 + 2 * g], m), ALU.subtract).then_inc(level_of("T_made", g), 1)
                        wl(dve, "YT_done", k, g, n)
                        wl(dve, "TT_made", k - 1, g, n)
                        part = (slice(0, m), slice(None), slice(0, m)) if k < 6 else (slice(0, 64), slice(None), slice(64, P))
                        nc.vector.tensor_tensor(four(TT, g, m)[part], four(TT, g, m)[part], four_b(psum[3 + 2 * g], m)[part], ALU.subtract).then_inc(level_of("TT_made", g), 1)

                update(1)
                first or yg()
                update(2)
                masked("MT0", psum[6], MT, 0, "after", m, n0, n1, "G_done")
                masked("MT1", psum[7], MT, 1, "after", m, n0, n1, "G_done")
                first or yr()
                masked("RBT0", psum[6], RBT, 0, "upto", m, n0, n1, "Y_done")
                masked("RBT1", psum[7], RBT, 1, "upto", m, n0, n1, "Y_done")
                update(3)
                first or add(0)
                first or add(1)
                update(4)
                masked("RKT0", psum[6], RKT, 0, "upto", m, n0, n1, "Y_done")
                masked("RKT1", psum[7], RKT, 1, "upto", m, n0, n1, "Y_done")
                w(dve, "ATT_done", n1)
                w(dve, "O_done", n0)
                nc.vector.tensor_tensor(ATT[0:m, :].rearrange("p (a b) -> p a b", a=4)[:, :, 0:m], four_b(psum[6], m), mask("upto", m), ALU.mult).then_inc(sg("ATT_read"), 1)
                first or norm()
                update(5)
                if m == P:
                    update(6)
                first or rt()
                w(dve, "U_done", n1)
                for v in range(2):
                    q = slice(64 * v, 64 * v + 64)
                    nc.vector.tensor_tensor(G[q, :, :], Gs[q, v::2, :], psum[2][q, 0:256].rearrange("p (a b) -> p a b", a=2), ALU.add).then_inc(sg("G_added"), 1)
                w(dve, "G_added", 2 * n + 2)
                nc.vector.tensor_tensor(G[:, :, :], G[:, :, :], c["gla_end"][:, :, at].to_broadcast([P, 2, P]), ALU.mult).then_inc(sg("G_made"), 1)
                w(dve, "SU_done", n1)
                for v in range(2):
                    q = slice(64 * v, 64 * v + 64)
                    nc.vector.tensor_tensor(S[q, :, :], Ss[q, :, q], psum[0][q, 0:256].rearrange("p (a b) -> p a b", a=4), ALU.add).then_inc(sg("S_added"), 1)
                w(dve, "S_added", 2 * n + 2)
                nc.vector.tensor_tensor(S[:, :, :], S[:, :, :], c["decay_end"][:, :, at].to_broadcast([P, NJ, 64]), ALU.mult).then_inc(sg("S_made"), 1)

            def keep(i):
                dve.wait_ge(sg("G_made"), 8 + i)
                nc.vector.tensor_copy(gkeep[:, i, :, :], G[:, :, :]).then_inc(sg("G_kept"), 1)

            steps(dve, front, constants)
            keep(0)
            dve.wait_ge(sg("state_loaded"), 48)
            dve.wait_ge(sg("S_turned"), 1)
            dve.wait_ge(sg("state_turned"), 1)
            dve.wait_ge(sg("G_kept"), 1)
            nc.vector.tensor_copy(S[:, :, :], psum[5][:, 0:256].rearrange("p (a b) -> p a b", a=4)).then_inc(sg("state_taken"), 1)
            nc.vector.tensor_copy(G[:, :, :], gin[:, :, :]).then_inc(sg("state_taken"), 1)
            dve.wait_ge(sg("state_taken"), 2)
            front(8, 0, DEC, 8, 9)
            keep(1)
            mu, yg, yr, add, norm, rt = back(9, 1, DEC, 1, 9)
            for stage in (mu, yg, yr):
                stage()
            add(0)
            add(1)
            norm()
            rt()
            dve.wait_ge(sg("G_kept"), 2)
            dve.wait_ge(sg("rt_read"), 9)


def experts_block(nc, a, d, c, psum, final_rows):
    with nc.cleanup_on_exit(), ExitStack() as ctx:
        sems = {}

        def sg(name):
            if name not in sems:
                sems[name] = nc.alloc_semaphore(name="moe_" + name)
            return sems[name]

        def sb(name, shape, dt=F32):
            return ctx.enter_context(nc.sbuf_tensor("moe_" + name, shape, dt))

        ident, ones, after, logits = c["ident"], c["ones"], c["after"], c["logits"]
        E4 = [P, NT, 4]
        E16 = [P, NT, NG, EG]
        lg, ex, eq, group = [sb(n, E4) for n in ("lg", "ex", "eq", "group")]
        le, prob, prob2 = [sb(n, E4) for n in ("le", "prob", "prob2")]
        picked = [sb(f"picked{i}", E4) for i in range(2)]
        tmp16 = sb("tmp16", E16)
        chosen = [sb(f"chosen{i}", E16) for i in range(2)]
        either = sb("either", E16)
        gmax, first, pg, emax, v1, v2 = [sb(n, [P, NT]) for n in ("gmax", "first", "pg", "emax", "v1", "v2")]
        count_i = sb("count_i", [P, P], I32)
        count = sb("count", [P, P])
        token = sb("token", [P, NT], I32)
        rank, counts, carry, slot = [sb(n, [P, NT, NE]) for n in ("rank", "counts", "carry", "slot")]
        total, nblk, end, start = [sb(n, [P, NE]) for n in ("total", "nblk", "end", "start")]
        over = sb("over", [P, NE, NT])
        tri, prod = sb("tri", [P, NE, NE]), sb("prod", [P, NE, NE])
        ended = sb("ended", [P, NB, NE])
        be, slot_f = sb("be", [P, NB]), sb("slot_f", [P, NT, 2])
        blk_i, pos_i, pos_f = sb("blk_i", [P, NT, 2], I32), sb("pos_i", [P, NT, 2], I32), sb("pos_f", [P, NT, 2])
        blk_f = sb("blk_f", [P, NT, 2])
        used = sb("used", [1, 1], I32)
        value = sb("value", [P, NT, 2, 2])
        at_pos = sb("at_pos", [P, NT, 2, P])
        at_blk = sb("at_blk", [P, NT, 2, 2, NB])
        zero_row = sb("zero_row", [P, D])
        plan_token, plan_weight = sb("plan_token", [P, NB], I32), sb("plan_weight", [P, NB])

        wg, wu = [sb(n, [P, 2, KT, DE]) for n in ("wg", "wu")]
        wd = sb("wd", [P, 2, DE // P, D])
        idx = sb("idx", [P, 2], I32)
        xg = sb("xg", [P, 2, D])
        xT = sb("xT", [P, 2, KT, P])
        sil, hid = sb("sil", [P, DE]), sb("hid", [P, DE])
        yrow = sb("yrow", [P, 2, D])
        slots, block_expert = c["slots"], c["block_expert"]

        gate = a["w_expert_gate"].rearrange("l e (k p) n -> p (l e) k n", p=P)
        up = a["w_expert_up"].rearrange("l e (k p) n -> p (l e) k n", p=P)
        down = a["w_expert_down"].rearrange("l e (k p) n -> p (l e) k n", p=P)

        block = ctx.enter_context(nc.Block())

        def w(eng, name, value):
            need(eng, sg(name), value)

        def blocks(eng, step, passed=None):
            eng.wait_ge(sg("block_expert_made"), 2)
            last = eng.value_load(block_expert[0:1, NB:NB + 1], min_val=0, max_val=NB // 2 - 1)
            step(0, 0)
            step(1, 1)
            with eng.Fori(1, NB // 2) as k:
                with eng.If_lt(eng.to_reg(k + 0), eng.to_reg(last + 1)):
                    for u in range(2):
                        step(2 * k + u, u)
                if passed:
                    with eng.Else():
                        passed(k)
            return last

        @block.sync
        def _(sp):
            for r in range(2):
                for i, at in enumerate((5, 7, 6)):
                    sp.dma_start(final_rows[:, r, i, :], d["mod"][r:r + 1, at * D:(at + 1) * D].to_broadcast([P, D])).then_inc(sg("rows_loaded"), 16)
            sp.dma_start(yrow[:, 0, :], a["normf_g"].rearrange("(l n) -> l n", l=1).to_broadcast([P, D])).then_inc(sg("rows_loaded"), 16)

            def step(b, u):
                if isinstance(b, int) and b == 1:
                    sp.wait_ge(sg("x0_loaded"), 16)
                e = sp.value_load(block_expert[0:1, bass.ds(b, 1)], min_val=0, max_val=NE - 1)
                before = reg(sp, b - 1)
                w(sp, "gate_done", before)
                sp.dma_start(wg[:, u], gate[:, bass.ds(e, 1)].rearrange("p e k n -> p (e k) n")).then_inc(sg(f"gate{u}_loaded"), 16)
                w(sp, "up_done", before)
                sp.dma_start(wu[:, u], up[:, bass.ds(e, 1)].rearrange("p e k n -> p (e k) n")).then_inc(sg(f"up{u}_loaded"), 16)
                w(sp, "down1_done", before)
                sp.dma_start(wd[:, u], down[:, bass.ds(e, 1)].rearrange("p e k n -> p (e k) n")).then_inc(sg(f"down{u}_loaded"), 16)
                sp.sem_inc(sg("y_zeroed"), 16)

            def passed(k):
                for u in range(2):
                    sp.dma_start(d["y"][bass.ds((2 * k + u) * P, P), :], zero_row[:, :]).then_inc(sg("y_zeroed"), 16)

            sp.wait_ge(sg("zero_made"), 1)
            blocks(sp, step, passed)
            sp.wait_ge(sg("y_zeroed"), 16 * NB)

        @block.gpsimd
        def _(pool):
            nc.gpsimd.memset(zero_row[:, :], 0.0).then_inc(sg("zero_made"), 1)
            nc.gpsimd.memset(carry[:, 0, :], 0.0).then_inc(sg("carry_zeroed"), 1)
            nc.gpsimd.iota(count_i[:, :], [[1, P]], base=0, channel_multiplier=0).then_inc(sg("iotas_made"), 1)
            nc.gpsimd.iota(token[:, :], [[P, NT]], base=0, channel_multiplier=1).then_inc(sg("iotas_made"), 1)
            def step(b, u):
                before = reg(pool, b - 1)
                if isinstance(b, int) and b == 0:
                    pool.wait_ge(sg("plan_made"), 2)
                w(pool, "xT1_done", before)
                nc.gpsimd.tensor_copy(idx[:, u:u + 1], plan_token[:, bass.ds(b, 1)]).then_inc(sg("idx_made"), 1)
                now = reg(pool, b + 1)
                pool.wait_ge(sg("plan_made"), 2)
                pool.wait_ge(sg("idx_made"), now)
                pool.indirect_dma_start(out=xg[:, u, :], out_offset=None, in_=d["h2"],
                                        in_offset=bass.IndirectOffsetOnAxis(ap=idx[:, u:u + 1], axis=0)).then_inc(sg(f"x{u}_loaded"), 16)

            blocks(pool, step)

        @block.tensor
        def _(pe):
            pe.wait_ge(sg("either_made"), 1)
            flat = either[:, :, :, :].rearrange("p n g e -> p (n g e)")
            pe.matmul(psum[0][:, 0:NT * NE], after[:, :], flat, start=True, stop=True).then_inc(sg("ranked"), 1)
            pe.matmul(psum[1][:, 0:NT * NE], ones[:, :], flat, start=True, stop=True).then_inc(sg("counted"), 1)

            pe.wait_ge(sg("hot_made"), 3)
            for n in range(NT):
                for i in range(2):
                    mm = pe.matmul(psum[2][:, 0:2 * NB], at_pos[:, n, i, :], at_blk[:, n, i, :, :].rearrange("p c b -> p (c b)"),
                                   start=n == 0 and i == 0, stop=n == NT - 1 and i == 1)
            mm.then_inc(sg("plan_done"), 1)

            def turn_x(b, u, h):
                pe.wait_ge(sg(f"x{u}_loaded"), 8 * (b + 2 - u))
                w(pe, f"xT{h}_read", b)
                for q in range(4):
                    mm = pe.transpose(psum[3 + h][:, q * P:(q + 1) * P], xg[:, u, (4 * h + q) * P:(4 * h + q + 1) * P], ident[:, :])
                mm.then_inc(sg(f"xT{h}_done"), 1)

            def gate_up(b, u, b1):
                pe.wait_ge(sg("xT0_read"), b1)
                pe.wait_ge(sg("xT1_read"), b1)
                for name, wt, bank, used in (("gate", wg, psum[0], "gate_read"), ("up", wu, psum[1], "hid_made")):
                    pe.wait_ge(sg(f"{name}{u}_loaded"), 8 * (b + 2 - u))
                    w(pe, used, b)
                    for t in range(DE // P):
                        for q in range(KT):
                            mm = pe.matmul(bank[:, t * P:(t + 1) * P], wt[:, u, q, t * P:(t + 1) * P], xT[:, u, q, :], start=q == 0, stop=q == KT - 1)
                    mm.then_inc(sg(f"{name}_done"), 1)

            def down_rows(b, u, b1):
                w(pe, "hid_made", b1)
                pe.wait_ge(sg(f"down{u}_loaded"), 8 * (b + 2 - u))
                for h in range(2):
                    w(pe, f"down{h}_read", b)
                    for q in range(DE // P):
                        mm = pe.matmul(psum[5 + h][:, :], hid[:, q * P:(q + 1) * P], wd[:, u, q, 512 * h:512 * h + 512], start=q == 0, stop=q == DE // P - 1)
                    mm.then_inc(sg(f"down{h}_done"), 1)

            def step(b, u):
                first = isinstance(b, int) and b == 0
                now, after_it = reg(pe, b), reg(pe, b + 1)
                turn_x(b, u, 0)
                turn_x(b, u, 1)
                first or down_rows(b - 1, 1 - u, now)
                gate_up(b, u, after_it)

            pe.wait_ge(sg("plan_made"), 2)
            last = blocks(pe, step)
            down_rows(2 * last + 1, 1, pe.to_reg(2 * last + 2))

        @block.scalar
        def _(act):
            nc.scalar.preload_act_table_set("natural_log_exp_and_others")
            act.wait_ge(sg("lg_shifted"), 1)
            nc.scalar.activation(ex[:, :, :], lg[:, :, :], ACT.Exp).then_inc(sg("ex_made"), 1)
            act.wait_ge(sg("le_shifted"), 1)
            nc.scalar.activation(prob[:, :, :], le[:, :, :], ACT.Exp).then_inc(sg("ex_made"), 1)

            def down_read(b, u, b1):
                w(act, f"y{u}_stored", 8 * (b - u))
                for h in range(2):
                    act.wait_ge(sg("plan_made"), 2)
                    act.wait_ge(sg(f"down{h}_done"), b1)
                    nc.scalar.activation(yrow[:, u, 512 * h:512 * h + 512], psum[5 + h][:, :], ACT.Copy,
                                         scale=plan_weight[:, bass.ds(b, 1)]).then_inc(sg(f"down{h}_read"), 1)
                act.wait_ge(sg("down0_read"), b1)
                act.wait_ge(sg("down1_read"), b1)
                act.dma_start(d["y"][bass.ds(b * P, P), :], yrow[:, u, :]).then_inc(sg(f"y{u}_stored"), 16)

            def step(b, u):
                before, now, after_it = [reg(act, b + i) for i in (-1, 0, 1)]
                act.wait_ge(sg("xT0_done"), after_it)
                w(act, "up_done", before)
                nc.scalar.copy(xT[:, u, 0:4, :], psum[3][:, :].rearrange("p (a b) -> p a b", a=4)).then_inc(sg("xT0_read"), 1)
                if not (isinstance(b, int) and b == 0):
                    down_read(b - 1, 1 - u, now)
                act.wait_ge(sg("gate_done"), after_it)
                w(act, "hid_made", now)
                nc.scalar.activation(sil[:, :], psum[0][:, :], ACT.Silu).then_inc(sg("gate_read"), 1)

            act.wait_ge(sg("plan_made"), 2)
            last = blocks(act, step)
            down_read(2 * last + 1, 1, act.to_reg(2 * last + 2))
            for u in range(2):
                act.wait_ge(sg(f"y{u}_stored"), 16 * last + 16)
            act.sem_inc(sg("all_stored"), 1)

        @block.vector
        def _(dve):
            done = [0]

            def then(op):
                done[0] += 1
                op.then_inc(sg("route_step"), 1)
                dve.wait_ge(sg("route_step"), done[0])

            def wide(v, shape):
                return v.unsqueeze(2).to_broadcast(shape)

            V = nc.vector
            def reduce(out, in_, op):
                return V.tensor_reduce(out=out, in_=in_, axis=AX_X, op=op)

            dve.wait_ge(sg("iotas_made"), 2)
            then(V.tensor_copy(count[:, :], count_i[:, :]))
            c4 = count[:, 0:4].unsqueeze(1).to_broadcast(E4)

            def one_hot_of_max(out, v, top):
                then(V.tensor_tensor(eq[:, :, :], v, wide(top, E4), ALU.is_equal))
                then(V.scalar_tensor_tensor(eq[:, :, :], c4, -4.0, eq[:, :, :], ALU.add, ALU.mult))
                then(reduce(first[:, :], eq[:, :, :], ALU.min))
                then(V.tensor_scalar(first[:, :], first[:, :], 4.0, None, ALU.add))
                then(V.tensor_tensor(out, c4, wide(first[:, :], E4), ALU.is_equal))

            then(reduce(gmax[:, :], logits[:, :, 0:NG], ALU.max))
            V.tensor_tensor(lg[:, :, :], logits[:, :, 0:NG], wide(gmax[:, :], E4), ALU.subtract).then_inc(sg("lg_shifted"), 1)
            one_hot_of_max(group[:, :, :], logits[:, :, 0:NG], gmax[:, :])
            then(V.tensor_tensor(tmp16[:, :, :, :], logits[:, :, NG:].rearrange("p n (g e) -> p n g e", g=NG),
                                 group[:, :, :].unsqueeze(3).to_broadcast(E16), ALU.mult))
            then(reduce(le[:, :, :], tmp16[:, :, :, :].rearrange("p n g e -> p n e g"), ALU.add))
            then(reduce(emax[:, :], le[:, :, :], ALU.max))
            V.tensor_tensor(le[:, :, :], le[:, :, :], wide(emax[:, :], E4), ALU.subtract).then_inc(sg("le_shifted"), 1)
            dve.wait_ge(sg("ex_made"), 1)
            then(reduce(pg[:, :], ex[:, :, :], ALU.add))
            then(V.reciprocal(pg[:, :], pg[:, :]))
            dve.wait_ge(sg("ex_made"), 2)
            then(reduce(emax[:, :], prob[:, :, :], ALU.add))
            then(V.reciprocal(emax[:, :], emax[:, :]))
            then(V.tensor_tensor(prob[:, :, :], prob[:, :, :], wide(emax[:, :], E4), ALU.mult))
            then(reduce(v1[:, :], prob[:, :, :], ALU.max))
            one_hot_of_max(picked[0][:, :, :], prob[:, :, :], v1[:, :])
            then(V.scalar_tensor_tensor(prob2[:, :, :], picked[0][:, :, :], -2.0, prob[:, :, :], ALU.mult, ALU.add))
            then(reduce(v2[:, :], prob2[:, :, :], ALU.max))
            one_hot_of_max(picked[1][:, :, :], prob2[:, :, :], v2[:, :])
            for i in range(2):
                then(V.tensor_tensor(chosen[i][:, :, :, :], group[:, :, :].unsqueeze(3).to_broadcast(E16),
                                     picked[i][:, :, :].unsqueeze(2).to_broadcast(E16), ALU.mult))
            then(V.tensor_tensor(either[:, :, :, :], chosen[0][:, :, :, :], chosen[1][:, :, :, :], ALU.add))
            V.memset(either[DEC:P, NP, :, :], 0.0).then_inc(sg("either_made"), 1)
            then(V.tensor_tensor(emax[:, :], v1[:, :], v2[:, :], ALU.add))
            then(V.reciprocal(emax[:, :], emax[:, :]))
            then(V.tensor_tensor(pg[:, :], pg[:, :], emax[:, :], ALU.mult))
            for i, v in enumerate((v1, v2)):
                V.tensor_tensor(value[:, :, i, 1], pg[:, :], v[:, :], ALU.mult)
                then(V.tensor_copy(value[:, :, i, 0], token[:, :]))
            then(V.memset(value[DEC:P, NP, :, :], 0.0))
            dve.wait_ge(sg("ranked"), 1)
            V.tensor_copy(rank[:, :, :].rearrange("p n e -> p (n e)"), psum[0][:, 0:NT * NE]).then_inc(sg("rank_read"), 1)
            dve.wait_ge(sg("counted"), 1)
            V.tensor_copy(counts[:, :, :].rearrange("p n e -> p (n e)"), psum[1][:, 0:NT * NE]).then_inc(sg("rank_read"), 1)
            dve.wait_ge(sg("rank_read"), 2)
            dve.wait_ge(sg("carry_zeroed"), 1)
            for n in range(1, NT):
                then(V.tensor_tensor(carry[:, n, :], carry[:, n - 1, :], counts[:, n - 1, :], ALU.add))
            then(V.tensor_tensor(total[:, :], carry[:, NP, :], counts[:, NP, :], ALU.add))
            then(V.tensor_scalar(first[:, :], count[:, 0:NT], float(P), None, ALU.mult))
            then(V.tensor_tensor(over[:, :, :], total[:, :].unsqueeze(2).to_broadcast([P, NE, NT]),
                                 first[:, :].unsqueeze(1).to_broadcast([P, NE, NT]), ALU.is_gt))
            then(reduce(nblk[:, :], over[:, :, :], ALU.add))
            then(V.tensor_tensor(tri[:, :, :], count[:, 0:NE].unsqueeze(1).to_broadcast([P, NE, NE]),
                                 count[:, 0:NE].unsqueeze(2).to_broadcast([P, NE, NE]), ALU.is_le))
            then(V.tensor_tensor(prod[:, :, :], tri[:, :, :], nblk[:, :].unsqueeze(1).to_broadcast([P, NE, NE]), ALU.mult))
            then(reduce(end[:, :], prod[:, :, :], ALU.add))
            then(V.tensor_tensor(ended[:, :, :], end[:, :].unsqueeze(1).to_broadcast([P, NB, NE]),
                                 count[:, 0:NB].unsqueeze(2).to_broadcast([P, NB, NE]), ALU.is_le))
            then(reduce(be[:, :], ended[:, :, :], ALU.add))
            V.tensor_scalar(block_expert[0:1, 0:NB], be[0:1, :], float(NE - 1), None, ALU.min).then_inc(sg("block_expert_made"), 1)
            then(V.tensor_scalar(used[0:1, :], end[0:1, NE - 1:NE], -1.0, None, ALU.add))
            V.tensor_scalar(block_expert[0:1, NB:NB + 1], used[0:1, :], 1, None, ALU.logical_shift_right).then_inc(sg("block_expert_made"), 1)
            then(V.tensor_tensor(start[:, :], end[:, :], nblk[:, :], ALU.subtract))
            then(V.scalar_tensor_tensor(slot[:, :, :], start[:, :].unsqueeze(1).to_broadcast([P, NT, NE]), float(P),
                                        carry[:, :, :], ALU.mult, ALU.add))
            then(V.tensor_tensor(slot[:, :, :], slot[:, :, :], rank[:, :, :], ALU.add))
            for i in range(2):
                then(V.tensor_tensor(rank[:, :, :], slot[:, :, :], chosen[i][:, :, :, :].rearrange("p n g e -> p n (g e)"), ALU.mult))
                then(reduce(slot_f[:, :, i], rank[:, :, :], ALU.add))
            then(V.tensor_copy(slots[:, :, :], slot_f[:, :, :]))
            then(V.tensor_scalar(blk_i[:, :, :], slots[:, :, :], 7, None, ALU.logical_shift_right))
            then(V.tensor_scalar(pos_i[:, :, :], slots[:, :, :], P - 1, None, ALU.bitwise_and))
            then(V.tensor_copy(blk_f[:, :, :], blk_i[:, :, :]))
            then(V.tensor_copy(pos_f[:, :, :], pos_i[:, :, :]))

            def choices(v):
                return v.rearrange("p n i -> p (n i)").unsqueeze(2)

            V.tensor_tensor(at_pos[:, :, :, :].rearrange("p n i c -> p (n i) c"), count[:, :].unsqueeze(1).to_broadcast([P, 2 * NT, P]),
                            choices(pos_f[:, :, :]).to_broadcast([P, 2 * NT, P]), ALU.is_equal).then_inc(sg("hot_made"), 1)
            by_choice = at_blk[:, :, :, :, :].rearrange("p n i c b -> p (n i) c b")
            then(V.tensor_tensor(by_choice[:, :, 0, :], count[:, 0:NB].unsqueeze(1).to_broadcast([P, 2 * NT, NB]),
                                 choices(blk_f[:, :, :]).to_broadcast([P, 2 * NT, NB]), ALU.is_equal))
            for i in (1, 0):
                V.tensor_tensor(by_choice[:, :, i, :], by_choice[:, :, 0, :],
                                value[:, :, :, i].rearrange("p n c -> p (n c)").unsqueeze(2).to_broadcast([P, 2 * NT, NB]), ALU.mult).then_inc(sg("hot_made"), 1)
            dve.wait_ge(sg("rows_loaded"), 112)
            for r in range(2):
                V.scalar_tensor_tensor(final_rows[:, r, 1, :], final_rows[:, r, 1, :], 1.0, yrow[:, 0, :], ALU.add, ALU.mult).then_inc(sg("rows_made"), 1)
            dve.wait_ge(sg("rows_made"), 2)
            dve.wait_ge(sg("plan_done"), 1)
            V.tensor_copy(plan_token[:, :], psum[2][:, 0:NB]).then_inc(sg("plan_made"), 1)
            V.tensor_copy(plan_weight[:, :], psum[2][:, NB:2 * NB]).then_inc(sg("plan_made"), 1)

            def step(b, u):
                before, now, after_it = [reg(dve, b + i) for i in (-1, 0, 1)]
                dve.wait_ge(sg("xT1_done"), after_it)
                w(dve, "up_done", before)
                V.tensor_copy(xT[:, u, 4:8, :], psum[4][:, :].rearrange("p (a b) -> p a b", a=4)).then_inc(sg("xT1_read"), 1)
                dve.wait_ge(sg("up_done"), after_it)
                dve.wait_ge(sg("gate_read"), after_it)
                w(dve, "down1_done", now)
                V.tensor_tensor(hid[:, :], sil[:, :], psum[1][:, :], ALU.mult).then_inc(sg("hid_made"), 1)

            blocks(dve, step)


def combine_block(nc, a, o, d, c, rows):
    with nc.cleanup_on_exit(), ExitStack() as ctx:
        sems = {}

        def sg(name):
            if name not in sems:
                sems[name] = nc.alloc_semaphore(name="final_" + name)
            return sems[name]

        def sb(name, shape, dt=F32):
            return ctx.enter_context(nc.sbuf_tensor("final_" + name, shape, dt))

        y1, y2, x, x2, out = [sb(n, [P, 2, D]) for n in ("y1", "y2", "x", "x2", "out")]
        idx = sb("idx", [P, 2, 2], I32)
        st = sb("st", [P, 2, 2])
        eps = sb("eps", [P, 1])
        slots = c["slots"]
        GATE, SCALE, SHIFT = 0, 1, 2
        yp = o[0].rearrange("a t d -> (a t) d")
        ys = o[1].rearrange("a t d -> (a t) d")
        block = ctx.enter_context(nc.Block())

        def w(eng, name, value):
            need(eng, sg(name), value)

        def tiles(eng, step):
            step(0, 0, P, 0, 1)
            step(1, 1, P, 1, 2)
            with eng.Fori(1, NP // 2) as k:
                for u in range(2):
                    n = 2 * k + u
                    step(n, u, P, eng.to_reg(n + 0), eng.to_reg(n + 1))
            step(8, 0, DEC, 8, 9)

        @block.sync
        def _(sp):
            for r, i in ((0, 2), (1, 5)):
                with nc.allow_non_contiguous_dma("a row of 13 x 128 from its columns"):
                    sp.dma_start(o[i].rearrange("a b (n p) -> p (a b n)", p=P), c["shifts"][:, :, r]).then_inc(sg("shifts_out"), 16)

            def step(n, u, m, n0, n1):
                before = reg(sp, n - 1)
                w(sp, "x2_made", before)
                sp.dma_start(x[0:m, u, :], d["x1"][bass.ds(n * P, m), :]).then_inc(sg(f"x{u}_loaded"), 16)

            tiles(sp, step)
            sp.wait_ge(sg("shifts_out"), 32)

        @block.gpsimd
        def _(pool):
            nc.gpsimd.memset(eps[:, :], RMS_EPS).then_inc(sg("eps_made"), 1)

            def step(n, u, m, n0, n1):
                before = reg(pool, n - 1)
                w(pool, "x2_made", before)
                nc.gpsimd.tensor_copy(idx[:, u, :], slots[:, bass.ds(n, 1), :].rearrange("p a b -> p (a b)")).then_inc(sg("idx_made"), 1)
                for i, y in enumerate((y1, y2)):
                    pool.wait_ge(sg("eps_made"), 1)
                    pool.wait_ge(sg("idx_made"), n1)
                    pool.indirect_dma_start(out=y[0:m, u, :], out_offset=None, in_=d["y"],
                                            in_offset=bass.IndirectOffsetOnAxis(ap=idx[0:m, u, i:i + 1], axis=0)).then_inc(sg(f"y{u}_loaded"), 16)

            tiles(pool, step)

        @block.scalar
        def _(act):
            nc.scalar.preload_act_table_set("natural_log_exp_and_others")
            act.wait_ge(sg("eps_made"), 1)

            def step(n, u, m, n0, n1):
                before = reg(act, n - 1)
                w(act, "out_scaled", before)
                w(act, f"out{u}_stored", 8 * (n - u))
                w(act, "x2_made", n1)
                nc.scalar.activation(out[0:m, u, :], x2[0:m, u, :], ACT.Square, accum_out=st[0:m, u, 0:1]).then_inc(sg("squared"), 1)
                w(act, "squared", n1)
                nc.scalar.activation(st[0:m, u, 1:2], st[0:m, u, 0:1], ACT.Ln, scale=1.0 / D, bias=eps[0:m, :]).then_inc(sg("log_made"), 1)
                w(act, "log_made", n1)
                nc.scalar.activation(st[0:m, u, 1:2], st[0:m, u, 1:2], ACT.Exp, scale=-0.5).then_inc(sg("rstd_made"), 1)
                act.wait_ge(sg("out_made"), n1)
                dst = yp[bass.ds(n * P, m), :] if m == P else ys
                act.dma_start(dst, out[0:m, u, :]).then_inc(sg(f"out{u}_stored"), 16)

            tiles(act, step)
            act.wait_ge(sg("out0_stored"), 80)
            act.wait_ge(sg("out1_stored"), 64)

        @block.vector
        def _(dve):
            V = nc.vector
            def head(n, u, m, n0, n1):
                r = 0 if m == P else 1
                dve.wait_ge(sg(f"y{u}_loaded"), 16 * (n + 2 - u))
                V.tensor_tensor(y1[0:m, u, :], y1[0:m, u, :], y2[0:m, u, :], ALU.add).then_inc(sg("y_summed"), 1)
                dve.wait_ge(sg("y_summed"), n1)
                V.tensor_tensor(y1[0:m, u, :], y1[0:m, u, :], rows[0:m, r, GATE, :], ALU.mult).then_inc(sg("y_gated"), 1)
                dve.wait_ge(sg(f"x{u}_loaded"), 8 * (n + 2 - u))
                dve.wait_ge(sg("y_gated"), n1)
                V.tensor_tensor(x2[0:m, u, :], x[0:m, u, :], y1[0:m, u, :], ALU.add).then_inc(sg("x2_made"), 1)

            def tail(n, u, m, n0, n1):
                r = 0 if m == P else 1
                dve.wait_ge(sg("rstd_made"), n1)
                w(dve, f"out{u}_stored", 8 * (n - u))
                V.scalar_tensor_tensor(out[0:m, u, :], x2[0:m, u, :], st[0:m, u, 1:2], rows[0:m, r, SCALE, :], ALU.mult, ALU.mult).then_inc(sg("out_scaled"), 1)
                dve.wait_ge(sg("out_scaled"), n1)
                V.tensor_tensor(out[0:m, u, :], out[0:m, u, :], rows[0:m, r, SHIFT, :], ALU.add).then_inc(sg("out_made"), 1)

            def step(n, u, m, n0, n1):
                head(n, u, m, n0, n1)
                if not (isinstance(n, int) and n == 0):
                    tail(n - 1, 1 - u, P, None, n0)

            tiles(dve, step)
            tail(NP, 0, DEC, NP, NT)


INPUTS = ["x_prompt", "x_sample", "c_prompt", "c_sample", "state_rwkv_shift", "state_rwkv_wkv", "state_gla_kv",
          "w_ada", "b_ada", "norm1_g", "norm2_g", "w_in", "mu_shift", "w0", "w_decay_up", "a0", "w_a_up", "w_g_up",
          "k_k", "k_a", "r_k", "lnx_w", "lnx_b", "w_gla_gate_up", "b_gla_gate", "gla_norm_g", "w_out",
          "w_router_group", "b_router_group", "w_router_expert", "b_router_expert",
          "w_expert_gate", "w_expert_up", "w_expert_down", "w_ada_final", "b_ada_final", "normf_g"]
OUTPUTS = [(1, SEQ, D), (1, DEC, D), (1, 1, RP), (1, 1, 8, 64, 64), (1, 1, 4, 64, 128),
           (1, 1, RP), (1, 1, 8, 64, 64), (1, 1, 4, 64, 128)]


def kernel(**inputs):
    import numpy as np
    import concourse.bacc as bacc
    from concourse.bass_utils import run_bass_kernel_spmd

    nc = bacc.Bacc("TRN2", target_bir_lowering=False, num_devices=1)
    arrays, a = {}, {}
    for name in INPUTS:
        arrays[name] = np.ascontiguousarray(inputs[name])
        a[name] = nc.dram_tensor(name, arrays[name].shape, F32, kind="ExternalInput").ap()
    o = [nc.dram_tensor(f"out_{i}", s, F32, kind="ExternalOutput").ap() for i, s in enumerate(OUTPUTS)]
    build(nc, a, o)
    r = run_bass_kernel_spmd(nc, [arrays], core_ids=[0])
    return tuple(r.results[0][f"out_{i}"] for i in range(len(OUTPUTS)))
```
